# Optimizing a Trainium2 kernel written in Bass

```python
import math
import jax, jax.numpy as jnp
from jax import lax
import numpy as np

D_MODEL = 1024
BATCH = 1
SEQ = 512
DEPTH = 1
DEC_BATCH = 8
DEC_SEQ = 8
PAST_LEN = 1024
PAGE_SIZE = 128

HEAD_DIM = 64
N_Q_HEADS = D_MODEL // HEAD_DIM
N_KV_HEADS = 4
Q_PER_KV = N_Q_HEADS // N_KV_HEADS
ATTN_WIDTH = N_Q_HEADS * HEAD_DIM
KV_WIDTH = N_KV_HEADS * HEAD_DIM
Q_BLOCK = 128
D_INNER = 2 * D_MODEL
SSD_HEAD_DIM = 64
SSD_HEADS = D_INNER // SSD_HEAD_DIM
N_GROUPS = 4
HEADS_PER_GROUP = SSD_HEADS // N_GROUPS
D_STATE = 128
CONV_W = 4
CONV_CH = D_INNER + 2 * N_GROUPS * D_STATE
SSD_CHUNK = 128
D_FF = -(-8 * D_MODEL // (3 * 256)) * 256
EPS = 1e-6
IN_SIZES = (ATTN_WIDTH, KV_WIDTH, KV_WIDTH, D_INNER, CONV_CH, SSD_HEADS, D_MODEL, D_MODEL)
IN_WIDTH = sum(IN_SIZES)

kernel_name = "stickbreak_ssd_gated_hybrid_step"

def _split_points(sizes):
    return np.cumsum(np.array(sizes))[:-1].tolist()

def rmsnorm(x, w):
    xf = x.astype(jnp.float32)
    y = xf * lax.rsqrt(jnp.mean(xf * xf, axis=-1, keepdims=True) + EPS) * w.astype(jnp.float32)
    return y.astype(x.dtype)

def stick_breaking_block(q, k, v, sb_bias, q_pos0):
    tq, tk = q.shape[1], k.shape[1]
    z = jnp.einsum('bqhgd,bkhd->bhgqk', q, k, preferred_element_type=jnp.float32) * (HEAD_DIM ** -0.5)
    z = z + sb_bias.astype(jnp.float32)[None, :, :, None, None]
    qpos = q_pos0 + jnp.arange(tq)
    kpos = jnp.arange(tk)
    mask = kpos[None, :] < qpos[:, None]
    log_beta = jax.nn.log_sigmoid(z)
    log_1m_beta = jnp.where(mask, jax.nn.log_sigmoid(-z), 0.0)
    suffix = lax.cumsum(log_1m_beta, axis=4, reverse=True) - log_1m_beta
    weights = jnp.where(mask, jnp.exp(log_beta + suffix), 0.0)
    return jnp.einsum('bhgqk,bkhd->bqhgd', weights.astype(v.dtype), v)

def stick_breaking_attention(q, k, v, sb_bias, q_start):
    T = q.shape[1]
    outs = []
    for s0 in range(0, T, Q_BLOCK):
        e0 = min(s0 + Q_BLOCK, T)
        lim = q_start + e0
        outs.append(stick_breaking_block(q[:, s0:e0], k[:, :lim], v[:, :lim], sb_bias, q_start + s0))
    return jnp.concatenate(outs, axis=1)

def causal_conv(xbc, conv_state, conv_w, conv_b):
    xp = jnp.concatenate([conv_state, xbc], axis=1)
    out = lax.conv_general_dilated(xp, conv_w[:, None, :].astype(xp.dtype), window_strides=(1,), padding='VALID',
                                   dimension_numbers=('NWC', 'WIO', 'NWC'), feature_group_count=CONV_CH)
    return out + conv_b, xp[:, xp.shape[1] - (CONV_W - 1):]

def ssd_chunked(x, dt, A, B, C, h0):
    b, T, H, P = x.shape
    f32 = jnp.float32
    Q = min(SSD_CHUNK, T)
    nc = -(-T // Q)
    pad = nc * Q - T
    pw4 = ((0, 0), (0, pad), (0, 0), (0, 0))
    xdt = jnp.pad(x.astype(f32) * dt[..., None], pw4).reshape(b, nc, Q, N_GROUPS, HEADS_PER_GROUP, P)
    a = jnp.pad(dt * A, ((0, 0), (0, pad), (0, 0))).reshape(b, nc, Q, N_GROUPS, HEADS_PER_GROUP)
    Bc = jnp.pad(B.astype(f32), pw4).reshape(b, nc, Q, N_GROUPS, D_STATE)
    Cc = jnp.pad(C.astype(f32), pw4).reshape(b, nc, Q, N_GROUPS, D_STATE)
    a_cum = jnp.cumsum(jnp.moveaxis(a, 2, -1), axis=-1)
    tril = jnp.tril(jnp.ones((Q, Q), dtype=bool))
    seg = jnp.where(tril, a_cum[..., :, None] - a_cum[..., None, :], -jnp.inf)
    Lmat = jnp.exp(seg)
    CB = jnp.einsum('bclgn,bcsgn->bcgls', Cc, Bc)
    y_diag = jnp.einsum('bcgls,bcgels,bcsgep->bclgep', CB, Lmat, xdt)
    decay_to_end = jnp.exp(a_cum[..., -1:] - a_cum)
    chunk_states = jnp.einsum('bclgn,bcgel,bclgep->bcgepn', Bc, decay_to_end, xdt)
    chunk_decay = jnp.exp(a_cum[..., -1])

    def step(h, inp):
        dec, st = inp
        return h * dec[..., None, None] + st, h

    h_init = h0.astype(f32).reshape(b, N_GROUPS, HEADS_PER_GROUP, P, D_STATE)
    h_last, h_prev = lax.scan(step, h_init, (jnp.moveaxis(chunk_decay, 1, 0), jnp.moveaxis(chunk_states, 1, 0)))
    h_prev = jnp.moveaxis(h_prev, 0, 1)
    y_off = jnp.einsum('bclgn,bcgepn,bcgel->bclgep', Cc, h_prev, jnp.exp(a_cum))
    y = (y_diag + y_off).reshape(b, nc * Q, H, P)[:, :T]
    return y.astype(x.dtype), h_last.reshape(b, H, P, D_STATE).astype(h0.dtype)

def hybrid_layer(x, k_past, v_past, conv_state, ssm_state, p):
    b, T, _ = x.shape
    past = k_past.shape[1]
    h = rmsnorm(x, p['norm1_w'])
    proj = h @ p['w_in']
    q, k, v, z, xbc, dt, ga, gb = jnp.split(proj, _split_points(IN_SIZES), axis=-1)
    q = rmsnorm(q.reshape(b, T, N_Q_HEADS, HEAD_DIM), p['q_norm_w']).reshape(b, T, N_KV_HEADS, Q_PER_KV, HEAD_DIM)
    k = rmsnorm(k.reshape(b, T, N_KV_HEADS, HEAD_DIM), p['k_norm_w'])
    v = v.reshape(b, T, N_KV_HEADS, HEAD_DIM)
    k_all = jnp.concatenate([k_past, k], axis=1)
    v_all = jnp.concatenate([v_past, v], axis=1)
    sb_bias = p['sb_bias'].reshape(N_KV_HEADS, Q_PER_KV)
    attn = stick_breaking_attention(q, k_all, v_all, sb_bias, past).reshape(b, T, ATTN_WIDTH)
    xbc, conv_new = causal_conv(xbc, conv_state, p['conv_w'], p['conv_b'])
    xbc = jax.nn.silu(xbc)
    xs, Bm, Cm = jnp.split(xbc, [D_INNER, D_INNER + N_GROUPS * D_STATE], axis=-1)
    xs = xs.reshape(b, T, SSD_HEADS, SSD_HEAD_DIM)
    Bm = Bm.reshape(b, T, N_GROUPS, D_STATE)
    Cm = Cm.reshape(b, T, N_GROUPS, D_STATE)
    dt = jax.nn.softplus(dt.astype(jnp.float32) + p['dt_bias'].astype(jnp.float32))
    A = -jnp.exp(p['a_log'].astype(jnp.float32))
    y, ssm_new = ssd_chunked(xs, dt, A, Bm, Cm, ssm_state)
    y = y + p['d_skip'][:, None].astype(y.dtype) * xs
    y = y.reshape(b, T, D_INNER) * jax.nn.silu(z)
    y = rmsnorm(y.reshape(b, T, N_GROUPS, D_INNER // N_GROUPS),
                p['ssd_norm_w'].reshape(N_GROUPS, D_INNER // N_GROUPS)).reshape(b, T, D_INNER)
    merged = jax.nn.sigmoid(ga) * (attn @ p['w_pa']) + jax.nn.sigmoid(gb) * (y @ p['w_pb'])
    x = x + merged @ p['w_out']
    h2 = rmsnorm(x, p['norm2_w'])
    x = x + (jax.nn.silu(h2 @ p['w_gate']) * (h2 @ p['w_up'])) @ p['w_down']
    return x, k, v, conv_new, ssm_new

def setup_inputs(seed: int = 0) -> dict:
    key = jax.random.key(seed)
    ks = jax.random.split(key, 25)
    f32 = jnp.float32
    n_pages = PAST_LEN // PAGE_SIZE
    n_used = DEC_BATCH * n_pages
    n_phys = n_used + (n_used + 3) // 4

    def nrm(k, shape, scale=1.0):
        return jax.random.normal(k, shape, f32) * scale

    x_prompt = nrm(ks[0], (BATCH, SEQ, D_MODEL))
    x_sample = nrm(ks[1], (DEC_BATCH, DEC_SEQ, D_MODEL))
    cache_k = nrm(ks[2], (DEPTH, n_phys, PAGE_SIZE, N_KV_HEADS, HEAD_DIM))
    cache_v = nrm(ks[3], (DEPTH, n_phys, PAGE_SIZE, N_KV_HEADS, HEAD_DIM))
    page_table = jax.random.permutation(ks[4], n_phys)[:n_used].reshape(DEC_BATCH, n_pages).astype(jnp.int32)
    state_ssm = nrm(ks[5], (DEPTH, DEC_BATCH, SSD_HEADS, SSD_HEAD_DIM, D_STATE), 0.3)
    state_conv = nrm(ks[6], (DEPTH, DEC_BATCH, CONV_W - 1, CONV_CH))
    norm1_w = 1.0 + nrm(ks[7], (DEPTH, D_MODEL), 0.02)
    w_in = nrm(ks[8], (DEPTH, D_MODEL, IN_WIDTH), D_MODEL ** -0.5)
    q_norm_w = 1.0 + nrm(ks[9], (DEPTH, HEAD_DIM), 0.02)
    k_norm_w = 1.0 + nrm(ks[10], (DEPTH, HEAD_DIM), 0.02)
    sb_bias = jax.random.uniform(ks[24], (DEPTH, N_Q_HEADS), f32, -8.0, -6.0)
    conv_w = nrm(ks[11], (DEPTH, CONV_W, CONV_CH), CONV_W ** -0.5)
    conv_b = nrm(ks[12], (DEPTH, CONV_CH), 0.02)
    dt0 = jnp.exp(jax.random.uniform(ks[13], (DEPTH, SSD_HEADS), f32, math.log(1e-3), math.log(1e-1)))
    dt_bias = dt0 + jnp.log(-jnp.expm1(-dt0))
    a_log = jnp.log(jax.random.uniform(ks[14], (DEPTH, SSD_HEADS), f32, 1.0, 16.0))
    d_skip = 1.0 + nrm(ks[15], (DEPTH, SSD_HEADS), 0.02)
    ssd_norm_w = 1.0 + nrm(ks[16], (DEPTH, D_INNER), 0.02)
    w_pa = nrm(ks[17], (DEPTH, ATTN_WIDTH, D_MODEL), ATTN_WIDTH ** -0.5)
    w_pb = nrm(ks[18], (DEPTH, D_INNER, D_MODEL), D_INNER ** -0.5)
    w_out = nrm(ks[19], (DEPTH, D_MODEL, D_MODEL), D_MODEL ** -0.5)
    norm2_w = 1.0 + nrm(ks[20], (DEPTH, D_MODEL), 0.02)
    w_gate = nrm(ks[21], (DEPTH, D_MODEL, D_FF), D_MODEL ** -0.5)
    w_up = nrm(ks[22], (DEPTH, D_MODEL, D_FF), D_MODEL ** -0.5)
    w_down = nrm(ks[23], (DEPTH, D_FF, D_MODEL), D_FF ** -0.5)
    return {"x_prompt": x_prompt, "x_sample": x_sample, "cache_k": cache_k, "cache_v": cache_v,
            "page_table": page_table, "state_ssm": state_ssm, "state_conv": state_conv,
            "norm1_w": norm1_w, "w_in": w_in, "q_norm_w": q_norm_w, "k_norm_w": k_norm_w,
            "sb_bias": sb_bias, "conv_w": conv_w, "conv_b": conv_b, "dt_bias": dt_bias, "a_log": a_log,
            "d_skip": d_skip, "ssd_norm_w": ssd_norm_w, "w_pa": w_pa, "w_pb": w_pb, "w_out": w_out,
            "norm2_w": norm2_w, "w_gate": w_gate, "w_up": w_up, "w_down": w_down}

def reference(x_prompt, x_sample, cache_k, cache_v, page_table, state_ssm, state_conv,
              norm1_w, w_in, q_norm_w, k_norm_w, sb_bias, conv_w, conv_b, dt_bias, a_log, d_skip,
              ssd_norm_w, w_pa, w_pb, w_out, norm2_w, w_gate, w_up, w_down):
    n_pages = page_table.shape[1]
    page = cache_k.shape[2]
    xp, xs = x_prompt, x_sample
    bp, bd = xp.shape[0], xs.shape[0]
    kp_l, vp_l, sp_l, cp_l, ks_l, vs_l, ss_l, cs_l = [], [], [], [], [], [], [], []
    for layer in range(DEPTH):
        p = dict(norm1_w=norm1_w[layer], w_in=w_in[layer], q_norm_w=q_norm_w[layer], k_norm_w=k_norm_w[layer],
                 sb_bias=sb_bias[layer], conv_w=conv_w[layer], conv_b=conv_b[layer], dt_bias=dt_bias[layer],
                 a_log=a_log[layer], d_skip=d_skip[layer], ssd_norm_w=ssd_norm_w[layer], w_pa=w_pa[layer],
                 w_pb=w_pb[layer], w_out=w_out[layer], norm2_w=norm2_w[layer], w_gate=w_gate[layer],
                 w_up=w_up[layer], w_down=w_down[layer])
        empty_kv = jnp.zeros((bp, 0, N_KV_HEADS, HEAD_DIM), xp.dtype)
        xp, k_p, v_p, c_p, s_p = hybrid_layer(
            xp, empty_kv, empty_kv, jnp.zeros((bp, CONV_W - 1, CONV_CH), xp.dtype),
            jnp.zeros((bp, SSD_HEADS, SSD_HEAD_DIM, D_STATE), xp.dtype), p)
        k_past = cache_k[layer][page_table].reshape(bd, n_pages * page, N_KV_HEADS, HEAD_DIM)
        v_past = cache_v[layer][page_table].reshape(bd, n_pages * page, N_KV_HEADS, HEAD_DIM)
        xs, k_s, v_s, c_s, s_s = hybrid_layer(xs, k_past, v_past, state_conv[layer], state_ssm[layer], p)
        kp_l.append(k_p); vp_l.append(v_p); sp_l.append(s_p); cp_l.append(c_p)
        ks_l.append(k_s); vs_l.append(v_s); ss_l.append(s_s); cs_l.append(c_s)
    return (xp, xs, jnp.stack(kp_l), jnp.stack(vp_l), jnp.stack(sp_l), jnp.stack(cp_l),
            jnp.stack(ks_l), jnp.stack(vs_l), jnp.stack(ss_l), jnp.stack(cs_l))


_drawn_inputs = setup_inputs


def setup_inputs(seed=0):
    import zlib

    import numpy as np

    out = dict(_drawn_inputs(seed))
    spreads = {}
    factors = {'cache_k': 2.81,
     'q_norm_w': 24.775,
     'sb_bias': 4.639,
     'd_skip': 26.358,
     'ssd_norm_w': 5.49,
     'norm2_w': 4.364}
    for name, (base, spread) in spreads.items():
        noise = np.random.default_rng([zlib.crc32(name.encode()), seed]).standard_normal(out[name].shape)
        drawn = base * np.exp(spread * noise) if base else spread * noise
        out[name] = __import__('jax').numpy.asarray(drawn.astype(out[name].dtype))
    for name, factor in factors.items():
        out[name] = (out[name] * factor).astype(out[name].dtype)
    return out
```

```python
from contextlib import ExitStack

import concourse.bass as bass
from concourse import mybir

F32 = mybir.dt.float32
F32R = mybir.dt.float32r
BF16 = mybir.dt.bfloat16
I32 = mybir.dt.int32
ALU = mybir.AluOpType
ACT = mybir.ActivationFunctionType

P = 128
D = 1024
KD = D // P
TP = 512
NB = 8
TD = 8
TS = NB * TD
T = TP + TS
HALF = T // 2
NC = TP // P
HD = 64
NQ = 16
NKV = 4
QG = NQ // NKV
PAGES = 8
DI = 2048
NH = 32
NG = 4
HG = NH // NG
PG = HG // 2
CH = 3072
CT = CH // P
CW = 4
FF = 2816
KF = FF // P
EPS = 1e-6
BIG = -1.0e30
K_SLOTS = 3
SEQS = NB // 2
SRC = 3 + TP + NB * (3 + TD)
CLAMP = 40.0
HALVES = [slice(0, HALF), slice(HALF, T)]

COL_Q, COL_K, COL_V = 0, D, D + 256
COL_Z = COL_V + 256
COL_X = COL_Z + DI
COL_B = COL_X + DI
COL_C = COL_B + NG * P
COL_DT = COL_C + NG * P
COL_GA = COL_DT + NH
COL_GB = COL_GA + D


def token_tiles():
    return [(c, P * c, P) for c in range(NC)] + [(NC, TP, TS)]


def attention_units():
    units = []
    for g in range(NKV):
        for i in range(NC):
            for n, j in enumerate(range(i, -1, -1)):
                units.append(dict(kind="prompt", g=g, i=i, j=j, n=n, last=j == 0))
    for h in range(2):
        units.append(dict(kind="new", h=h, n=0, last=False))
        for n, p in enumerate(range(PAGES - 1, -1, -1)):
            units.append(dict(kind="page", h=h, p=p, n=n + 1, last=p == 0))
    chain = accs = page = 0
    for u, x in enumerate(units):
        accs += x["n"] >= 2
        x.update(u=u, chain=chain, accs=accs, page=page)
        page += SEQS if x["kind"] == "page" else 0
        chain += x["last"]
    return units


def build(nc, x_prompt, x_sample, cache_k, cache_v, page_table, state_ssm, state_conv, norm1_w, w_in,
          q_norm_w, k_norm_w, sb_bias, conv_w, conv_b, dt_bias, a_log, d_skip, ssd_norm_w, w_pa, w_pb,
          w_out, norm2_w, w_gate, w_up, w_down,
          y_prompt, y_sample, k_prompt, v_prompt, ssm_prompt, conv_prompt, k_sample, v_sample,
          ssm_sample, conv_sample):
    units = attention_units()
    NU = len(units)
    n_phys = cache_k.shape[1]
    STEPS = NG * 5

    N_FIRST = KD + 2 + 2 + 1
    C_GATE_A = N_FIRST
    C_SSD = C_GATE_A + 2 * KD
    C_GROUP = 10 + 4
    C_GATE_B = C_SSD + NG * C_GROUP
    C_OUT = C_GATE_B + KD
    C_FFN = C_OUT + KD
    C_DOWN = C_FFN + 2 * KF
    N_CHUNKS = C_DOWN + 3 * KD
    DOWN_K = [(0, 8), (8, 8), (16, 6)]
    T_SSD = C_SSD
    T_GROUP = 10 + KD
    T_GATE_B = T_SSD + NG * T_GROUP
    T_OUT = T_GATE_B + KD
    T_FFN = T_OUT + KD
    T_DOWN = T_FFN + 2 * KF

    with ExitStack() as ctx:
        def sb(name, shape, dt=F32, scope=ctx):
            return scope.enter_context(nc.sbuf_tensor(name, shape, dt))

        sems = {}

        def sem(name):
            if name not in sems:
                sems[name] = ctx.enter_context(nc.semaphore(name))
            return sems[name]

        G = [ctx.enter_context(nc.psum_tensor(f"tile_banks{i}", [P, 2, 512], F32)) for i in range(2)]
        W = [ctx.enter_context(nc.psum_tensor(f"spare_bank{i}", [P, 512], F32)) for i in range(4)]

        ident = sb("ident", [P, P])
        ones = sb("ones", [P, P])
        upto = sb("upto", [P, P])
        after = sb("after", [P, P])
        upto_b = sb("upto_b", [TS, TS])
        after_b = sb("after_b", [TS, TS])
        in_seq = sb("in_seq", [TS, NB])
        conv_par = sb("conv_par", [P, 5 * CT])
        par = sb("par", [P, 50])
        PAR_N1, PAR_N2, PAR_SSD, PAR_D, PAR_Q, PAR_K = 0, 8, 16, 32, 48, 49
        pages_sb = sb("pages_sb", [1, NB * PAGES], I32)
        stats = sb("stats", [P, 3, 5])
        eps_col = sb("eps_col", [P, 1])
        dt_par = sb("dt_par", [NH, 3])
        dt_tok = sb("dt_tok", [P, 5, 2 * NH])
        conv_in = sb("conv_in", [P, CT, 24])
        conv_out = sb("conv_out", [P, CT, 27])

        w_raw = sb("w_raw", [P, 2, KD, P])
        w_hi = sb("w_hi", [P, 2, KD, P], F32R)
        w_lo = sb("w_lo", [P, 2, KD, P], F32R)
        raw_in = [sem("weights_in0"), sem("weights_in1")]
        hi_made = sem("weights_hi_made")
        split = sem("weights_split")
        tile_done = sem("tile_done")
        part_done = sem("down_part_done")
        tile_free = [sem("tile_free0"), sem("tile_free1")]

        x_hi = sb("x_hi", [P, KD, T], F32R)
        x_lo = sb("x_lo", [P, KD, T], F32R)

        early = ExitStack()
        o_hi = sb("o_hi", [P, KD, T], F32R, early)
        o_lo = sb("o_lo", [P, KD, T], F32R, early)
        attn = ExitStack()
        neg_suffix = sb("neg_suffix", [P, P], F32, attn)
        neg_ones = sb("neg_ones", [P, P], F32, attn)
        pair_ones = sb("pair_ones", [P, P], F32, attn)
        big_diag = sb("big_diag", [P, P], BF16, attn)
        bad_prompt = sb("bad_prompt", [P, QG, P], BF16, attn)
        bad_new = sb("bad_new", [TS, 2, SEQS, 16, TD], BF16, attn)
        bias_row = sb("bias_row", [HD + 1, NQ], F32, attn)
        q_t = sb("q_t", [HD + 1, NQ, T], F32, attn)
        k_t = sb("k_t", [HD + 1, NKV, T], F32, attn)
        v_tok = sb("v_tok", [P, 5, NKV * HD], F32, attn)
        k_page = sb("k_page", [P, K_SLOTS, NKV * HD], F32, attn)
        v_page = sb("v_page", [P, 8, NKV * HD], F32, attn)
        first = ExitStack()
        x_tok = sb("x_tok", [P, 5, D], F32, first)
        par_rows = sb("par_rows", [5 * CT, P], F32, first)
        par2_rows = sb("par2_rows", [50, P], F32, first)
        d_rows = sb("d_rows", [48, 2], F32, first)
        sc_rows = sb("sc_rows", [24, CH], F32, first)
        first.close()
        qkv = ExitStack()
        pre = sb("pre", [P, 2, T], F32, qkv)
        sq = sb("sq", [P, 2, T], F32, qkv)
        root = sb("root", [P, T], F32, qkv)
        rinv = sb("rinv", [P, T], F32, qkv)
        v_t = sb("v_t", [P, 2, T], F32, qkv)
        dt_t = sb("dt_t", [2 * NH, T], F32, qkv)
        dt_w = sb("dt_w", [NH, 2, T], F32, qkv)
        k_out = sb("k_out", [P, 5, NKV * HD], F32, qkv)
        qkv.close()
        zs = sb("zs", [P, 2, 512], F32, attn)
        sp = sb("sp", [P, 4, 512], F32, attn)
        acc = sb("acc", [P, 2, 512], F32, attn)
        wts = sb("wts", [P, 2, 512], F32, attn)
        kt_page = sb("kt_page", [HD + 1, 8, NKV, P], F32, attn)
        attn.close()
        gate = sb("gate", [P, 2, T], F32, early)
        gated = sb("gated", [P, 2, T], F32, early)
        early.close()
        ssd = ExitStack()
        pb_sum = sb("pb_sum", [P, KD, T], F32, ssd)
        y_hi = sb("y_hi", [P, PG, T], F32R, ssd)
        y_lo = sb("y_lo", [P, PG, T], F32R, ssd)
        conv_src = sb("conv_src", [P, 2, SRC], F32, ssd)
        conv_acc = sb("conv_acc", [P, 2, SRC], F32, ssd)
        bc_t = sb("bc_t", [P, 2, 2, T], F32, ssd)
        xs_t = sb("xs_t", [P, PG, T], F32, ssd)
        y_t = sb("y_t", [P, PG, T], F32, ssd)
        z_s = sb("z_s", [P, PG, T], F32, ssd)
        xdt = sb("xdt", [P, 5, HG, HD], F32, ssd)
        xend = sb("xend", [P, 2, HG, HD], F32, ssd)
        b_tok = sb("b_tok", [P, 5, P], F32, ssd)
        cb_m = sb("cb_m", [P, 5, P], F32, ssd)
        a_after = sb("a_after", [P, HG, P], F32, ssd)
        decay = sb("decay", [P, HG, P], F32, ssd)
        e_t = sb("e_t", [P, PG, P], F32, ssd)
        state = sb("state", [P, 2, HG * HD], F32, ssd)
        old = sb("old", [P, 2, PG, P], F32, ssd)
        old_t = sb("old_t", [P, 2, PG, P], F32, ssd)
        b_seq = sb("b_seq", [TS, NB, P], F32, ssd)
        xend_s = sb("xend_s", [TS, HG, HD], F32, ssd)
        y_old = sb("y_old", [P, PG, TS], F32, ssd)
        end_decay = sb("end_decay", [P, 5, NH], F32, ssd)
        chunk_decay = sb("chunk_decay", [P, NC, NH], F32, ssd)
        seq_decay = sb("seq_decay", [P, NH // 2, NB], F32, ssd)
        state_out = sb("state_out", [P, PG, P], F32, ssd)
        y_root = a_after[:, 0:5, :].rearrange("p h l -> p (h l)")[:, 0:T]
        y_rinv = decay[:, 0:5, :].rearrange("p h l -> p (h l)")[:, 0:T]
        ssd.close()
        tail = ExitStack()
        x_res = sb("x_res", [P, KD, T], F32, tail)
        mid = ExitStack()
        m_hi = sb("m_hi", [P, KD, T], F32R, mid)
        m_lo = sb("m_lo", [P, KD, T], F32R, mid)
        x_again = sb("x_again", [P, 5, D], F32, mid)
        conv_rows = sb("conv_rows", [27, CH], F32, mid)
        gated_in = sb("gated_in", [P, 2, T], F32, mid)
        mid.close()
        f_hi = sb("f_hi", [P, KF, T], F32R, tail)
        f_lo = sb("f_lo", [P, KF, T], F32R, tail)
        gate2 = sb("gate2", [P, 2, T], F32, tail)
        prod2 = sb("prod2", [P, 2, T], F32, tail)
        root2 = sb("root2", [P, T], F32, tail)
        rinv2 = sb("rinv2", [P, T], F32, tail)
        y_tok = sb("y_tok", [P, 5, P], F32, tail)
        tail.close()
        gated_dram = nc.dram_tensor("gated_dram", (KD, P, T), F32, kind="Internal").ap()

        keys = [("par", 0), ("par", 1), ("conv_in", 0), ("conv_in", 1)]
        keys += [("x", k, j) for k in range(KD) for j in range(2)]
        keys += [(w, n, j) for n in range(KD + 2) for w, j in (("ss", 0), ("ss", 1))]
        keys += [("v", n, c) for n in range(2) for c in range(5)] + [("k", c) for c in range(5)]
        keys += [("dt", 0)]
        FIRST_USES = len(keys)
        keys += [("decays", 0)]
        for g in range(NG):
            keys += [("x_tok", g, c) for c in range(5)] + [("b_tok", g), ("cb", g), ("sample_bc", g)]
            for c in range(5):
                keys += [("e", g, c)] if c else []
                keys += [("seg", g, c, 0), ("seg", g, c, 1)]
                keys += [("y_chunk_old", g, c)] if 0 < c < NC else []
                keys += [("state", g, c)] if c < NC else []
                keys += [("y_new", g, c)]
                if c < NC:
                    for b in (2 * c, 2 * c + 1):
                        keys += [("old_t", g, b), ("y_seq_old", g, b), ("new_state", g, b)]
            keys += [("state_out", g), ("y_ss", g, 0), ("y_ss", g, 1)]
        keys += [("conv_out", j) for j in range(6)]
        use = {key: (n % 4, n // 4) for n, key in enumerate(keys)}
        N_USES = len(keys)
        bank_full = [sem(f"bank_full{i}") for i in range(4)]
        bank_read = [sem(f"bank_read{i}") for i in range(4)]

        def spare(key):
            return W[use[key][0]]

        def wait_full(eng, key):
            i, n = use[key]
            eng.wait_ge(bank_full[i], n + 1)

        def wait_read(eng, key):
            i, n = use[key]
            if n:
                eng.wait_ge(bank_read[i], n)

        block = ctx.enter_context(nc.Block())

        def half(base, step=0, i=0):
            return base // 2 + (step // 2) * i

        def f32(ap):
            return ap.bitcast(F32)

        def load_chunk(eng, src, c, step=0, i=0, width=P, tiles=KD, dst=None):
            if step or c >= 2:
                eng.wait_ge(split, c - 1 + step * i)
            dst = w_raw[:, c % 2, 0:tiles, 0:width] if dst is None else dst
            eng.dma_start(dst, src).then_inc(raw_in[c % 2], 16)

        def make_hi(c, step=0, i=0, width=P, tiles=KD, after_tiles=None, after_part=None):
            nc.scalar.wait_ge(raw_in[c % 2], 16 * (half(c, step, i) + 1))
            if after_tiles is not None:
                nc.scalar.wait_ge(tile_done, after_tiles)
            if after_part is not None:
                nc.scalar.wait_ge(part_done, after_part)
            nc.scalar.activation(w_hi[:, c % 2, 0:tiles, 0:width], w_raw[:, c % 2, 0:tiles, 0:width],
                                 ACT.Copy).then_inc(hi_made, 1)

        def make_lo(c, step=0, i=0, width=P, tiles=KD):
            nc.vector.wait_ge(hi_made, c + 1 + step * i)
            nc.vector.tensor_tensor(w_lo[:, c % 2, 0:tiles, 0:width], w_raw[:, c % 2, 0:tiles, 0:width],
                                    f32(w_hi[:, c % 2, 0:tiles, 0:width]), ALU.subtract).then_inc(split, 1)

        def wait_tile(eng, t, step=0, i=0):
            eng.wait_ge(tile_done, t + 1 + step * i)

        def wait_freed(eng, t, step=0, i=0):
            eng.wait_ge(tile_free[t % 2], half(t, step, i) + 2)

        def tile(t, rows=P):
            return G[t % 2][0:rows, :, 0:HALF]

        def halves(ap):
            return ap.rearrange("p (h t) -> p h t", h=2)

        def product(pe, t, w, x, start=True, stop=True, rows=P, step=0, i=0, onto=False):
            if start:
                pe.wait_ge(tile_free[t % 2], half(t, step, i) + 1)
            last = len(w) - 1
            for k, ((wh, wl), (xh, xl)) in enumerate(zip(w, x)):
                for h in range(2):
                    out = G[t % 2][0:rows, h, 0:HALF]
                    nc.tensor.matmul(out, wh, xh[:, HALVES[h]], start=start and k == 0, stop=False, skip_group_check=onto)
                    nc.tensor.matmul(out, wh, xl[:, HALVES[h]], start=False, stop=False, skip_group_check=onto)
                for h in range(2):
                    out = G[t % 2][0:rows, h, 0:HALF]
                    mm = nc.tensor.matmul(out, wl, xh[:, HALVES[h]], start=False, stop=stop and k == last, skip_group_check=onto)
            return mm

        def chunk_tile(pe, c, t, xh, xl, step=0, i=0, width=P):
            pe.wait_ge(split, c + 1 + step * i)
            w = [(w_hi[:, c % 2, k, 0:width], w_lo[:, c % 2, k, 0:width]) for k in range(KD)]
            x = [(xh[:, k, :], xl[:, k, :]) for k in range(KD)]
            mm = product(pe, t, w, x, rows=width, step=step, i=i)
            mm.then_inc(tile_done, 1)
            return mm

        def group_inputs(g):
            return [("bc", g, 0), ("bc", g, 1)] + [("x", g, j) for j in range(PG)]

        ssd_slots = {g: (group_inputs(g + 1) if g + 1 < NG else []) + [("z", g, j) for j in range(PG)]
                     for g in range(NG)}
        ssd_chunks = group_inputs(0)
        for g in range(NG):
            ssd_chunks += ssd_slots[g] + [("pb", g, n) for n in range(0, KD, 2)]
        chunk_of = {key: C_SSD + n for n, key in enumerate(ssd_chunks)}
        tile_of, n_t = {}, T_SSD
        for key in ssd_chunks:
            tile_of[key] = n_t
            n_t += 2 if key[0] == "pb" else 1
        assert n_t == T_GATE_B and len(ssd_chunks) == NG * C_GROUP

        def ssd_col(key):
            what, g, j = key
            if what == "bc":
                return (COL_B, COL_C)[j] + g * P
            return (COL_X if what == "x" else COL_Z) + (g * PG + j) * P

        def src_tile(key):
            what, g, j = key
            return DI // P + NG * j + g if what == "bc" else g * PG + j

        conv_keys = [k for k in ssd_chunks if k[0] in ("bc", "x")]
        conv_n = {key: n for n, key in enumerate(conv_keys)}

        def score_bank(u):
            return G[u % 4 // 2][:, u % 2, :]

        def wait_after_read(eng, key):
            i, n = use[key]
            eng.wait_ge(bank_read[i], n + 1)

        page_unit = {x["page"] + b: x["u"] for x in units if x["kind"] == "page" for b in range(SEQS)}

        def decode_block(ap_rows, t0):
            return ap_rows[:, t0:t0 + TS].rearrange("p (b t) -> p b t", b=NB)

        def conv_dst(key):
            what, g, j = key
            return bc_t[:, g % 2, j, :] if what == "bc" else xs_t[:, j, :]

        def tiles_after(c):
            if c < C_SSD:
                return c + 1
            if c < C_GATE_B:
                key = ssd_chunks[c - C_SSD]
                return tile_of[key] + (2 if key[0] == "pb" else 1)
            return c + 1 + T_GATE_B - C_GATE_B

        def chain_views(x, e):
            out = W[x["chain"] % 2][0:HD, :]
            rows = slice(e * HD, (e + 1) * HD)
            if x["kind"] == "prompt":
                src = out.rearrange("p (h q) -> p h q", h=QG)[:, e::2, :]
                at = (slice(x["g"] * 2, x["g"] * 2 + 2), slice(x["i"] * P, (x["i"] + 1) * P))
                return src, o_hi[rows, at[0], at[1]], o_lo[rows, at[0], at[1]]
            src = out.rearrange("p (b x t) -> p b x t", b=SEQS, t=TD)[:, :, e::2, :]
            t0 = TP + x["h"] * SEQS * TD
            return (src, *(o[rows, :, t0:t0 + SEQS * TD].rearrange("p k (b t) -> p b k t", b=SEQS) for o in (o_hi, o_lo)))

        def wait_chain(eng, x):
            eng.wait_ge(sem("pv_done"), x["u"] + 1)

        def read_turned(eng, copy, x, b):
            n = x["page"] + b
            eng.wait_ge(sem("k_turned"), n + 1)
            eng.wait_ge(sem("kt_ones"), 1)
            if n >= 8:
                eng.wait_ge(sem("logits_done"), page_unit[n - 8] + 1)
            copy(kt_page[0:HD, n % 8], W[2 + n % 2][0:HD, :].rearrange("p (g k) -> p g k", g=NKV), ACT.Copy).then_inc(sem(f"kt_made{n % 2}"), 1)

        sem_const_first, sem_const_all = [], []

        @block.sync
        def _(sp_eng):
            eng = sp_eng
            eng.dma_start(x_tok[:, 0:NC, :], x_prompt[0].rearrange("(c p) n -> p c n", p=P)).then_inc(sem("x_in"), 16)
            eng.dma_start(x_tok[0:TS, NC, :], x_sample.rearrange("b t n -> (b t) n")).then_inc(sem("x_in"), 16)

            def first_src(c):
                if c < N_FIRST - 1:
                    return w_in[0, :, c * P:(c + 1) * P].rearrange("(t p) n -> p t n", p=P)
                return w_in[0, :, COL_DT:COL_DT + NH].rearrange("(t p) n -> p t n", p=P)

            for c in range(N_FIRST):
                load_chunk(eng, first_src(c), c, width=P if c < N_FIRST - 1 else NH)
            def col_tile(w, k):
                return w.rearrange("p t (m n) -> p t m n", n=P)[:, :, bass.ds(k, 1), :].rearrange("p t o n -> p t (o n)")

            cols = [w_in[0, :, COL_GA:COL_GA + D].rearrange("(t p) n -> p t n", p=P),
                    w_pa[0].rearrange("(t p) n -> p t n", p=P)]
            for k in range(2):
                load_chunk(eng, cols[k][:, :, 0:P], C_GATE_A + k)
            eng.dma_start(pages_sb[:, :], page_table.rearrange("b p -> (b p)").rearrange("(o n) -> o n", o=1)).then_inc(sem("pages_in"), 16)
            eng.wait_ge(sem("pages_in"), 16)

            def page_of(x, b):
                at = (x["h"] * SEQS + b) * PAGES + x["p"]
                return eng.value_load(pages_sb[0:1, at:at + 1], min_val=0, max_val=n_phys - 1)

            page_units = [x for x in units if x["kind"] == "page"]
            for k in range(len(page_units) + 2):
                for b in range(SEQS if k < len(page_units) else 0):
                    x = page_units[k]
                    n = x["page"] + b
                    if n >= K_SLOTS:
                        eng.wait_ge(sem("k_turned"), n - K_SLOTS + 1)
                    eng.dma_start(k_page[:, n % K_SLOTS, :], cache_k[0, bass.ds(page_of(x, b), 1)].rearrange("o p h d -> p (o h d)")).then_inc(sem(f"k_page_in{n % K_SLOTS}"), 16)
                for b in range(SEQS if k >= 2 else 0):
                    x = page_units[k - 2]
                    n = x["page"] + b
                    if n >= 8:
                        eng.wait_ge(sem("pv_done"), page_units[k - 4]["u"] + 1)
                    eng.dma_start(v_page[:, n % 8, :], cache_v[0, bass.ds(page_of(x, b), 1)].rearrange("o p h d -> p (o h d)")).then_inc(sem(f"v_page_in{n % 8}"), 16)

            def load_in_turn(sources, c, n):
                again = eng.alloc_register(f"column_tile{c}")
                with eng.Fori(1, n) as i:
                    load_chunk(eng, col_tile(sources[0], i), c, 2, i)
                    eng.reg_mov(again, i)
                    load_chunk(eng, col_tile(sources[1], eng.snap(again)), c + 1, 2, i)

            load_in_turn(cols, C_GATE_A, KD)
            for key in ssd_chunks:
                c = chunk_of[key]
                if key[0] == "pb":
                    _, g, n0 = key
                    src = w_pb[0, g * PG * P:(g + 1) * PG * P, n0 * P:(n0 + 2) * P].rearrange("(t p) n -> p t n", p=P)
                    dst = w_raw[:, c % 2].rearrange("p t n -> p (t n)").rearrange("p (t n) -> p t n", t=PG)
                    load_chunk(eng, src, c, dst=dst)
                else:
                    n0 = ssd_col(key)
                    load_chunk(eng, w_in[0, :, n0:n0 + P].rearrange("(t p) n -> p t n", p=P), c)
            gate_b = w_in[0, :, COL_GB:COL_GB + D].rearrange("(t p) n -> p t n", p=P)
            out_w = w_out[0].rearrange("(t p) n -> p t n", p=P)
            for base, w in ((C_GATE_B, gate_b), (C_OUT, out_w)):
                with eng.Fori(0, KD // 2) as i:
                    for k in range(2):
                        load_chunk(eng, w[:, :, bass.ds(2 * P * i + k * P, P)], base + k, 2, i)
            up = [w_gate[0].rearrange("(t p) n -> p t n", p=P), w_up[0].rearrange("(t p) n -> p t n", p=P)]
            for k in range(2):
                load_chunk(eng, up[k][:, :, 0:P], C_FFN + k)
            load_in_turn(up, C_FFN, KF)
            down = w_down[0].rearrange("(t p) n -> p t n", p=P)
            with eng.Fori(0, KD // 2) as i:
                for n in range(2):
                    for k, (k0, kn) in enumerate(DOWN_K):
                        load_chunk(eng, down[:, k0:k0 + kn, bass.ds(2 * P * i + n * P, P)], C_DOWN + 3 * n + k, 6, i, tiles=kn)

        @block.gpsimd
        def _(pool):
            eng = pool
            made = sem("constants")
            n_made = [0]

            def put(make, *args, **kwargs):
                if n_made[0]:
                    eng.wait_ge(made, n_made[0])
                n_made[0] += 1
                make(*args, **kwargs).then_inc(made, 1)

            def select(ap, op, base, pattern, cm, fill):
                put(eng.affine_select, out=ap, in_=ap, compare_op=op, fill=fill, base=base, pattern=pattern, channel_multiplier=cm)

            def rule(ap, value, conditions, fill):
                put(eng.memset, ap, value)
                for op, base, pattern, cm in conditions:
                    select(ap, op, base, pattern, cm, fill)

            ge, gt = ALU.is_ge, ALU.is_gt
            rule(ident[:, :], 0.0, [(ALU.not_equal, 0, [[-1, P]], 1)], 1.0)
            put(eng.memset, ones[:, :], 1.0)
            put(eng.memset, eps_col[:, :], EPS)
            put(eng.memset, stats[:, :, :], 1.0)
            rule(pair_ones[:, :], 1.0, [(ge, 0, [[-HD, 2], [0, HD]], 1), (ge, HD - 1, [[HD, 2], [0, HD]], -1)], 0.0)
            put(eng.memset, k_t[HD:HD + 1, :, :], 1.0)
            FIRST_CONST = n_made[0]
            sem_const_first.append(FIRST_CONST)
            eng.dma_start(bias_row[HD:HD + 1, :], sb_bias).then_inc(sem("bias_in"), 16)
            eng.wait_ge(sem("bias_in"), 16)
            put(eng.tensor_copy, q_t[HD:HD + 1, :, :], bias_row[HD:HD + 1, :].unsqueeze(2).to_broadcast([1, NQ, T]))
            rule(upto[:, :], 1.0, [(ge, 0, [[1, P]], -1)], 0.0)
            rule(after[:, :], 1.0, [(gt, 0, [[-1, P]], 1)], 0.0)
            rule(neg_suffix[:, :], -1.0, [(ge, 0, [[-1, P]], 1)], 0.0)
            put(eng.memset, neg_ones[:, :], -1.0)
            rule(big_diag[:, :], 0.0, [(ALU.not_equal, 0, [[-1, P]], 1)], BIG)
            rule(bad_prompt[:, :, :], 0.0, [(gt, 0, [[0, QG], [1, P]], -1)], 1.0)
            for h in range(2):
                first_token = h * SEQS * TD
                rule(bad_new[:, h], 0.0,
                     [(ge, -first_token, [[-TD, SEQS], [0, 16], [0, TD]], 1),
                      (gt, first_token, [[TD, SEQS], [0, 16], [1, TD]], -1)], 1.0)
            rule(upto_b[:, :], 1.0, [(ge, 0, [[-TD, NB], [0, TD]], 1), (ge, 0, [[TD, NB], [1, TD]], -1)], 0.0)
            rule(after_b[:, :], 1.0, [(gt, 0, [[-TD, NB], [-1, TD]], 1), (ge, TD - 1, [[TD, NB], [0, TD]], -1)], 0.0)
            rule(in_seq[:, :], 1.0, [(ge, 0, [[-TD, NB]], 1), (ge, TD - 1, [[TD, NB]], -1)], 0.0)
            sem_const_all.append(n_made[0])

            for n in range(2):
                for c in range(5):
                    wait_after_read(eng, ("v", n, c))
            eng.dma_start(v_prompt[0, 0].rearrange("(c p) h d -> p c (h d)", p=P), v_tok[:, 0:NC, :]).then_inc(sem("stored_v"), 16)
            eng.dma_start(v_sample[0].rearrange("b t h d -> (b t) (h d)"), v_tok[0:TS, NC, :]).then_inc(sem("stored_v"), 16)
            for c in range(5):
                wait_after_read(eng, ("k", c))
            eng.dma_start(k_prompt[0, 0].rearrange("(c p) h d -> p c (h d)", p=P), k_out[:, 0:NC, :]).then_inc(sem("stored_k"), 16)
            eng.dma_start(k_sample[0].rearrange("b t h d -> (b t) (h d)"), k_out[0:TS, NC, :]).then_inc(sem("stored_k"), 16)
            eng.wait_ge(sem("stored_k"), 32)
            wait_after_read(eng, ("dt", 0))
            eng.memset(kt_page[HD:HD + 1, :, :, :], 1.0).then_inc(sem("kt_ones"), 1)
            eng.wait_ge(sem("kt_ones"), 1)
            for x in units:
                u = x["u"]
                if x["n"] >= 2:
                    eng.wait_ge(sem("sp_made"), u)
                    if x["accs"] > 1:
                        eng.wait_ge(sem("acc_made"), x["accs"] - 1)
                    if u >= 2:
                        eng.wait_ge(sem("sums_done"), u - 1)
                    prev = sp[:, (u - 2) % 4, :] if x["n"] == 2 else acc[:, (u - 1) % 2, :]
                    eng.tensor_tensor(acc[:, u % 2, :], prev, sp[:, (u - 1) % 4, :], ALU.add).then_inc(sem("acc_made"), 1)

            with eng.Fori(0, KD // 2) as i:
                for k in range(2):
                    wait_freed(eng, C_GATE_A + 2 * k + 1, 4, i)
                    eng.dma_start(gated_dram[bass.ds(2 * i + k, 1)].rearrange("o p t -> p (o t)"), gated[:, k, :]).then_inc(sem(f"gated_out{k}"), 16)

            eng.wait_ge(sem("gated_out0"), 16 * (KD // 2))
            eng.wait_ge(sem("gated_out1"), 16 * (KD // 2))
            for j in range(2):
                eng.memset(conv_src[:, j, 0:3], 0.0).then_inc(sem("conv_zeros"), 1)
                eng.wait_ge(sem("conv_zeros"), j + 1)

            def conv_io(key):
                n, ct = conv_n[key], src_tile(key)
                seqs = conv_src[:, n % 2, 3 + TP:SRC].rearrange("p (b t) -> p b t", b=NB)
                if n >= 2:
                    eng.wait_ge(sem("conv_made"), n - 1)
                eng.tensor_copy(seqs[:, :, 0:3], conv_in[:, ct, :].rearrange("p (b t) -> p b t", b=NB)).then_inc(sem("conv_heads"), 1)
                eng.wait_ge(sem("conv_heads"), n + 1)
                wait_freed(eng, tile_of[key])
                eng.tensor_copy(conv_out[:, ct, 0:3], conv_src[:, n % 2, TP:TP + 3]).then_inc(sem("conv_tail_made"), 1)
                eng.wait_ge(sem("conv_tail_made"), n + 1)
                eng.tensor_copy(conv_out[:, ct, 3:27].rearrange("p (b t) -> p b t", b=NB), seqs[:, :, TD:TD + 3]).then_inc(sem("conv_tails"), 1)
                eng.wait_ge(sem("conv_tails"), n + 1)

            def old_states_in(g, b):
                n = g * NB + b
                if n >= 2:
                    eng.wait_ge(sem(f"state_stored{b % 2}"), 16 * (n // 2))
                eng.dma_start(old[:, b % 2], state_ssm[0, b, g * HG:(g + 1) * HG].rearrange("(j e) p n -> (e p) j n", e=2)).then_inc(sem(f"state_in{b % 2}"), 16)

            for key in group_inputs(0):
                conv_io(key)
            for g in range(NG):
                eng.wait_ge(sem("b_tok_made"), g + 1)
                if g:
                    wait_full(eng, ("new_state", g - 1, NB - 1))
                eng.tensor_tensor(b_seq[:, :, :], b_tok[0:TS, NC, :].unsqueeze(1).to_broadcast([TS, NB, P]),
                                  in_seq[:, :].unsqueeze(2).to_broadcast([TS, NB, P]), ALU.mult).then_inc(sem("b_seq_made"), 1)
                eng.wait_ge(sem("b_seq_made"), g + 1)
                slots = list(ssd_slots[g])
                for c in range(5):
                    st = g * 5 + c
                    m = P if c < NC else TS
                    mask = after if c < NC else after_b
                    if st:
                        wait_full(eng, ("seg", (st - 1) // 5, (st - 1) % 5, 1))
                    if g and c == 0:
                        eng.wait_ge(sem("y_scaled"), PG * g)
                    eng.tensor_tensor(a_after[0:m, :, 0:m], mask[0:m, 0:m].unsqueeze(1).to_broadcast([m, HG, m]),
                                      dt_tok[0:m, c, NH + g * HG:NH + (g + 1) * HG].unsqueeze(2).to_broadcast([m, HG, m]),
                                      ALU.mult).then_inc(sem("a_after_made"), 1)
                    eng.wait_ge(sem("a_after_made"), st + 1)
                    if c < NC:
                        for b in (2 * c, 2 * c + 1):
                            old_states_in(g, b)
                    for key in slots[2 * c:2 * c + 2]:
                        if key[0] in ("bc", "x"):
                            conv_io(key)
                    if c < NC:
                        for b in (2 * c, 2 * c + 1):
                            wait_full(eng, ("old_t", g, b))
                            eng.tensor_tensor(old[:, b % 2], old[:, b % 2],
                                              seq_decay[:, g * PG:(g + 1) * PG, b:b + 1].to_broadcast([P, PG, P]), ALU.mult)\
                               .then_inc(sem("old_decayed"), 1)
                            eng.wait_ge(sem("old_decayed"), g * NB + b + 1)
                        for b in (2 * c, 2 * c + 1):
                            wait_after_read(eng, ("new_state", g, b))
                            eng.dma_start(ssm_sample[0, b, g * HG:(g + 1) * HG].rearrange("(j e) p n -> (e p) j n", e=2), old[:, b % 2]).then_inc(sem(f"state_stored{b % 2}"), 16)
                wait_after_read(eng, ("state_out", g))
                eng.dma_start(ssm_prompt[0, 0, g * HG:(g + 1) * HG].rearrange("(j e) p n -> (e p) j n", e=2), state_out[:, :, :]).then_inc(sem("stored_prompt_state"), 16)
            for n in range(2):
                eng.wait_ge(sem(f"state_stored{n}"), 16 * NG * NB // 2)
            eng.wait_ge(sem("stored_prompt_state"), 16 * NG)
            eng.wait_ge(sem("y_split"), NG)
            eng.wait_ge(tile_done, T_GATE_B)
            eng.dma_start(x_again[:, 0:NC, :], x_prompt[0].rearrange("(c p) n -> p c n", p=P)).then_inc(sem("x_again_in"), 16)
            eng.dma_start(x_again[0:TS, NC, :], x_sample.rearrange("b t n -> (b t) n")).then_inc(sem("x_again_in"), 16)
            with eng.Fori(0, KD // 2) as i:
                for k in range(2):
                    eng.wait_ge(sem("merged_split"), k + 1 + 2 * i)
                    eng.dma_start(gated_in[:, k, :], gated_dram[bass.ds(2 * i + k, 1)].rearrange("o p t -> p (o t)")).then_inc(sem(f"gated_back{k}"), 16)
            for j in range(6):
                wait_after_read(eng, ("conv_out", j))
            eng.dma_start(conv_prompt[0, 0], conv_rows[0:3, :]).then_inc(sem("stored_conv"), 16)
            eng.dma_start(conv_sample[0].rearrange("b t n -> (b t) n"), conv_rows[3:27, :]).then_inc(sem("stored_conv"), 16)
            eng.wait_ge(sem("stored_conv"), 32)
            eng.wait_ge(sem("stored_v"), 32)
            with eng.Fori(0, KD) as i:
                eng.wait_ge(sem("y_tok_made"), i + 2)
                eng.dma_start(y_prompt[0].rearrange("(c p) n -> p c n", p=P)[:, :, bass.ds(P * i, P)], y_tok[:, 0:NC, :]).then_inc(sem("y_out"), 16)
                eng.dma_start(y_sample.rearrange("b t n -> (b t) n")[:, bass.ds(P * i, P)], y_tok[0:TS, NC, :]).then_inc(sem("y_out_s"), 16)
            eng.wait_ge(sem("y_out"), 16 * KD)
            eng.wait_ge(sem("y_out_s"), 16 * KD)

        @block.tensor
        def _(pe):
            for k in range(2):
                pe.sem_inc(tile_free[k], 1)
            pe.wait_ge(sem("constants"), sem_const_first[0])
            pe.wait_ge(sem("par_in"), 16 * 9)
            pe.transpose(spare(("par", 0))[:, 0:5 * CT], par_rows[:, :], ident[0:5 * CT, 0:5 * CT]).then_inc(bank_full[use[("par", 0)][0]], 1)
            pe.wait_ge(sem("d_spread"), 1)
            pe.transpose(spare(("par", 1))[:, 0:50], par2_rows[:, :], ident[0:50, 0:50]).then_inc(bank_full[use[("par", 1)][0]], 1)
            pe.wait_ge(sem("conv_state_in"), 16)
            for j in range(2):
                for n in range(12):
                    ct = 12 * j + n
                    mm = pe.transpose(spare(("conv_in", j))[:, 24 * n:24 * n + 24], sc_rows[:, ct * P:(ct + 1) * P], ident[0:24, 0:24])
                mm.then_inc(bank_full[use[("conv_in", j)][0]], 1)
            pe.wait_ge(sem("x_scaled"), 5)
            for k in range(KD):
                for j in range(2):
                    key = ("x", k, j)
                    wait_read(pe, key)
                    for c, t0, m in (token_tiles()[0:NC] if j == 0 else token_tiles()[NC:]):
                        mm = pe.transpose(spare(key)[:, t0 % TP:t0 % TP + m], x_tok[0:m, c, k * P:(k + 1) * P], ident[0:m, 0:m])
                    mm.then_inc(bank_full[use[key][0]], 1)
            for key in [("x", k, j) for k in (KD - 2, KD - 1) for j in range(2)]:
                wait_after_read(pe, key)

            def norm_sums(n):
                pe.wait_ge(sem("squared"), n + 1)
                for h in range(2):
                    key = ("ss", n, h)
                    wait_read(pe, key)
                    pe.matmul(spare(key)[:, 0:HALF], pair_ones[:, :], sq[:, n % 2, HALVES[h]]).then_inc(bank_full[use[key][0]], 1)

            for c in range(N_FIRST):
                chunk_tile(pe, c, c, x_hi, x_lo, width=P if c < N_FIRST - 1 else NH)
                if 1 <= c <= KD + 2:
                    norm_sums(c - 1)
            for n in range(2):
                wait_freed(pe, KD + 2 + n)
                for c, t0, m in token_tiles():
                    key = ("v", n, c)
                    wait_read(pe, key)
                    pe.transpose(spare(key)[0:m, 0:P], v_t[:, n, t0:t0 + m], ident[:, :]).then_inc(bank_full[use[key][0]], 1)
            pe.wait_ge(sem("qk_made"), 2 * (KD + 2))
            for c, t0, m in token_tiles():
                key = ("k", c)
                wait_read(pe, key)
                for g in range(NKV):
                    mm = pe.transpose(spare(key)[0:m, g * HD:(g + 1) * HD], k_t[0:HD, g, t0:t0 + m], ident[0:HD, 0:HD])
                mm.then_inc(bank_full[use[key][0]], 1)
            key = ("dt", 0)
            wait_read(pe, key)
            pe.wait_ge(sem("dt_made"), 1)
            for c, t0, m in token_tiles():
                mm = pe.transpose(spare(key)[0:m, 2 * NH * c:2 * NH * (c + 1)], dt_t[:, t0:t0 + m], ident[0:2 * NH, 0:2 * NH])
            mm.then_inc(bank_full[use[key][0]], 1)

            pe.wait_ge(sem("constants"), sem_const_all[0])
            for t in (N_FIRST - 1, N_FIRST - 2):
                wait_freed(pe, t)
            for key in keys[FIRST_USES - 4:FIRST_USES]:
                wait_after_read(pe, key)

            def turn_pages(x):
                for b in range(SEQS):
                    n = x["page"] + b
                    pe.wait_ge(sem(f"k_page_in{n % K_SLOTS}"), 16 * (n // K_SLOTS + 1))
                    if n >= 2:
                        pe.wait_ge(sem(f"kt_made{n % 2}"), n // 2)
                    for g in range(NKV):
                        mm = pe.transpose(W[2 + n % 2][0:HD, g * P:(g + 1) * P], k_page[:, n % K_SLOTS, g * HD:(g + 1) * HD], ident[:, :])
                    mm.then_inc(sem("k_turned"), 1)

            def logits(x):
                u = x["u"]
                if u >= 4:
                    pe.wait_ge(sem("weights_made"), u - 3)
                out = score_bank(u)
                if x["kind"] == "prompt":
                    g, i, j = x["g"], x["i"], x["j"]
                    masked = i == j
                    mm = pe.matmul(out[:, :], k_t[:, g, j * P:(j + 1) * P], q_t[:, g * QG:(g + 1) * QG, i * P:(i + 1) * P],
                                   start=True, stop=not masked, skip_group_check=True)
                    if masked:
                        mm = pe.matmul(out[:, :], big_diag[:, :], bad_prompt[:, :, :], start=False, stop=True, skip_group_check=True)
                else:
                    for b in range(SEQS):
                        q0 = TP + (x["h"] * SEQS + b) * TD
                        if x["kind"] == "page":
                            n = x["page"] + b
                            pe.wait_ge(sem(f"kt_made{n % 2}"), n // 2 + 1)
                            if b == 0:
                                pe.wait_ge(sem("kt_ones"), 1)
                        for g in range(NKV):
                            if x["kind"] == "page":
                                keys_t, m = kt_page[:, n % 8, g, :], P
                            else:
                                keys_t, m = k_t[:, g, TP:T], TS
                            at = (b * NKV + g) * QG * TD
                            mm = pe.matmul(out[0:m, at:at + QG * TD], keys_t, q_t[:, g * QG:(g + 1) * QG, q0:q0 + TD],
                                           start=b == 0 and g == 0, stop=True, skip_group_check=True)
                    if x["kind"] == "new":
                        mm = pe.matmul(out[0:TS, :], big_diag[0:TS, 0:TS], bad_new[:, x["h"]].rearrange("p b x t -> p (b x t)"),
                                       start=False, stop=True, skip_group_check=True)
                mm.then_inc(sem("logits_done"), 1)

            def subtract_sums(x):
                u = x["u"]
                m = TS if x["kind"] == "new" else P
                pe.wait_ge(sem("sp_made"), u + 1)
                mm = pe.matmul(score_bank(u)[0:m, :], neg_suffix[0:m, 0:m], sp[0:m, u % 4, :], start=False, stop=x["n"] == 0, skip_group_check=True)
                if x["n"]:
                    if x["n"] >= 2:
                        pe.wait_ge(sem("acc_made"), x["accs"])
                    later = sp[:, (u - 1) % 4, :] if x["n"] == 1 else acc[:, u % 2, :]
                    mm = pe.matmul(score_bank(u)[:, :], neg_ones[:, :], later, start=False, stop=True, skip_group_check=True)
                mm.then_inc(sem("sums_done"), 1)

            def weigh_values(x):
                u, ch = x["u"], x["chain"]
                out = W[ch % 2]
                pe.wait_ge(sem("weights_made"), u + 1)
                if x["n"] == 0 and ch >= 2:
                    pe.wait_ge(sem("out_read"), ch - 1)
                if x["kind"] == "prompt":
                    g = x["g"]
                    mm = pe.matmul(out[0:HD, :], v_tok[:, x["j"], g * HD:(g + 1) * HD], wts[:, u % 2, :], start=x["n"] == 0, stop=x["last"], skip_group_check=True)
                else:
                    for b in range(SEQS):
                        if x["kind"] == "page":
                            n = x["page"] + b
                            pe.wait_ge(sem(f"v_page_in{n % 8}"), 16 * (n // 8 + 1))
                        for g in range(NKV):
                            if x["kind"] == "page":
                                v, m = v_page[:, n % 8, g * HD:(g + 1) * HD], P
                            else:
                                v, m = v_tok[0:TS, NC, g * HD:(g + 1) * HD], TS
                            at = (b * NKV + g) * QG * TD
                            mm = pe.matmul(out[0:HD, at:at + QG * TD], v, wts[0:m, u % 2, at:at + QG * TD],
                                           start=x["n"] == 0 and b == 0 and g == 0, stop=x["last"], skip_group_check=True)
                mm.then_inc(sem("pv_done"), 1)

            for t in range(NU + 3):
                if t < NU:
                    logits(units[t])
                if t + 1 < NU and units[t + 1]["kind"] == "page":
                    turn_pages(units[t + 1])
                if 2 <= t < NU + 2:
                    subtract_sums(units[t - 2])
                if t >= 3:
                    weigh_values(units[t - 3])

            pe.wait_ge(sem("weights_made"), NU)
            pe.wait_ge(sem("out_read"), units[-1]["chain"] + 1)
            with pe.Fori(0, KD) as i:
                chunk_tile(pe, C_GATE_A, C_GATE_A, x_hi, x_lo, 2, i)
                chunk_tile(pe, C_GATE_A + 1, C_GATE_A + 1, o_hi, o_lo, 2, i)

            key = ("decays", 0)
            pe.wait_ge(sem("kt_made1"), NB * PAGES // 2)
            pe.wait_ge(sem("kt_made0"), NB * PAGES // 2)
            pe.wait_ge(sem("out_read"), units[-1]["chain"] + 1)
            out = spare(key)
            for c, t0, m in token_tiles():
                mask = after if c < NC else after_b
                pe.matmul(out[0:m, NH * c:NH * (c + 1)], mask[0:m, 0:m], dt_tok[0:m, c, NH:2 * NH], start=c == 0, stop=True, skip_group_check=True)
            for c in range(NC):
                pe.matmul(out[:, 256 + NH * c:256 + NH * (c + 1)], ones[:, :], dt_tok[:, c, NH:2 * NH], start=False, stop=True, skip_group_check=True)
            for h in range(NH):
                j, rows = h // 2, slice(h % 2 * HD, (h % 2 + 1) * HD)
                mm = pe.matmul(out[rows, 384 + NB * j:384 + NB * (j + 1)], dt_tok[0:TS, NC, NH + h:NH + h + 1].to_broadcast([TS, HD]),
                               in_seq[:, :], start=False, stop=True, skip_group_check=True)
            mm.then_inc(bank_full[use[key][0]], 1)

            def gemm(key):
                c, t = chunk_of[key], tile_of[key]
                if key[0] != "pb":
                    chunk_tile(pe, c, t, x_hi, x_lo)
                    return
                pe.wait_ge(split, c + 1)
                pe.wait_ge(sem("y_split"), key[1] + 1)
                wh = w_hi[:, c % 2].rearrange("p t n -> p (t n)").rearrange("p (t n) -> p t n", t=PG)
                wl = w_lo[:, c % 2].rearrange("p t n -> p (t n)").rearrange("p (t n) -> p t n", t=PG)
                for n in range(2):
                    w = [(wh[:, k, n * P:(n + 1) * P], wl[:, k, n * P:(n + 1) * P]) for k in range(PG)]
                    mm = product(pe, t + n, w, [(y_hi[:, k, :], y_lo[:, k, :]) for k in range(PG)])
                    mm.then_inc(tile_done, 1)

            def by_token(g):
                pe.wait_ge(sem("conv_done"), 6 * (g + 1))
                for c, t0, m in token_tiles():
                    key = ("x_tok", g, c)
                    wait_read(pe, key)
                    for j in range(PG):
                        mm = pe.transpose(spare(key)[0:m, j * P:(j + 1) * P], xs_t[:, j, t0:t0 + m], ident[:, :])
                    mm.then_inc(bank_full[use[key][0]], 1)
                b_t, c_t = bc_t[:, g % 2, 0, :], bc_t[:, g % 2, 1, :]
                key = ("b_tok", g)
                wait_read(pe, key)
                for c in range(NC):
                    mm = pe.transpose(spare(key)[:, c * P:(c + 1) * P], b_t[:, c * P:(c + 1) * P], ident[:, :])
                mm.then_inc(bank_full[use[key][0]], 1)
                key = ("cb", g)
                wait_read(pe, key)
                for c in range(NC):
                    mm = pe.matmul(spare(key)[:, c * P:(c + 1) * P], b_t[:, c * P:(c + 1) * P], c_t[:, c * P:(c + 1) * P],
                                   start=c == 0, stop=True, skip_group_check=True)
                mm.then_inc(bank_full[use[key][0]], 1)
                key = ("sample_bc", g)
                wait_read(pe, key)
                pe.transpose(spare(key)[0:TS, 0:P], b_t[:, TP:T], ident[:, :])
                pe.matmul(spare(key)[0:TS, P:P + TS], b_t[:, TP:T], c_t[:, TP:T], start=True, stop=True,
                          skip_group_check=True).then_inc(bank_full[use[key][0]], 1)

            def segments(g, c):
                m = P if c < NC else TS
                mask = upto if c < NC else upto_b
                key = ("e", g, c)
                if c:
                    wait_read(pe, key)
                for h in range(HG if c else 0):
                    j, rows = h // 2, slice(h % 2 * HD, (h % 2 + 1) * HD)
                    a = dt_tok[0:m, c, NH + g * HG + h:NH + g * HG + h + 1].to_broadcast([m, HD])
                    mm = pe.matmul(spare(key)[rows, j * P:j * P + m], a, mask[0:m, 0:m], start=j == 0, stop=True, skip_group_check=True)
                if c:
                    mm.then_inc(bank_full[use[key][0]], 1)
                pe.wait_ge(sem("a_after_made"), g * 5 + c + 1)
                for q in range(2):
                    key = ("seg", g, c, q)
                    wait_read(pe, key)
                    for e in range(4):
                        mm = pe.matmul(spare(key)[0:m, e * P:e * P + m], a_after[0:m, 4 * q + e, 0:m], mask[0:m, 0:m],
                                       start=e == 0, stop=True, skip_group_check=True)
                    mm.then_inc(bank_full[use[key][0]], 1)

            def outputs(g, c):
                st = g * 5 + c
                m = P if c < NC else TS
                if 0 < c < NC:
                    key = ("y_chunk_old", g, c)
                    wait_read(pe, key)
                    wait_after_read(pe, ("state", g, c - 1))
                    for j in range(PG):
                        mm = pe.matmul(spare(key)[:, j * P:(j + 1) * P], state[:, (c - 1) % 2, j * P:(j + 1) * P],
                                       bc_t[:, g % 2, 1, c * P:(c + 1) * P], start=j == 0, stop=True, skip_group_check=True)
                    mm.then_inc(bank_full[use[key][0]], 1)
                if c < NC:
                    key = ("state", g, c)
                    wait_read(pe, key)
                    pe.wait_ge(sem("xend_made"), g * NC + c + 1)
                    pe.matmul(spare(key)[:, :], b_tok[:, c, :], xend[:, c % 2].rearrange("p h d -> p (h d)")).then_inc(bank_full[use[key][0]], 1)
                key = ("y_new", g, c)
                wait_read(pe, key)
                pe.wait_ge(sem("decay_made"), st + 1)
                for j in range(PG):
                    for e in range(2):
                        h = 2 * j + e
                        mm = pe.matmul(spare(key)[e * HD:(e + 1) * HD, j * P:j * P + m], xdt[0:m, c, h, :], decay[0:m, h, 0:m],
                                       start=j == 0, stop=True, skip_group_check=True)
                mm.then_inc(bank_full[use[key][0]], 1)

            def sequence(g, b):
                n = g * NB + b
                key = ("old_t", g, b)
                wait_read(pe, key)
                pe.wait_ge(sem(f"state_in{b % 2}"), 16 * (n // 2 + 1))
                for j in range(PG):
                    mm = pe.transpose(spare(key)[:, j * P:(j + 1) * P], old[:, b % 2, j, :], ident[:, :])
                mm.then_inc(bank_full[use[key][0]], 1)
                key = ("y_seq_old", g, b)
                wait_read(pe, key)
                wait_after_read(pe, ("old_t", g, b))
                for j in range(PG):
                    mm = pe.matmul(spare(key)[:, j * TD:(j + 1) * TD], old_t[:, b % 2, j, :],
                                   bc_t[:, g % 2, 1, TP + b * TD:TP + (b + 1) * TD], start=j == 0, stop=True, skip_group_check=True)
                mm.then_inc(bank_full[use[key][0]], 1)
                key = ("new_state", g, b)
                wait_read(pe, key)
                pe.wait_ge(sem("b_seq_made"), g + 1)
                pe.wait_ge(sem("xend_s_made"), g + 1)
                for j in range(PG):
                    mm = pe.matmul(spare(key)[:, j * P:(j + 1) * P], xend_s[:, 2 * j:2 * j + 2, :].rearrange("p h d -> p (h d)"),
                                   b_seq[:, b, :], start=j == 0, stop=True, skip_group_check=True)
                mm.then_inc(bank_full[use[key][0]], 1)

            for key in group_inputs(0):
                gemm(key)
            for g in range(NG):
                by_token(g)
                slots = list(ssd_slots[g])
                for c in range(5):
                    segments(g, c)
                    for key in slots[2 * c:2 * c + 1]:
                        gemm(key)
                    outputs(g, c)
                    for key in slots[2 * c + 1:2 * c + 2]:
                        gemm(key)
                    if c < NC:
                        for b in (2 * c, 2 * c + 1):
                            sequence(g, b)
                key = ("state_out", g)
                wait_read(pe, key)
                wait_after_read(pe, ("state", g, NC - 1))
                for j in range(PG):
                    mm = pe.transpose(spare(key)[:, j * P:(j + 1) * P], state[:, (NC - 1) % 2, j * P:(j + 1) * P], ident[:, :])
                mm.then_inc(bank_full[use[key][0]], 1)
                for j in range(PG):
                    pe.wait_ge(sem("y_squared"), PG * g + j + 1)
                    for h in range(2):
                        key = ("y_ss", g, h)
                        if j == 0:
                            wait_read(pe, key)
                        mm = pe.matmul(spare(key)[:, 0:HALF], ones[:, :], conv_acc[:, j % 2, HALVES[h]], start=j == 0, stop=j == PG - 1, skip_group_check=True)
                        if j == PG - 1:
                            mm.then_inc(bank_full[use[key][0]], 1)
                    if j < 2:
                        mm.then_inc(sem("y_summed"), 1)
                for n0 in range(0, KD, 2):
                    gemm(("pb", g, n0))

            with pe.Fori(0, KD // 2) as i:
                for k in range(2):
                    chunk_tile(pe, C_GATE_B + k, T_GATE_B + k, x_hi, x_lo, 2, i)
            pe.wait_ge(sem("conv_tails"), CT)
            for j in range(6):
                key = ("conv_out", j)
                wait_read(pe, key)
                for n in range(4):
                    mm = pe.transpose(spare(key)[0:27, n * P:(n + 1) * P], conv_out[:, 4 * j + n, :], ident[:, :])
                mm.then_inc(bank_full[use[key][0]], 1)
            for key in keys[N_USES - 4:]:
                wait_after_read(pe, key)
            pe.wait_ge(sem("merged_split"), KD + 2)
            pe.wait_ge(sem("x_again_in"), 32)

            def res_sums(n):
                pe.wait_ge(sem("res_squared"), n + 1)
                for h in range(2):
                    mm = pe.matmul(W[h][:, 0:HALF], ones[:, :], prod2[:, n % 2, HALVES[h]], start=n == 0, stop=n == KD - 1, skip_group_check=True)
                mm.then_inc(sem("res_summed"), 1)

            for n in range(KD):
                c, t = C_OUT + n, T_OUT + n
                pe.wait_ge(tile_free[t % 2], t // 2 + 1)
                begun = set()
                for cc, t0, m in token_tiles():
                    for h in range(2):
                        a, z = max(t0, HALF * h), min(t0 + m, HALF * (h + 1))
                        if a < z:
                            pe.matmul(G[t % 2][:, h, a - HALF * h:z - HALF * h], x_again[0:m, cc, n * P:(n + 1) * P],
                                      ident[0:m, a - t0:z - t0], start=h not in begun, stop=True, skip_group_check=True)
                            begun.add(h)
                pe.wait_ge(split, c + 1)
                w = [(w_hi[:, c % 2, k, :], w_lo[:, c % 2, k, :]) for k in range(KD)]
                mm = product(pe, t, w, [(m_hi[:, k, :], m_lo[:, k, :]) for k in range(KD)], start=False, onto=True)
                mm.then_inc(tile_done, 1)
                if n:
                    res_sums(n - 1)
            res_sums(KD - 1)
            pe.wait_ge(sem("h2_split"), KD)
            with pe.Fori(0, KF) as i:
                for k in range(2):
                    chunk_tile(pe, C_FFN + k, T_FFN + k, x_hi, x_lo, 2, i)
            pe.wait_ge(sem("f_split"), KF + 2)
            with pe.Fori(0, KD // 2) as i:
                for n in range(2):
                    for k, (k0, kn) in enumerate(DOWN_K):
                        c = C_DOWN + 3 * n + k
                        pe.wait_ge(split, c + 1 + 6 * i)
                        w = [(w_hi[:, c % 2, q, :], w_lo[:, c % 2, q, :]) for q in range(kn)]
                        x = [(f_hi[:, k0 + q, :], f_lo[:, k0 + q, :]) for q in range(kn)]
                        mm = product(pe, T_DOWN + n, w, x, start=k == 0, stop=k == 2, step=2, i=i)
                        mm.then_inc(tile_done if k == 2 else part_done, 1)
                    wait_freed(pe, T_DOWN + n, 2, i)
                    for cc, t0, m in token_tiles():
                        if cc < NC:
                            if cc == 0:
                                pe.wait_ge(sem("y_tok_made"), n + 1 + 2 * i)
                            mm = pe.transpose(W[2][:, cc * P:(cc + 1) * P], prod2[:, n, t0:t0 + m], ident[:, :])
                        else:
                            mm = pe.transpose(W[3][0:m, 0:P], prod2[:, n, t0:t0 + m], ident[:, :])
                    mm.then_inc(sem("y_turned"), 1)

        @block.scalar
        def _(act):
            eng = act
            eng.dma_start(par_rows[0:CW * CT, :], conv_w[0].rearrange("w (t p) -> (w t) p", p=P)).then_inc(sem("par_in"), 16)
            eng.dma_start(par_rows[CW * CT:5 * CT, :], conv_b[0].rearrange("(t p) -> t p", p=P)).then_inc(sem("par_in"), 16)
            for at, w, n in ((PAR_N1, norm1_w, KD), (PAR_N2, norm2_w, KD), (PAR_SSD, ssd_norm_w, DI // P)):
                eng.dma_start(par2_rows[at:at + n, :], w[0].rearrange("(t p) -> t p", p=P)).then_inc(sem("par_in"), 16)
            for at, w in ((PAR_Q, q_norm_w), (PAR_K, k_norm_w)):
                for e in range(2):
                    eng.dma_start(par2_rows[at:at + 1, e * HD:(e + 1) * HD], w).then_inc(sem("par_in"), 16)
            eng.dma_start(d_rows[32:48, :], d_skip[0].rearrange("(j e) -> j e", e=2)).then_inc(sem("d_in"), 16)
            eng.dma_start(dt_par[:, 0:1], dt_bias[0].rearrange("(h o) -> h o", o=1)).then_inc(sem("dt_par_in"), 16)
            eng.dma_start(dt_par[:, 1:2], a_log[0].rearrange("(h o) -> h o", o=1)).then_inc(sem("dt_par_in"), 16)
            eng.dma_start(sc_rows[:, :], state_conv[0].rearrange("b t c -> (b t) c")).then_inc(sem("conv_state_in"), 16)

            eng.wait_ge(sem("constants"), sem_const_first[0])
            eng.wait_ge(sem("x_in"), 32)
            for c, t0, m in token_tiles():
                junk = (o_hi if c < NC else o_lo)[0:m, 2 * (c % NC):2 * (c % NC) + 2, 0:512]
                eng.activation(junk, x_tok[0:m, c, :].rearrange("p (a b) -> p a b", a=2), ACT.Square,
                               accum_out=stats[0:m, 0, c:c + 1]).then_inc(sem("x_squared"), 1)
            eng.wait_ge(sem("x_squared"), 5)
            eng.activation(stats[:, 1, :], stats[:, 0, :], ACT.Sqrt, scale=1.0 / D, bias=eps_col[:, 0:1]).then_inc(sem("x_rooted"), 1)
            make_hi(0)
            for j, dst in ((0, conv_par), (1, par)):
                key = ("par", j)
                wait_full(eng, key)
                n = 5 * CT if j == 0 else 50
                eng.activation(dst[:, :], spare(key)[:, 0:n], ACT.Copy).then_inc(bank_read[use[key][0]], 1)
            for j in range(2):
                key = ("conv_in", j)
                wait_full(eng, key)
                eng.activation(conv_in[:, 12 * j:12 * j + 12, :].rearrange("p t n -> p (t n)"), spare(key)[:, 0:288], ACT.Copy)\
                   .then_inc(bank_read[use[key][0]], 1)
            wait_after_read(eng, ("par", 1))
            for k in range(KD):
                for j in range(2):
                    wait_full(eng, ("x", k, j))
                    cols = slice(0, TP) if j == 0 else slice(TP, T)
                    n = TP if j == 0 else TS
                    eng.activation(x_hi[:, k, cols], spare(("x", k, j))[:, 0:n], ACT.Copy, scale=par[:, PAR_N1 + k:PAR_N1 + k + 1])\
                       .then_inc(sem("x_hi_made"), 1)

            def root_of_sums(n):
                for h in range(2):
                    key = ("ss", n, h)
                    wait_full(eng, key)
                    if n:
                        eng.wait_ge(sem("rinv_made"), n)
                    eng.activation(root[:, HALVES[h]], spare(key)[:, 0:HALF], ACT.Sqrt, scale=1.0 / HD, bias=eps_col[:, 0:1])\
                       .then_inc(bank_read[use[key][0]], 1)

            for c in range(N_FIRST):
                make_hi(c + 1, width=NH if c + 1 == N_FIRST - 1 else P, after_tiles=c if c else None)
                if 1 <= c <= KD + 2:
                    root_of_sums(c - 1)
                if c < KD + 2:
                    wait_freed(eng, c)
                    if c >= 2:
                        wait_full(eng, ("ss", c - 2, 1))
                    eng.activation(sq[:, c % 2, :], pre[:, c % 2, :], ACT.Square).then_inc(sem("squared"), 1)
            eng.wait_ge(sem("dt_par_in"), 32)
            eng.activation(dt_par[:, 2:3], dt_par[:, 1:2], ACT.Exp).then_inc(sem("a_exp"), 1)
            eng.wait_ge(sem("dt_clamped"), 1)
            eng.activation(dt_w[:, 1, :], dt_w[:, 1, :], ACT.Exp).then_inc(sem("dt_exp"), 1)
            eng.wait_ge(sem("dt_exp"), 1)
            eng.activation(dt_w[:, 1, :], dt_w[:, 1, :], ACT.Ln, bias=1.0).then_inc(sem("dt_ln"), 1)
            for n in range(2):
                for c, t0, m in token_tiles():
                    key = ("v", n, c)
                    wait_full(eng, key)
                    eng.activation(v_tok[0:m, c, n * P:(n + 1) * P], spare(key)[0:m, 0:P], ACT.Copy).then_inc(bank_read[use[key][0]], 1)
            for c, t0, m in token_tiles():
                key = ("k", c)
                wait_full(eng, key)
                eng.activation(k_out[0:m, c, :], spare(key)[0:m, 0:NKV * HD], ACT.Copy).then_inc(bank_read[use[key][0]], 1)
            key = ("dt", 0)
            wait_full(eng, key)
            n = NC * 2 * NH
            eng.activation(dt_tok[:, 0:NC, :].rearrange("p c h -> p (c h)"), spare(key)[:, 0:n], ACT.Copy)
            eng.activation(dt_tok[0:TS, NC, :], spare(key)[0:TS, n:n + 2 * NH], ACT.Copy).then_inc(bank_read[use[key][0]], 1)

            eng.preload_act_table_set("natural_log_exp_and_others")
            for key in [("k", c) for c in range(5)]:
                wait_after_read(eng, key)
            eng.wait_ge(sem("stored_k"), 32)

            def read_output(x):
                wait_chain(eng, x)
                for e in range(2):
                    src, hi, _ = chain_views(x, e)
                    eng.activation(hi, src, ACT.Copy).then_inc(sem("o_hi_made"), 1)

            for t in range(NU + 4):
                if t < NU:
                    x = units[t]
                    m = TS if x["kind"] == "new" else P
                    z = zs[0:m, t % 2, :]
                    eng.wait_ge(sem("clamped"), t + 1)
                    eng.activation(z, z, ACT.Exp).then_inc(sem("exp_made"), 1)
                    eng.wait_ge(sem("exp_made"), t + 1)
                    eng.activation(z, z, ACT.Ln, bias=1.0).then_inc(sem("ln_made"), 1)
                if t + 1 < NU and units[t + 1]["kind"] == "page":
                    for b in (0, 2):
                        read_turned(eng, nc.scalar.activation, units[t + 1], b)
                if 2 <= t < NU + 2:
                    u = t - 2
                    m = TS if units[u]["kind"] == "new" else P
                    eng.wait_ge(sem("sums_done"), u + 1)
                    if u >= 2:
                        eng.wait_ge(sem("pv_done"), u - 1)
                    eng.activation(wts[0:m, u % 2, :], score_bank(u)[0:m, :], ACT.Exp).then_inc(sem("weights_made"), 1)
                if t >= 4 and units[t - 4]["last"]:
                    read_output(units[t - 4])

            with eng.Fori(0, KD // 2) as i:
                for n in range(2):
                    c = C_GATE_A + 2 * n
                    make_hi(c + 1, 4, i, after_tiles=c + 4 * i)
                    wait_tile(eng, c, 4, i)
                    eng.wait_ge(tile_free[(c + 1) % 2], half(c + 1 - 4, 4, i) + 2)
                    eng.activation(halves(gate[:, n, :]), tile(c), ACT.Sigmoid).then_inc(tile_free[c % 2], 1)
                    make_hi(c + 2, 4, i, after_tiles=c + 1 + 4 * i)

            key = ("decays", 0)
            wait_full(eng, key)
            for e in range(2):
                eng.wait_ge(sem(f"gated_out{e}"), 16 * (KD // 2))
            src = spare(key)
            eng.activation(end_decay[:, 0:NC, :].rearrange("p c h -> p (c h)"), src[:, 0:NC * NH], ACT.Exp)
            eng.activation(end_decay[0:TS, NC, :], src[0:TS, NC * NH:5 * NH], ACT.Exp)
            eng.activation(chunk_decay[:, :, :].rearrange("p c h -> p (c h)"), src[:, 256:256 + NC * NH], ACT.Exp)
            eng.activation(seq_decay[:, :, :].rearrange("p j b -> p (j b)"), src[:, 384:384 + NB * NH // 2], ACT.Exp)\
               .then_inc(bank_read[use[key][0]], 1)

            def conv_silu(key):
                n = conv_n[key]
                dst = conv_dst(key)
                eng.wait_ge(sem("conv_made"), n + 1)
                src = conv_acc[:, n % 2, :]
                eng.activation(dst[:, 0:TP], src[:, 0:TP], ACT.Silu)
                eng.activation(decode_block(dst, TP), src[:, 3 + TP:SRC].rearrange("p (b t) -> p b t", b=NB)[:, :, 0:TD], ACT.Silu)\
                   .then_inc(sem("conv_done"), 1)

            pending = []

            def flush():
                while pending:
                    conv_silu(pending.pop(0))

            def slot(key):
                c, t = chunk_of[key], tile_of[key]
                if c + 1 < N_CHUNKS:
                    make_hi(c + 1, after_tiles=tiles_after(c - 1))
                if key[0] in ("bc", "x"):
                    n = conv_n[key]
                    wait_tile(eng, t)
                    eng.wait_ge(sem("conv_zeros"), 2)
                    if n >= 2:
                        eng.wait_ge(sem("conv_made"), n - 1)
                        eng.wait_ge(sem("conv_tails"), n - 1)
                    dst = conv_src[:, n % 2, :]
                    eng.activation(dst[:, 3:3 + HALF], G[t % 2][:, 0, 0:HALF], ACT.Copy)
                    eng.activation(dst[:, 3 + HALF:3 + TP], G[t % 2][:, 1, 0:TP - HALF], ACT.Copy)
                    eng.activation(dst[:, 3 + TP:SRC].rearrange("p (b t) -> p b t", b=NB)[:, :, 3:3 + TD],
                                   decode_block(G[t % 2][:, 1, :], TP - HALF), ACT.Copy).then_inc(tile_free[t % 2], 1)
                    flush()
                    pending.append(key)
                elif key[0] == "z":
                    flush()
                    wait_tile(eng, t)
                    if key[1]:
                        eng.wait_ge(sem("y_gated"), PG * key[1])
                    eng.activation(halves(z_s[:, key[2], :]), tile(t), ACT.Silu).then_inc(tile_free[t % 2], 1)

            def by_token(g):
                flush()
                if g:
                    wait_full(eng, ("state", g - 1, NC - 1))
                key = ("b_tok", g)
                wait_full(eng, key)
                eng.activation(b_tok[:, 0:NC, :].rearrange("p c n -> p (c n)"), spare(key)[:, :], ACT.Copy).then_inc(bank_read[use[key][0]], 1)
                key = ("sample_bc", g)
                wait_full(eng, key)
                if g:
                    eng.wait_ge(sem("b_seq_made"), g)
                eng.activation(b_tok[0:TS, NC, :], spare(key)[0:TS, 0:P], ACT.Copy).then_inc(sem("b_tok_made"), 1)

            def segments(g, c):
                st = g * 5 + c
                m = P if c < NC else TS
                if c:
                    key = ("e", g, c)
                    wait_full(eng, key)
                    if g * NC + c - 1:
                        eng.wait_ge(sem("y_added"), g * NC + c - 1)
                    eng.activation(e_t[:, :, 0:m], spare(key).rearrange("p (j l) -> p j l", l=P)[:, :, 0:m], ACT.Exp)\
                       .then_inc(bank_read[use[key][0]], 1)
                for q in range(2):
                    key = ("seg", g, c, q)
                    wait_full(eng, key)
                    if st:
                        wait_full(eng, ("y_new", (st - 1) // 5, (st - 1) % 5))
                    if g and c == 0:
                        eng.wait_ge(sem("y_scaled"), PG * g)
                    eng.activation(decay[0:m, 4 * q:4 * q + 4, 0:m], spare(key).rearrange("p (e l) -> p e l", l=P)[0:m, :, 0:m], ACT.Exp)\
                       .then_inc(bank_read[use[key][0]], 1)

            def sequence(g, b):
                key = ("old_t", g, b)
                wait_full(eng, key)
                n = g * NB + b
                if n >= 2:
                    wait_full(eng, ("y_seq_old", (n - 2) // NB, (n - 2) % NB))
                eng.activation(old_t[:, b % 2].rearrange("p j n -> p (j n)"), spare(key)[:, :], ACT.Copy).then_inc(bank_read[use[key][0]], 1)

            for key in group_inputs(0):
                slot(key)
            for g in range(NG):
                by_token(g)
                slots = list(ssd_slots[g])
                for c in range(5):
                    segments(g, c)
                    for key in slots[2 * c:2 * c + 2]:
                        slot(key)
                    if c < NC:
                        for b in (2 * c, 2 * c + 1):
                            sequence(g, b)
                flush()
                key = ("state_out", g)
                wait_full(eng, key)
                if g:
                    eng.wait_ge(sem("stored_prompt_state"), 16 * g)
                eng.activation(state_out[:, :, :].rearrange("p j n -> p (j n)"), spare(key)[:, :], ACT.Copy).then_inc(bank_read[use[key][0]], 1)
                for j in range(PG):
                    eng.wait_ge(sem("y_gated"), PG * g + j + 1)
                    if j >= 2:
                        eng.wait_ge(sem("y_summed"), 2 * g + j - 1)
                    eng.activation(conv_acc[:, j % 2, 0:T], y_t[:, j, :], ACT.Square).then_inc(sem("y_squared"), 1)
                for h in range(2):
                    key = ("y_ss", g, h)
                    wait_full(eng, key)
                    eng.activation(y_root[:, HALVES[h]], spare(key)[:, 0:HALF], ACT.Sqrt, scale=1.0 / (PG * P), bias=eps_col[:, 0:1])\
                       .then_inc(bank_read[use[key][0]], 1)
                for j in range(PG):
                    eng.wait_ge(sem("y_scaled"), PG * g + j + 1)
                    if g:
                        wait_tile(eng, tile_of[("pb", g - 1, KD - 2)] + 1)
                    eng.activation(y_hi[:, j, :], y_t[:, j, :], ACT.Copy).then_inc(sem("y_hi_made"), 1)
                for n0 in range(0, KD, 2):
                    slot(("pb", g, n0))

            for n in range(2):
                eng.wait_ge(sem(f"state_stored{n}"), 16 * NG * NB // 2)
            eng.wait_ge(sem("stored_prompt_state"), 16 * NG)
            with eng.Fori(0, KD // 2) as i:
                for n in range(2):
                    c, t = C_GATE_B + n, T_GATE_B + n
                    make_hi(c + 1, 2, i, after_tiles=t + 2 * i)
                    wait_tile(eng, t, 2, i)
                    eng.wait_ge(sem("merged_split"), n + 1 + 2 * i)
                    eng.activation(halves(gate2[:, n, :]), tile(t), ACT.Sigmoid).then_inc(tile_free[t % 2], 1)
                    eng.wait_ge(sem("merged_made"), n + 1 + 2 * i)
                    eng.activation(m_hi[:, bass.ds(2 * i + n, 1), :], prod2[:, n:n + 1, :], ACT.Copy).then_inc(sem("m_hi_made"), 1)
            eng.wait_ge(sem("x_again_in"), 32)
            for j in range(6):
                key = ("conv_out", j)
                wait_full(eng, key)
                eng.activation(conv_rows[:, 512 * j:512 * (j + 1)], spare(key)[0:27, :], ACT.Copy).then_inc(bank_read[use[key][0]], 1)

            def res_square(n):
                wait_freed(eng, T_OUT + n)
                if n >= 2:
                    eng.wait_ge(sem("res_summed"), n - 1)
                eng.activation(prod2[:, n % 2, :], x_res[:, n, :], ACT.Square).then_inc(sem("res_squared"), 1)

            for n in range(KD):
                make_hi(C_OUT + n + 1, after_tiles=T_OUT + n)
                res_square(n)
            eng.wait_ge(sem("res_summed"), KD)
            for h in range(2):
                eng.activation(root2[:, HALVES[h]], W[h][:, 0:HALF], ACT.Sqrt, scale=1.0 / D, bias=eps_col[:, 0:1]).then_inc(sem("res_rooted"), 1)
            for k in range(KD):
                eng.wait_ge(sem("h2_made"), k + 1)
                eng.activation(x_hi[:, k, :], gate2[:, k % 2, :], ACT.Copy).then_inc(sem("h2_hi_made"), 1)
            eng.wait_ge(sem("stored_conv"), 32)
            with eng.Fori(0, KF // 2) as i:
                for n in range(2):
                    c, t = C_FFN + 2 * n, T_FFN + 2 * n
                    make_hi(c + 1, 4, i, after_tiles=t + 4 * i)
                    wait_tile(eng, t, 4, i)
                    eng.wait_ge(tile_free[(t + 1) % 2], half(t + 1 - 4, 4, i) + 2)
                    eng.activation(halves(gate2[:, n, :]), tile(t), ACT.Silu).then_inc(tile_free[t % 2], 1)
                    make_hi(c + 2, 4, i, after_tiles=t + 1 + 4 * i)
                    wait_freed(eng, t + 1, 4, i)
                    eng.activation(f_hi[:, bass.ds(2 * i + n, 1), :], prod2[:, n:n + 1, :], ACT.Copy).then_inc(sem("f_hi_made"), 1)

            def down_tile(n, i, first=False, last=False):
                for k in range(3):
                    if last and n == 1 and k == 2:
                        continue
                    after_tiles = T_DOWN + n + 2 * i if k == 0 else None
                    after_part = {0: None, 1: 2 * n + 1 + 4 * i, 2: 2 * n + 2 + 4 * i}[k]
                    make_hi(C_DOWN + 3 * n + k + 1, 6, i, tiles=DOWN_K[(k + 1) % 3][1], after_tiles=after_tiles, after_part=after_part)
                eng.wait_ge(sem("y_turned"), n + 1 + 2 * i)
                if not first or n:
                    eng.wait_ge(sem("y_out"), 16 * (n + 2 * i))
                    eng.wait_ge(sem("y_out_s"), 16 * (n + 2 * i))
                eng.activation(y_tok[:, 0:NC, :].rearrange("p c n -> p (c n)"), W[2][:, :], ACT.Copy)
                eng.activation(y_tok[0:TS, NC, :], W[3][0:TS, 0:P], ACT.Copy).then_inc(sem("y_tok_made"), 1)

            eng.sem_inc(sem("y_tok_made"), 1)
            for n in range(2):
                down_tile(n, 0, first=True)
            with eng.Fori(1, KD // 2 - 1) as i:
                for n in range(2):
                    down_tile(n, i)
            for n in range(2):
                down_tile(n, KD // 2 - 1, last=True)

        @block.vector
        def _(dve):
            eng = dve
            n_chain = [0]
            chain = sem("dve_chain")

            def link(ins):
                n_chain[0] += 1
                ins.then_inc(chain, 1)
                eng.wait_ge(chain, n_chain[0])

            eng.wait_ge(sem("d_in"), 16)
            eng.tensor_copy(par2_rows[32:48, :].rearrange("j (e p) -> j e p", e=2), d_rows[32:48, :].unsqueeze(2).to_broadcast([16, 2, HD]))\
               .then_inc(sem("d_spread"), 1)
            make_lo(0)
            eng.wait_ge(sem("x_rooted"), 1)
            link(eng.reciprocal(stats[:, 2, :], stats[:, 1, :]))
            for c, t0, m in token_tiles():
                eng.tensor_scalar(x_tok[0:m, c, :], x_tok[0:m, c, :], stats[0:m, 2, c:c + 1], None, ALU.mult).then_inc(sem("x_scaled"), 1)
            for k in range(KD):
                for j in range(2):
                    key = ("x", k, j)
                    eng.wait_ge(sem("x_hi_made"), 2 * k + j + 1)
                    cols = slice(0, TP) if j == 0 else slice(TP, T)
                    n = TP if j == 0 else TS
                    eng.scalar_tensor_tensor(out=x_lo[:, k, cols], in0=spare(key)[:, 0:n], scalar=par[:, PAR_N1 + k:PAR_N1 + k + 1],
                                             in1=f32(x_hi[:, k, cols]), op0=ALU.mult, op1=ALU.subtract).then_inc(bank_read[use[key][0]], 1)
            wait_after_read(eng, ("par", 1))
            link(eng.tensor_scalar(par[:, PAR_Q:PAR_Q + 1], par[:, PAR_Q:PAR_Q + 1], HD ** -0.5, None, ALU.mult))

            def finish_norm(n):
                for h in range(2):
                    wait_after_read(eng, ("ss", n, h))
                if n:
                    eng.wait_ge(sem("qk_made"), 2 * n)
                eng.reciprocal(rinv[:, :], root[:, :]).then_inc(sem("rinv_made"), 1)
                eng.wait_ge(sem("rinv_made"), n + 1)
                dst, at, col = (q_t, 2 * n, PAR_Q) if n < KD else (k_t, 2 * (n - KD), PAR_K)
                for e in range(2):
                    rows = slice(e * HD, (e + 1) * HD)
                    eng.scalar_tensor_tensor(out=dst[0:HD, at + e, :], in0=pre[rows, n % 2, :], scalar=par[rows, col:col + 1],
                                             in1=rinv[rows, :], op0=ALU.mult, op1=ALU.mult).then_inc(sem("qk_made"), 1)

            for c in range(N_FIRST):
                make_lo(c + 1, width=NH if c + 1 == N_FIRST - 1 else P)
                if c < KD + 2:
                    wait_tile(eng, c)
                    if c >= 2:
                        eng.wait_ge(sem("squared"), c - 1)
                        eng.wait_ge(sem("qk_made"), 2 * (c - 1))
                    eng.tensor_copy(halves(pre[:, c % 2, :]), tile(c)).then_inc(tile_free[c % 2], 1)
                elif c < N_FIRST - 1:
                    wait_tile(eng, c)
                    eng.tensor_copy(halves(v_t[:, c - KD - 2, :]), tile(c)).then_inc(tile_free[c % 2], 1)
                if 1 <= c <= KD + 2:
                    finish_norm(c - 1)
            c = N_FIRST - 1
            wait_tile(eng, c)
            eng.wait_ge(sem("dt_par_in"), 32)
            eng.tensor_scalar(halves(dt_w[:, 0, :]), tile(c, NH), dt_par[:, 0:1], None, ALU.add).then_inc(tile_free[c % 2], 1)
            wait_freed(eng, c)
            eng.tensor_scalar(dt_w[:, 1, :], dt_w[:, 0, :], CLAMP, None, ALU.min).then_inc(sem("dt_clamped"), 1)
            eng.wait_ge(sem("dt_ln"), 1)
            link(eng.tensor_tensor(dt_t[0:NH, :], dt_w[:, 0, :], dt_w[:, 1, :], ALU.max))
            eng.wait_ge(sem("a_exp"), 1)
            link(eng.tensor_scalar(dt_w[:, 0, :], dt_t[0:NH, :], dt_par[:, 2:3], None, ALU.mult))
            eng.tensor_scalar(dt_t[NH:2 * NH, :], dt_w[:, 0, :], -1.0, None, ALU.mult).then_inc(sem("dt_made"), 1)

            eng.wait_ge(sem("stored_k"), 32)

            def softplus(u):
                x = units[u]
                m = TS if x["kind"] == "new" else P
                eng.wait_ge(sem("ln_made"), u + 1)
                if u >= 4:
                    eng.wait_ge(sem("sums_done"), u - 2)
                    if units[u - 2]["accs"]:
                        eng.wait_ge(sem("acc_made"), units[u - 2]["accs"])
                if x["kind"] == "new":
                    link(eng.memset(sp[TS:P, u % 4, :], 0.0))
                eng.tensor_tensor(sp[0:m, u % 4, :], score_bank(u)[0:m, :], zs[0:m, u % 2, :], ALU.max).then_inc(sem("sp_made"), 1)

            for t in range(NU + 4):
                if t < NU:
                    m = TS if units[t]["kind"] == "new" else P
                    eng.wait_ge(sem("logits_done"), t + 1)
                    if t >= 2:
                        eng.wait_ge(sem("sp_made"), t - 1)
                    eng.tensor_scalar(zs[0:m, t % 2, :], score_bank(t)[0:m, :], CLAMP, None, ALU.min).then_inc(sem("clamped"), 1)
                if 1 <= t <= NU:
                    softplus(t - 1)
                if t + 1 < NU and units[t + 1]["kind"] == "page":
                    for b in (1, 3):
                        read_turned(eng, lambda o, i, f: nc.vector.tensor_copy(o, i), units[t + 1], b)
                if t >= 4 and units[t - 4]["last"]:
                    x = units[t - 4]
                    for e in range(2):
                        src, hi, lo = chain_views(x, e)
                        eng.wait_ge(sem("o_hi_made"), 2 * x["chain"] + 2)
                        ins = eng.tensor_tensor(lo, src, f32(hi), ALU.subtract)
                        if e:
                            ins.then_inc(sem("out_read"), 1)

            def gate_a_tiles(i, first=False):
                for n in range(2):
                    c = C_GATE_A + 2 * n
                    make_lo(c + 1, 4, i)
                    make_lo(c + 2, 4, i)
                    wait_tile(eng, c + 1, 4, i)
                    wait_freed(eng, c, 4, i)
                    if not first:
                        eng.wait_ge(sem(f"gated_out{n}"), 16 * i)
                    eng.tensor_tensor(halves(gated[:, n, :]), tile(c + 1), halves(gate[:, n, :]), ALU.mult).then_inc(tile_free[(c + 1) % 2], 1)

            gate_a_tiles(0, first=True)
            with eng.Fori(1, KD // 2) as i:
                gate_a_tiles(i)

            for e in range(2):
                eng.wait_ge(sem(f"gated_out{e}"), 16 * (KD // 2))

            def slot(key):
                c, t = chunk_of[key], tile_of[key]
                make_lo(c + 1)
                if key[0] in ("bc", "x"):
                    n, ct = conv_n[key], src_tile(key)
                    wait_freed(eng, t)
                    eng.wait_ge(sem("conv_heads"), n + 1)
                    if n >= 2:
                        eng.wait_ge(sem("conv_done"), n - 1)
                    src, dst, m = conv_src[:, n % 2, :], conv_acc[:, n % 2, 0:SRC - 3], SRC - 3
                    link(eng.tensor_scalar(dst, src[:, 0:m], conv_par[:, ct:ct + 1], conv_par[:, CW * CT + ct:CW * CT + ct + 1], ALU.mult, ALU.add))
                    for w in range(1, CW):
                        ins = eng.scalar_tensor_tensor(out=dst, in0=src[:, w:w + m], scalar=conv_par[:, w * CT + ct:w * CT + ct + 1],
                                                       in1=dst, op0=ALU.mult, op1=ALU.add)
                        if w < CW - 1:
                            link(ins)
                    ins.then_inc(sem("conv_made"), 1)
                elif key[0] == "pb":
                    _, g, n0 = key
                    for n in range(2):
                        wait_tile(eng, t + n)
                        dst = halves(pb_sum[:, n0 + n, :])
                        if g == 0:
                            ins = eng.tensor_copy(dst, tile(t + n))
                        else:
                            wait_freed(eng, tile_of[("pb", g - 1, n0)] + n)
                            ins = eng.tensor_tensor(dst, dst, tile(t + n), ALU.add)
                        ins.then_inc(tile_free[(t + n) % 2], 1)

            def by_token(g):
                eng.wait_ge(sem("conv_done"), 6 * (g + 1))
                wait_after_read(eng, ("decays", 0))
                if g:
                    eng.wait_ge(sem("y_split"), g)
                    wait_full(eng, ("y_new", g - 1, NC))
                for c, t0, m in token_tiles():
                    key = ("x_tok", g, c)
                    wait_full(eng, key)
                    eng.tensor_tensor(xdt[0:m, c], spare(key)[0:m, :].rearrange("p (h d) -> p h d", h=HG),
                                      dt_tok[0:m, c, g * HG:(g + 1) * HG].unsqueeze(2).to_broadcast([m, HG, HD]), ALU.mult)\
                       .then_inc(bank_read[use[key][0]], 1)
                for j in range(PG):
                    eng.tensor_scalar(y_t[:, j, :], xs_t[:, j, :], par[:, PAR_D + g * PG + j:PAR_D + g * PG + j + 1], None, ALU.mult)\
                       .then_inc(sem("y_begun"), 1)
                key = ("cb", g)
                wait_full(eng, key)
                eng.tensor_tensor(cb_m[:, 0:NC, :], spare(key).rearrange("p (c l) -> p c l", l=P),
                                  upto[:, :].unsqueeze(1).to_broadcast([P, NC, P]), ALU.mult).then_inc(bank_read[use[key][0]], 1)
                key = ("sample_bc", g)
                eng.wait_ge(sem("b_tok_made"), g + 1)
                eng.tensor_tensor(cb_m[0:TS, NC, 0:TS], spare(key)[0:TS, P:P + TS], upto_b[:, :], ALU.mult).then_inc(bank_read[use[key][0]], 1)
                wait_after_read(eng, ("x_tok", g, NC))
                if g:
                    wait_full(eng, ("new_state", g - 1, NB - 1))
                eng.tensor_tensor(xend_s[:, :, :], xdt[0:TS, NC], end_decay[0:TS, NC, g * HG:(g + 1) * HG].unsqueeze(2).to_broadcast([TS, HG, HD]),
                                  ALU.mult).then_inc(sem("xend_s_made"), 1)

            def prepare(g, c):
                m = P if c < NC else TS
                for q in range(2):
                    wait_after_read(eng, ("seg", g, c, q))
                wait_after_read(eng, ("cb", g) if c < NC else ("sample_bc", g))
                eng.tensor_tensor(decay[0:m, :, 0:m], decay[0:m, :, 0:m], cb_m[0:m, c, 0:m].unsqueeze(1).to_broadcast([m, HG, m]), ALU.mult)\
                   .then_inc(sem("decay_made"), 1)
                if c < NC:
                    wait_after_read(eng, ("x_tok", g, c))
                    n = g * NC + c
                    if n >= 2:
                        wait_full(eng, ("state", (n - 2) // NC, (n - 2) % NC))
                    eng.tensor_tensor(xend[:, c % 2], xdt[:, c], end_decay[:, c, g * HG:(g + 1) * HG].unsqueeze(2).to_broadcast([P, HG, HD]), ALU.mult)\
                       .then_inc(sem("xend_made"), 1)

            def outputs(g, c):
                m, t0 = (P, c * P) if c < NC else (TS, TP)
                new = spare(("y_new", g, c)).rearrange("p (j l) -> p j l", l=P)[:, :, 0:m]
                e = e_t[:, :, 0:m]
                y = y_t[:, :, t0:t0 + m]
                eng.wait_ge(sem("y_begun"), PG * (g + 1))
                if c == 0:
                    wait_full(eng, ("y_new", g, c))
                    eng.tensor_tensor(y, y, new, ALU.add).then_inc(bank_read[use[("y_new", g, c)][0]], 1)
                else:
                    wait_after_read(eng, ("e", g, c))
                    if c < NC:
                        key = ("y_chunk_old", g, c)
                        wait_full(eng, key)
                        eng.tensor_tensor(e, e, spare(key).rearrange("p (j l) -> p j l", l=P), ALU.mult).then_inc(bank_read[use[key][0]], 1)
                        wait_after_read(eng, key)
                    else:
                        wait_after_read(eng, ("y_seq_old", g, NB - 1))
                        link(eng.tensor_tensor(e, e, y_old[:, :, :], ALU.mult))
                    wait_full(eng, ("y_new", g, c))
                    eng.tensor_tensor(e, e, new, ALU.add).then_inc(bank_read[use[("y_new", g, c)][0]], 1)
                    wait_after_read(eng, ("y_new", g, c))
                    eng.tensor_tensor(y, y, e, ALU.add).then_inc(sem("y_added"), 1)
                if c < NC:
                    key = ("state", g, c)
                    wait_full(eng, key)
                    if c == 0:
                        if g:
                            wait_full(eng, ("state_out", g - 1))
                        eng.tensor_copy(state[:, 0, :], spare(key)[:, :]).then_inc(bank_read[use[key][0]], 1)
                    else:
                        if c >= 2:
                            wait_full(eng, ("y_chunk_old", g, c - 1))
                        elif g:
                            wait_full(eng, ("state_out", g - 1))
                        wait_after_read(eng, ("state", g, c - 1))
                        s3 = [state[:, k % 2, :].rearrange("p (h d) -> p h d", h=HG) for k in (c - 1, c)]
                        link(eng.tensor_tensor(s3[1], s3[0], chunk_decay[:, c, g * HG:(g + 1) * HG].unsqueeze(2).to_broadcast([P, HG, HD]), ALU.mult))
                        eng.tensor_tensor(state[:, c % 2, :], state[:, c % 2, :], spare(key)[:, :], ALU.add).then_inc(bank_read[use[key][0]], 1)

            def sequence(g, b):
                n = g * NB + b
                key = ("y_seq_old", g, b)
                wait_full(eng, key)
                if g:
                    eng.wait_ge(sem("y_added"), NC * g)
                eng.tensor_copy(y_old[:, :, b * TD:(b + 1) * TD], spare(key)[:, 0:PG * TD].rearrange("p (j t) -> p j t", j=PG))\
                   .then_inc(bank_read[use[key][0]], 1)
                key = ("new_state", g, b)
                wait_full(eng, key)
                eng.wait_ge(sem("old_decayed"), n + 1)
                eng.tensor_tensor(old[:, b % 2], old[:, b % 2], spare(key).rearrange("p (j n) -> p j n", j=PG), ALU.add)\
                   .then_inc(bank_read[use[key][0]], 1)

            for key in group_inputs(0):
                slot(key)
            for g in range(NG):
                by_token(g)
                slots = list(ssd_slots[g])
                for c in range(5):
                    prepare(g, c)
                    for key in slots[2 * c:2 * c + 1]:
                        slot(key)
                    outputs(g, c)
                    for key in slots[2 * c + 1:2 * c + 2]:
                        slot(key)
                    if c < NC:
                        for b in (2 * c, 2 * c + 1):
                            sequence(g, b)
                eng.wait_ge(sem("y_added"), NC * (g + 1))
                wait_after_read(eng, ("y_new", g, 0))
                for j in range(PG):
                    wait_freed(eng, tile_of[("z", g, j)])
                    eng.tensor_tensor(y_t[:, j, :], y_t[:, j, :], z_s[:, j, :], ALU.mult).then_inc(sem("y_gated"), 1)
                for h in range(2):
                    wait_after_read(eng, ("y_ss", g, h))
                link(eng.reciprocal(y_rinv, y_root))
                for j in range(PG):
                    col = PAR_SSD + g * PG + j
                    eng.wait_ge(sem("y_squared"), PG * g + j + 1)
                    eng.scalar_tensor_tensor(out=y_t[:, j, :], in0=y_t[:, j, :], scalar=par[:, col:col + 1], in1=y_rinv,
                                             op0=ALU.mult, op1=ALU.mult).then_inc(sem("y_scaled"), 1)
                for j in range(PG):
                    eng.wait_ge(sem("y_hi_made"), PG * g + j + 1)
                    ins = eng.tensor_tensor(y_lo[:, j, :], y_t[:, j, :], f32(y_hi[:, j, :]), ALU.subtract)
                ins.then_inc(sem("y_split"), 1)
                for n0 in range(0, KD, 2):
                    slot(("pb", g, n0))

            eng.sem_inc(sem("merged_split"), 2)
            with eng.Fori(0, KD // 2) as i:
                for n in range(2):
                    c, t = C_GATE_B + n, T_GATE_B + n
                    one = bass.ds(2 * i + n, 1)
                    make_lo(c + 1, 2, i)
                    wait_freed(eng, t, 2, i)
                    eng.tensor_tensor(prod2[:, n:n + 1, :], gate2[:, n:n + 1, :], pb_sum[:, one, :], ALU.mult).then_inc(sem("merged_part"), 1)
                    eng.wait_ge(sem("merged_part"), n + 1 + 2 * i)
                    eng.wait_ge(sem(f"gated_back{n}"), 16 + 16 * i)
                    eng.tensor_tensor(prod2[:, n, :], prod2[:, n, :], gated_in[:, n, :], ALU.add).then_inc(sem("merged_made"), 1)
                    eng.wait_ge(sem("m_hi_made"), n + 1 + 2 * i)
                    eng.tensor_tensor(m_lo[:, one, :], prod2[:, n:n + 1, :], f32(m_hi[:, one, :]), ALU.subtract).then_inc(sem("merged_split"), 1)
            for n in range(KD):
                make_lo(C_OUT + n + 1)
                t = T_OUT + n
                wait_tile(eng, t)
                eng.tensor_copy(halves(x_res[:, n, :]), tile(t)).then_inc(tile_free[t % 2], 1)
            eng.wait_ge(sem("res_rooted"), 2)
            link(eng.reciprocal(rinv2[:, :], root2[:, :]))
            for k in range(KD):
                if k >= 2:
                    eng.wait_ge(sem("h2_split"), k - 1)
                eng.scalar_tensor_tensor(out=gate2[:, k % 2, :], in0=x_res[:, k, :], scalar=par[:, PAR_N2 + k:PAR_N2 + k + 1], in1=rinv2[:, :],
                                         op0=ALU.mult, op1=ALU.mult).then_inc(sem("h2_made"), 1)
                eng.wait_ge(sem("h2_hi_made"), k + 1)
                eng.tensor_tensor(x_lo[:, k, :], gate2[:, k % 2, :], f32(x_hi[:, k, :]), ALU.subtract).then_inc(sem("h2_split"), 1)
            eng.sem_inc(sem("f_split"), 2)
            eng.wait_ge(sem("stored_conv"), 32)
            with eng.Fori(0, KF // 2) as i:
                for n in range(2):
                    c, t = C_FFN + 2 * n, T_FFN + 2 * n
                    one = bass.ds(2 * i + n, 1)
                    make_lo(c + 1, 4, i)
                    make_lo(c + 2, 4, i)
                    wait_tile(eng, t + 1, 4, i)
                    wait_freed(eng, t, 4, i)
                    eng.wait_ge(sem("f_split"), n + 1 + 2 * i)
                    eng.tensor_tensor(halves(prod2[:, n, :]), halves(gate2[:, n, :]), tile(t + 1), ALU.mult).then_inc(tile_free[(t + 1) % 2], 1)
                    eng.wait_ge(sem("f_hi_made"), n + 1 + 2 * i)
                    eng.tensor_tensor(f_lo[:, one, :], prod2[:, n:n + 1, :], f32(f_hi[:, one, :]), ALU.subtract).then_inc(sem("f_split"), 1)

            def down_tile(n, i, last):
                for k in range(3):
                    if last and n == 1 and k == 2:
                        continue
                    make_lo(C_DOWN + 3 * n + k + 1, 6, i, tiles=DOWN_K[(k + 1) % 3][1])
                t = T_DOWN + n
                wait_tile(eng, t, 2, i)
                eng.tensor_tensor(prod2[:, n, :].rearrange("p (o h t) -> p o h t", o=1, h=2),
                                  x_res[:, bass.ds(2 * i + n, 1), :].rearrange("p o (h t) -> p o h t", h=2),
                                  tile(t).unsqueeze(1), ALU.add).then_inc(tile_free[t % 2], 1)

            with eng.Fori(0, KD // 2 - 1) as i:
                for n in range(2):
                    down_tile(n, i, False)
            for n in range(2):
                down_tile(n, KD // 2 - 1, True)


_INS = ["x_prompt", "x_sample", "cache_k", "cache_v", "page_table", "state_ssm", "state_conv",
        "norm1_w", "w_in", "q_norm_w", "k_norm_w", "sb_bias", "conv_w", "conv_b", "dt_bias", "a_log",
        "d_skip", "ssd_norm_w", "w_pa", "w_pb", "w_out", "norm2_w", "w_gate", "w_up", "w_down"]
_OUTS = [("y_prompt", (1, TP, D)), ("y_sample", (NB, TD, D)),
         ("k_prompt", (1, 1, TP, NKV, HD)), ("v_prompt", (1, 1, TP, NKV, HD)),
         ("ssm_prompt", (1, 1, NH, HD, P)), ("conv_prompt", (1, 1, CW - 1, CH)),
         ("k_sample", (1, NB, TD, NKV, HD)), ("v_sample", (1, NB, TD, NKV, HD)),
         ("ssm_sample", (1, NB, NH, HD, P)), ("conv_sample", (1, NB, CW - 1, CH))]


def kernel(**inputs):
    import numpy as np
    import concourse.bacc as bacc
    from concourse.bass_utils import run_bass_kernel_spmd

    nc = bacc.Bacc("TRN2", target_bir_lowering=False, num_devices=1)
    arrays, args = {}, []
    for name in _INS:
        a = np.ascontiguousarray(inputs[name])
        arrays[f"in_{name}"] = a
        args.append(nc.dram_tensor(f"in_{name}", a.shape, mybir.dt.from_np(a.dtype), kind="ExternalInput").ap())
    for name, shape in _OUTS:
        args.append(nc.dram_tensor(f"out_{name}", shape, F32, kind="ExternalOutput").ap())
    build(nc, *args)
    r = run_bass_kernel_spmd(nc, [arrays], core_ids=[0])
    return tuple(r.results[0][f"out_{name}"] for name, _ in _OUTS)
```

```python
from contextlib import ExitStack

import concourse.bass as bass
from concourse import mybir

F32 = mybir.dt.float32
F32R = mybir.dt.float32r
BF16 = mybir.dt.bfloat16
I32 = mybir.dt.int32
ALU = mybir.AluOpType
ACT = mybir.ActivationFunctionType

P = 128
D = 1024
KD = D // P
TP = 512
NB = 8
TD = 8
TS = NB * TD
T = TP + TS
HALF = T // 2
NC = TP // P
HD = 64
NQ = 16
NKV = 4
QG = NQ // NKV
PAGES = 8
DI = 2048
NH = 32
NG = 4
HG = NH // NG
PG = HG // 2
CH = 3072
CT = CH // P
CW = 4
FF = 2816
KF = FF // P
EPS = 1e-6
BIG = -1.0e30
K_SLOTS = 6
SEQS = NB // 2
SRC = 3 + TP + NB * (3 + TD)
CLAMP = 40.0
HALVES = [slice(0, HALF), slice(HALF, T)]

COL_Q, COL_K, COL_V = 0, D, D + 256
COL_Z = COL_V + 256
COL_X = COL_Z + DI
COL_B = COL_X + DI
COL_C = COL_B + NG * P
COL_DT = COL_C + NG * P
COL_GA = COL_DT + NH
COL_GB = COL_GA + D


def token_tiles():
    return [(c, P * c, P) for c in range(NC)] + [(NC, TP, TS)]


def attention_units():
    units = []
    for g in range(NKV):
        for i in range(NC):
            for n, j in enumerate(range(i, -1, -1)):
                units.append(dict(kind="prompt", g=g, i=i, j=j, n=n, last=j == 0))
    for h in range(2):
        units.append(dict(kind="new", h=h, n=0, last=False))
        for n, p in enumerate(range(PAGES - 1, -1, -1)):
            units.append(dict(kind="page", h=h, p=p, n=n + 1, last=p == 0))
    chain = accs = laters = page = 0
    for u, x in enumerate(units):
        accs += x["n"] >= 2
        laters += x["n"] >= 1
        x.update(u=u, chain=chain, accs=accs, laters=laters, page=page)
        page += SEQS if x["kind"] == "page" else 0
        chain += x["last"]
    return units


def build(nc, x_prompt, x_sample, cache_k, cache_v, page_table, state_ssm, state_conv, norm1_w, w_in,
          q_norm_w, k_norm_w, sb_bias, conv_w, conv_b, dt_bias, a_log, d_skip, ssd_norm_w, w_pa, w_pb,
          w_out, norm2_w, w_gate, w_up, w_down,
          y_prompt, y_sample, k_prompt, v_prompt, ssm_prompt, conv_prompt, k_sample, v_sample,
          ssm_sample, conv_sample):
    units = attention_units()
    NU = len(units)
    n_phys = cache_k.shape[1]
    STEPS = NG * 5

    N_FIRST = KD + 2 + 2 + 1
    C_GATE_A = N_FIRST
    C_SSD = C_GATE_A + 2 * KD
    C_GROUP = 10 + 4
    C_GATE_B = C_SSD + NG * C_GROUP
    C_OUT = C_GATE_B + KD
    C_FFN = C_OUT + KD
    C_DOWN = C_FFN + 2 * KF
    N_CHUNKS = C_DOWN + 3 * KD
    DOWN_K = [(0, 8), (8, 8), (16, 6)]
    T_SSD = C_SSD
    T_GROUP = 10 + KD
    T_GATE_B = T_SSD + NG * T_GROUP
    T_OUT = T_GATE_B + KD
    T_FFN = T_OUT + KD
    T_DOWN = T_FFN + 2 * KF

    with ExitStack() as ctx:
        def sb(name, shape, dt=F32, scope=ctx):
            return scope.enter_context(nc.sbuf_tensor(name, shape, dt))

        sems = {}

        def sem(name):
            if name not in sems:
                sems[name] = ctx.enter_context(nc.semaphore(name))
            return sems[name]

        G = [ctx.enter_context(nc.psum_tensor(f"tile_banks{i}", [P, 2, 512], F32)) for i in range(2)]
        W = [ctx.enter_context(nc.psum_tensor(f"spare_bank{i}", [P, 512], F32)) for i in range(4)]

        ident = sb("ident", [P, P])
        ones = sb("ones", [P, P])
        upto = sb("upto", [P, P])
        after = sb("after", [P, P])
        upto_b = sb("upto_b", [TS, TS])
        after_b = sb("after_b", [TS, TS])
        in_seq = sb("in_seq", [TS, NB])
        conv_par = sb("conv_par", [P, 5 * CT])
        par = sb("par", [P, 50])
        PAR_N1, PAR_N2, PAR_SSD, PAR_D, PAR_Q, PAR_K = 0, 8, 16, 32, 48, 49
        pages_sb = sb("pages_sb", [1, NB * PAGES], I32)
        stats = sb("stats", [P, 3, 5])
        eps_col = sb("eps_col", [P, 1])
        dt_par = sb("dt_par", [NH, 3])
        dt_tok = sb("dt_tok", [P, 5, 2 * NH])
        conv_in = sb("conv_in", [P, CT, 24])
        conv_out = sb("conv_out", [P, CT, 27])

        w_raw = sb("w_raw", [P, 2, KD, P])
        w_hi = sb("w_hi", [P, 2, KD, P], F32R)
        w_lo = sb("w_lo", [P, 2, KD, P], F32R)
        raw_in = [sem("weights_in0"), sem("weights_in1")]
        hi_made = sem("weights_hi_made")
        split = sem("weights_split")
        tile_done = sem("tile_done")
        part_done = sem("down_part_done")
        tile_free = [sem("tile_free0"), sem("tile_free1")]

        x_hi = sb("x_hi", [P, KD, T], F32R)
        x_lo = sb("x_lo", [P, KD, T], F32R)

        early = ExitStack()
        o_hi = sb("o_hi", [P, KD, T], F32R, early)
        o_lo = sb("o_lo", [P, KD, T], F32R, early)
        attn = ExitStack()
        neg_suffix = sb("neg_suffix", [P, P], F32, attn)
        neg_ones = sb("neg_ones", [P, P], F32R, attn)
        pair_ones = conv_out[:, :, :].rearrange("p c k -> p (c k)")[:, 0:P]
        big_diag = sb("big_diag", [P, P], BF16, attn)
        bad_prompt = sb("bad_prompt", [P, QG, P], BF16, attn)
        bad_new = sb("bad_new", [TS, 2, SEQS, 16, TD], BF16, attn)
        bias_row = sb("bias_row", [HD + 1, NQ], F32, attn)
        bias_cols = sb("bias_cols", [HD + 1, 2, NQ, TD], F32R, attn)
        ones_row = sb("ones_row", [HD + 1, P], F32R, attn)
        q_pair = sb("q_pair", [P, NB, 2, 2, QG * TD], F32, attn)
        q_t = sb("q_t", [HD + 1, NQ, T], F32, attn)
        k_t = sb("k_t", [HD + 1, NKV, T], F32, attn)
        v_tok = sb("v_tok", [P, 5, NKV * HD], F32, attn)
        k_page = sb("k_page", [P, K_SLOTS, NKV * HD], F32, attn)
        first = ExitStack()
        x_tok = sb("x_tok", [P, 5, D], F32, first)
        par_rows = sb("par_rows", [5 * CT, P], F32, first)
        par2_rows = sb("par2_rows", [50, P], F32, first)
        d_rows = sb("d_rows", [48, 2], F32, first)
        sc_rows = sb("sc_rows", [24, CH], F32, first)
        first.close()
        qkv = ExitStack()
        pre = sb("pre", [P, 2, T], F32, qkv)
        sq = sb("sq", [P, 2, T], F32, qkv)
        root = sb("root", [P, T], F32, qkv)
        rinv = sb("rinv", [P, T], F32, qkv)
        v_t = sb("v_t", [P, 2, T], F32, qkv)
        dt_t = sb("dt_t", [2 * NH, T], F32, qkv)
        dt_w = sb("dt_w", [NH, 2, T], F32, qkv)
        k_out = sb("k_out", [P, 5, NKV * HD], F32, qkv)
        qkv.close()
        v_page = sb("v_page", [P, 8, NKV * HD], F32, attn)
        zs = sb("zs", [P, 2, 512], F32, attn)
        sp = sb("sp", [P, 4, 512], F32, attn)
        acc = sb("acc", [P, 512], F32, attn)
        later_hi = sb("later_hi", [P, 2, 512], F32R, attn)
        later_lo = sb("later_lo", [P, 512], F32R, attn)
        wts = sb("wts", [P, 2, 512], F32, attn)
        kt_page = sb("kt_page", [P, SEQS, 2, P], F32, attn)
        attn.close()
        gate = sb("gate", [P, 2, T], F32, early)
        gated = sb("gated", [P, 2, T], F32, early)
        early.close()
        ssd = ExitStack()
        pb_sum = sb("pb_sum", [P, KD, T], F32, ssd)
        y_hi = sb("y_hi", [P, PG, T], F32R, ssd)
        y_lo = sb("y_lo", [P, PG, T], F32R, ssd)
        conv_src = sb("conv_src", [P, 2, SRC], F32, ssd)
        conv_acc = sb("conv_acc", [P, 2, SRC], F32, ssd)
        bc_t = sb("bc_t", [P, 2, 2, T], F32, ssd)
        xs_t = sb("xs_t", [P, PG, T], F32, ssd)
        y_t = sb("y_t", [P, PG, T], F32, ssd)
        z_s = sb("z_s", [P, PG, T], F32, ssd)
        xdt = sb("xdt", [P, 5, HG, HD], F32, ssd)
        xend = sb("xend", [P, 2, HG, HD], F32, ssd)
        b_tok = sb("b_tok", [P, 5, P], F32, ssd)
        cb_m = sb("cb_m", [P, 5, P], F32, ssd)
        a_upto_hi = sb("a_upto_hi", [P, HG, P], F32R, ssd)
        a_upto_lo = sb("a_upto_lo", [P, HG, P], F32R, ssd)
        a_hi = sb("a_hi", [P, 5, NH], F32R, ssd)
        a_lo = sb("a_lo", [P, 5, NH], F32R, ssd)
        after_r = sb("after_r", [P, P], F32R, ssd)
        after_b_r = sb("after_b_r", [TS, TS], F32R, ssd)
        one_half = sb("one_half", [P, 2, P], F32R, ssd)
        decay = sb("decay", [P, HG, P], F32, ssd)
        e_t = sb("e_t", [P, PG, P], F32, ssd)
        state = sb("state", [P, 2, HG * HD], F32, ssd)
        old = sb("old", [P, 2, PG, P], F32, ssd)
        old_t = sb("old_t", [P, 2, PG, P], F32, ssd)
        b_seq = sb("b_seq", [TS, NB, P], F32, ssd)
        xend_s = sb("xend_s", [TS, HG, HD], F32, ssd)
        y_old = sb("y_old", [P, PG, TS], F32, ssd)
        end_decay = sb("end_decay", [P, 5, NH], F32, ssd)
        chunk_decay = sb("chunk_decay", [P, NC, NH], F32, ssd)
        seq_decay = sb("seq_decay", [P, NH // 2, NB], F32, ssd)
        a_seq = e_t[0:TS].rearrange("p j l -> p (j l)")[:, 0:NH * NB].rearrange("p (h b) -> p h b", b=NB)
        state_out = e_t
        conv_rows = [xdt[0:27, j].rearrange("p h d -> p (h d)") for j in range(5)] + [xend[0:27, 0].rearrange("p h d -> p (h d)")]
        y_root = old_t.rearrange("p s j n -> p (s j n)")[:, 0:T]
        y_rinv = decay[:, 0:5, :].rearrange("p h l -> p (h l)")[:, 0:T]
        ssd.close()
        tail = ExitStack()
        x_res = sb("x_res", [P, KD, T], F32, tail)
        mid = ExitStack()
        m_hi = sb("m_hi", [P, KD, T], F32R, mid)
        m_lo = sb("m_lo", [P, KD, T], F32R, mid)
        x_again = sb("x_again", [P, 5, D], F32, mid)
        gated_in = sb("gated_in", [P, 2, T], F32, mid)
        mid.close()
        f_hi = sb("f_hi", [P, KF, T], F32R, tail)
        f_lo = sb("f_lo", [P, KF, T], F32R, tail)
        gate2 = sb("gate2", [P, 2, T], F32, tail)
        prod2 = sb("prod2", [P, 2, T], F32, tail)
        root2 = sb("root2", [P, T], F32, tail)
        rinv2 = sb("rinv2", [P, T], F32, tail)
        y_tok = sb("y_tok", [P, 5, P], F32, tail)
        tail.close()
        gated_dram = nc.dram_tensor("gated_dram", (KD, P, T), F32, kind="Internal").ap()

        keys = [("par", 0), ("par", 1), ("conv_in", 0), ("conv_in", 1)]
        keys += [("x", k, j) for k in range(KD) for j in range(2)]
        keys += [(w, n, j) for n in range(KD + 2) for w, j in (("ss", 0), ("ss", 1))]
        keys += [("v", n, c) for n in range(2) for c in range(5)] + [("k", c) for c in range(5)]
        keys += [("dt", 0)]
        FIRST_USES = len(keys)
        keys += [("decays", 0)]
        for g in range(NG):
            keys += [("x_tok", g, c) for c in range(5)] + [("b_tok", g), ("cb", g), ("sample_bc", g)]
            for c in range(5):
                keys += [("seg", g, c, 0), ("seg", g, c, 1)]
                keys += [("e", g, c)] if c else []
                keys += [("y_chunk_old", g, c)] if 0 < c < NC else []
                keys += [("state", g, c)] if c < NC else []
                keys += [("y_new", g, c)]
                if c < NC:
                    keys += [("old_t", g, b) for b in (2 * c, 2 * c + 1)]
                    keys += [(what, g, b) for b in (2 * c, 2 * c + 1) for what in ("y_seq_old", "new_state")]
            keys += [("state_out", g), ("y_ss", g, 0), ("y_ss", g, 1)]
            keys += [("conv_out", j) for j in range(6)] if g == NG - 1 else []
        use = {key: (n % 4, n // 4) for n, key in enumerate(keys)}
        N_USES = len(keys)
        bank_full = [sem(f"bank_full{i}") for i in range(4)]
        bank_read = [sem(f"bank_read{i}") for i in range(4)]

        def spare(key):
            return W[use[key][0]]

        def wait_full(eng, key):
            i, n = use[key]
            eng.wait_ge(bank_full[i], n + 1)

        def wait_read(eng, key):
            i, n = use[key]
            if n:
                eng.wait_ge(bank_read[i], n)

        block = ctx.enter_context(nc.Block())

        def half(base, step=0, i=0):
            return base // 2 + (step // 2) * i

        def f32(ap):
            return ap.bitcast(F32)

        def load_chunk(eng, src, c, step=0, i=0, width=P, tiles=KD, dst=None):
            if step or c >= 2:
                eng.wait_ge(split, c - 1 + step * i)
            dst = w_raw[:, c % 2, 0:tiles, 0:width] if dst is None else dst
            eng.dma_start(dst, src).then_inc(raw_in[c % 2], 16)

        def make_hi(c, step=0, i=0, width=P, tiles=KD, after_tiles=None, after_part=None):
            nc.scalar.wait_ge(raw_in[c % 2], 16 * (half(c, step, i) + 1))
            if after_tiles is not None:
                nc.scalar.wait_ge(tile_done, after_tiles)
            if after_part is not None:
                nc.scalar.wait_ge(part_done, after_part)
            nc.scalar.activation(w_hi[:, c % 2, 0:tiles, 0:width], w_raw[:, c % 2, 0:tiles, 0:width],
                                 ACT.Copy).then_inc(hi_made, 1)

        def make_lo(c, step=0, i=0, width=P, tiles=KD):
            nc.vector.wait_ge(hi_made, c + 1 + step * i)
            nc.vector.tensor_tensor(w_lo[:, c % 2, 0:tiles, 0:width], w_raw[:, c % 2, 0:tiles, 0:width],
                                    f32(w_hi[:, c % 2, 0:tiles, 0:width]), ALU.subtract).then_inc(split, 1)

        def wait_tile(eng, t, step=0, i=0):
            eng.wait_ge(tile_done, t + 1 + step * i)

        def wait_freed(eng, t, step=0, i=0):
            eng.wait_ge(tile_free[t % 2], half(t, step, i) + 2)

        def tile(t, rows=P):
            return G[t % 2][0:rows, :, 0:HALF]

        def halves(ap):
            return ap.rearrange("p (h t) -> p h t", h=2)

        def product(pe, t, w, x, start=True, stop=True, rows=P, step=0, i=0, onto=False):
            if start:
                pe.wait_ge(tile_free[t % 2], half(t, step, i) + 1)
            last = len(w) - 1
            for k, ((wh, wl), (xh, xl)) in enumerate(zip(w, x)):
                for h in range(2):
                    out = G[t % 2][0:rows, h, 0:HALF]
                    nc.tensor.matmul(out, wh, xh[:, HALVES[h]], start=start and k == 0, stop=False, skip_group_check=onto)
                    nc.tensor.matmul(out, wh, xl[:, HALVES[h]], start=False, stop=False, skip_group_check=onto)
                for h in range(2):
                    out = G[t % 2][0:rows, h, 0:HALF]
                    mm = nc.tensor.matmul(out, wl, xh[:, HALVES[h]], start=False, stop=stop and k == last, skip_group_check=onto)
            return mm

        def chunk_tile(pe, c, t, xh, xl, step=0, i=0, width=P):
            pe.wait_ge(split, c + 1 + step * i)
            w = [(w_hi[:, c % 2, k, 0:width], w_lo[:, c % 2, k, 0:width]) for k in range(KD)]
            x = [(xh[:, k, :], xl[:, k, :]) for k in range(KD)]
            mm = product(pe, t, w, x, rows=width, step=step, i=i)
            mm.then_inc(tile_done, 1)
            return mm

        def group_inputs(g):
            return [("bc", g, 0), ("bc", g, 1)] + [("x", g, j) for j in range(PG)]

        def ssd_plan(g):
            z = [("z", g, j) for j in range(PG)]
            pb = [("pb", g - 1, n) for n in range(0, KD, 2)]
            into = group_inputs(g + 1)
            if g == 0:
                return [([z[1]], [into[0]]), ([z[2]], [into[1]]), ([z[3]], [into[2]]), ([], [into[3]]), ([into[4]], [into[5]]),
                        ([("z", 1, 0)], [("z", 1, 1)])]
            if g < NG - 1:
                return [([z[2]], [into[0]]), ([z[3]], [pb[0]]), ([into[1]], [pb[1]]), ([into[2]], [pb[2]]), ([into[3], into[4]], [into[5]]),
                        ([pb[3]], [("z", g + 1, 0), ("z", g + 1, 1)])]
            return [([z[2]], []), ([z[3]], [pb[0]]), ([], [pb[1]]), ([], [pb[2]]), ([], []), ([pb[3]], [])]

        last_pb = [("pb", NG - 1, n) for n in range(0, KD, 2)]
        before_groups = group_inputs(0) + [("z", 0, 0)]
        ssd_chunks = before_groups + [key for g in range(NG) for pair in ssd_plan(g) for keys_ in pair for key in keys_] + last_pb
        chunk_of = {key: C_SSD + n for n, key in enumerate(ssd_chunks)}
        tile_of, n_t = {}, T_SSD
        for key in ssd_chunks:
            tile_of[key] = n_t
            n_t += 2 if key[0] == "pb" else 1
        assert n_t == T_GATE_B and len(ssd_chunks) == NG * C_GROUP

        def ssd_col(key):
            what, g, j = key
            if what == "bc":
                return (COL_B, COL_C)[j] + g * P
            return (COL_X if what == "x" else COL_Z) + (g * PG + j) * P

        def src_tile(key):
            what, g, j = key
            return DI // P + NG * j + g if what == "bc" else g * PG + j

        conv_keys = [k for k in ssd_chunks if k[0] in ("bc", "x")]
        conv_n = {key: n for n, key in enumerate(conv_keys)}

        def score_bank(u):
            return G[u % 4 // 2][:, u % 2, :]

        def wait_after_read(eng, key):
            i, n = use[key]
            eng.wait_ge(bank_read[i], n + 1)

        page_unit = {x["page"] + b: x["u"] for x in units if x["kind"] == "page" for b in range(SEQS)}

        def decode_block(ap_rows, t0):
            return ap_rows[:, t0:t0 + TS].rearrange("p (b t) -> p b t", b=NB)

        def conv_dst(key):
            what, g, j = key
            return bc_t[:, g % 2, j, :] if what == "bc" else xs_t[:, j, :]

        def tiles_after(c):
            if c < C_SSD:
                return c + 1
            if c < C_GATE_B:
                key = ssd_chunks[c - C_SSD]
                return tile_of[key] + (2 if key[0] == "pb" else 1)
            return c + 1 + T_GATE_B - C_GATE_B

        def chain_views(x):
            out, views = W[x["chain"] % 2], []
            if x["kind"] == "prompt":
                at = (slice(x["g"] * 2, x["g"] * 2 + 2), slice(x["i"] * P, (x["i"] + 1) * P))
                for e in range(2):
                    src = out[0:HD, :].rearrange("p (h q) -> p h q", h=QG)[:, e::2, :]
                    rows = slice(e * HD, (e + 1) * HD)
                    views.append((src, o_hi[rows, at[0], at[1]], o_lo[rows, at[0], at[1]]))
                return views
            t0 = TP + x["h"] * SEQS * TD
            for g in range(NKV):
                here = slice(g % 2 * HD, (g % 2 + 1) * HD)
                for e in range(2):
                    src = out[here, :].rearrange("p (b x t) -> p b x t", b=SEQS, t=TD)[:, :, QG * g + e:QG * (g + 1):2, :]
                    rows = slice(e * HD, (e + 1) * HD)
                    views.append((src, *(o[rows, 2 * g:2 * g + 2, t0:t0 + SEQS * TD].rearrange("p k (b t) -> p b k t", b=SEQS)
                                         for o in (o_hi, o_lo))))
            return views

        def views_before(chain, plus=0):
            return sum(len(chain_views(y)) for y in units if y["last"] and y["chain"] < chain + plus)

        def wait_chain(eng, x):
            eng.wait_ge(sem("pv_done"), x["u"] + 1)

        def read_turned(eng, copy, x, half):
            n = x["page"] // SEQS
            eng.wait_ge(sem("k_turned"), 2 * n + half + 1)
            if n:
                eng.wait_ge(sem("logits_done"), page_unit[x["page"] - 1] + 1)
            copy(kt_page[:, 2 * half:2 * half + 2, :, :].rearrange("p b g k -> p (b g k)"), W[2 + half][:, :], ACT.Copy).then_inc(sem(f"kt_made{half}"), 1)

        laters_at = {x["laters"]: x["u"] for x in units if x["n"]}

        def later_sum(x):
            return sp[:, (x["u"] - 1) % 4, :] if x["n"] == 1 else acc[:, :]

        def page_of(eng, x, b):
            at = (x["h"] * SEQS + b) * PAGES + x["p"]
            return eng.value_load(pages_sb[0:1, at:at + 1], min_val=0, max_val=n_phys - 1)

        def load_values(eng, x, b):
            n = x["page"] + b
            if n >= 8:
                eng.wait_ge(sem("pv_done"), page_unit[n - 8] + 1)
            else:
                eng.wait_ge(sem("stored_k"), 32)
            eng.dma_start(v_page[:, n % 8, :], cache_v[0, bass.ds(page_of(eng, x, b), 1)].rearrange("o p h d -> p (o h d)")).then_inc(sem(f"v_page_in{n % 8}"), 16)

        sem_const_first, sem_const_all = [], []

        @block.sync
        def _(sp_eng):
            eng = sp_eng
            for c in range(NC):
                eng.dma_start(x_tok[:, c, :], x_prompt[0, c * P:(c + 1) * P, :]).then_inc(sem(f"x_in{c}"), 16)
            eng.dma_start(x_tok[0:TS, NC, :], x_sample.rearrange("b t n -> (b t) n")).then_inc(sem(f"x_in{NC}"), 16)

            def first_src(c):
                if c < N_FIRST - 1:
                    return w_in[0, :, c * P:(c + 1) * P].rearrange("(t p) n -> p t n", p=P)
                return w_in[0, :, COL_DT:COL_DT + NH].rearrange("(t p) n -> p t n", p=P)

            for c in range(N_FIRST):
                load_chunk(eng, first_src(c), c, width=P if c < N_FIRST - 1 else NH)
            def col_tile(w, k):
                return w.rearrange("p t (m n) -> p t m n", n=P)[:, :, bass.ds(k, 1), :].rearrange("p t o n -> p t (o n)")

            cols = [w_in[0, :, COL_GA:COL_GA + D].rearrange("(t p) n -> p t n", p=P),
                    w_pa[0].rearrange("(t p) n -> p t n", p=P)]
            for k in range(2):
                load_chunk(eng, cols[k][:, :, 0:P], C_GATE_A + k)
            eng.dma_start(pages_sb[:, :], page_table.rearrange("b p -> (b p)").rearrange("(o n) -> o n", o=1)).then_inc(sem("pages_in"), 16)
            eng.wait_ge(sem("pages_in"), 16)

            page_units = [x for x in units if x["kind"] == "page"]
            for k in range(len(page_units) + 3):
                for b in range(SEQS if k < len(page_units) else 0):
                    x = page_units[k]
                    n = x["page"] + b
                    if n >= K_SLOTS:
                        eng.wait_ge(sem("k_turned"), (n - K_SLOTS) // 2 + 1)
                    eng.dma_start(k_page[:, n % K_SLOTS, :], cache_k[0, bass.ds(page_of(eng, x, b), 1)].rearrange("o p h d -> p (o h d)")).then_inc(sem(f"k_page_in{n % K_SLOTS}"), 16)
                if k >= 3:
                    load_values(eng, page_units[k - 3], SEQS - 1)

            def load_in_turn(sources, c, n):
                again = eng.alloc_register(f"column_tile{c}")
                with eng.Fori(1, n) as i:
                    load_chunk(eng, col_tile(sources[0], i), c, 2, i)
                    eng.reg_mov(again, i)
                    load_chunk(eng, col_tile(sources[1], eng.snap(again)), c + 1, 2, i)

            load_in_turn(cols, C_GATE_A, KD)
            for key in ssd_chunks:
                c = chunk_of[key]
                if key[0] == "pb":
                    _, g, n0 = key
                    src = w_pb[0, g * PG * P:(g + 1) * PG * P, n0 * P:(n0 + 2) * P].rearrange("(t p) n -> p t n", p=P)
                    dst = w_raw[:, c % 2].rearrange("p t n -> p (t n)").rearrange("p (t n) -> p t n", t=PG)
                    load_chunk(eng, src, c, dst=dst)
                else:
                    n0 = ssd_col(key)
                    load_chunk(eng, w_in[0, :, n0:n0 + P].rearrange("(t p) n -> p t n", p=P), c)
            gate_b = w_in[0, :, COL_GB:COL_GB + D].rearrange("(t p) n -> p t n", p=P)
            out_w = w_out[0].rearrange("(t p) n -> p t n", p=P)
            for base, w in ((C_GATE_B, gate_b), (C_OUT, out_w)):
                with eng.Fori(0, KD // 2) as i:
                    for k in range(2):
                        load_chunk(eng, w[:, :, bass.ds(2 * P * i + k * P, P)], base + k, 2, i)
            up = [w_gate[0].rearrange("(t p) n -> p t n", p=P), w_up[0].rearrange("(t p) n -> p t n", p=P)]
            for k in range(2):
                load_chunk(eng, up[k][:, :, 0:P], C_FFN + k)
            load_in_turn(up, C_FFN, KF)
            down = w_down[0].rearrange("(t p) n -> p t n", p=P)
            with eng.Fori(0, KD // 2) as i:
                for n in range(2):
                    for k, (k0, kn) in enumerate(DOWN_K):
                        load_chunk(eng, down[:, k0:k0 + kn, bass.ds(2 * P * i + n * P, P)], C_DOWN + 3 * n + k, 6, i, tiles=kn)

        @block.gpsimd
        def _(pool):
            eng = pool
            made = sem("constants")
            n_made = [0]

            def put(make, *args, **kwargs):
                if n_made[0]:
                    eng.wait_ge(made, n_made[0])
                n_made[0] += 1
                make(*args, **kwargs).then_inc(made, 1)

            def select(ap, op, base, pattern, cm, fill):
                put(eng.affine_select, out=ap, in_=ap, compare_op=op, fill=fill, base=base, pattern=pattern, channel_multiplier=cm)

            def rule(ap, value, conditions, fill):
                put(eng.memset, ap, value)
                for op, base, pattern, cm in conditions:
                    select(ap, op, base, pattern, cm, fill)

            ge, gt = ALU.is_ge, ALU.is_gt
            rule(ident[:, :], 0.0, [(ALU.not_equal, 0, [[-1, P]], 1)], 1.0)
            put(eng.memset, ones[:, :], 1.0)
            put(eng.memset, eps_col[:, :], EPS)
            put(eng.memset, stats[:, :, :], 1.0)
            rule(pair_ones[:, :], 1.0, [(ge, 0, [[-HD, 2], [0, HD]], 1), (ge, HD - 1, [[HD, 2], [0, HD]], -1)], 0.0)
            put(eng.memset, k_t[HD:HD + 1, :, :], 1.0)
            FIRST_CONST = n_made[0]
            sem_const_first.append(FIRST_CONST)
            eng.dma_start(bias_row[HD:HD + 1, :], sb_bias).then_inc(sem("bias_in"), 16)
            eng.wait_ge(sem("bias_in"), 16)
            put(eng.tensor_copy, q_t[HD:HD + 1, :, :], bias_row[HD:HD + 1, :].unsqueeze(2).to_broadcast([1, NQ, T]))
            rule(upto[:, :], 1.0, [(ge, 0, [[1, P]], -1)], 0.0)
            rule(after[:, :], 1.0, [(gt, 0, [[-1, P]], 1)], 0.0)
            rule(neg_suffix[:, :], -1.0, [(ge, 0, [[-1, P]], 1)], 0.0)
            put(eng.tensor_scalar, neg_ones[:, :], upto[:, :], 0.0, -1.0, ALU.mult, ALU.add)
            put(eng.memset, q_pair[:, :, :, :, :], 0.0)
            rule(big_diag[:, :], 0.0, [(ALU.not_equal, 0, [[-1, P]], 1)], BIG)
            rule(bad_prompt[:, :, :], 0.0, [(gt, 0, [[0, QG], [1, P]], -1)], 1.0)
            for h in range(2):
                first_token = h * SEQS * TD
                rule(bad_new[:, h], 0.0,
                     [(ge, -first_token, [[-TD, SEQS], [0, 16], [0, TD]], 1),
                      (gt, first_token, [[TD, SEQS], [0, 16], [1, TD]], -1)], 1.0)
            rule(upto_b[:, :], 1.0, [(ge, 0, [[-TD, NB], [0, TD]], 1), (ge, 0, [[TD, NB], [1, TD]], -1)], 0.0)
            rule(after_b[:, :], 1.0, [(gt, 0, [[-TD, NB], [-1, TD]], 1), (ge, TD - 1, [[TD, NB], [0, TD]], -1)], 0.0)
            rule(in_seq[:, :], 1.0, [(ge, 0, [[-TD, NB]], 1), (ge, TD - 1, [[TD, NB]], -1)], 0.0)
            sem_const_all.append(n_made[0])

            for n in range(2):
                for c in range(5):
                    wait_after_read(eng, ("v", n, c))
            eng.dma_start(v_prompt[0, 0].rearrange("(c p) h d -> p c (h d)", p=P), v_tok[:, 0:NC, :]).then_inc(sem("stored_v"), 16)
            eng.dma_start(v_sample[0].rearrange("b t h d -> (b t) (h d)"), v_tok[0:TS, NC, :]).then_inc(sem("stored_v"), 16)
            for c in range(5):
                wait_after_read(eng, ("k", c))
            eng.dma_start(k_prompt[0, 0].rearrange("(c p) h d -> p c (h d)", p=P), k_out[:, 0:NC, :]).then_inc(sem("stored_k"), 16)
            eng.dma_start(k_sample[0].rearrange("b t h d -> (b t) (h d)"), k_out[0:TS, NC, :]).then_inc(sem("stored_k"), 16)
            eng.wait_ge(sem("stored_k"), 32)
            eng.wait_ge(sem("pages_in"), 16)

            def split_later_lo(x):
                eng.wait_ge(sem("later_hi_made"), x["laters"])
                if x["laters"] > 1:
                    eng.wait_ge(sem("sums_done"), laters_at[x["laters"] - 1] + 1)
                eng.tensor_tensor(later_lo[:, :], later_sum(x), f32(later_hi[:, x["u"] % 2, :]), ALU.subtract).then_inc(sem("later_lo_made"), 1)

            for x in units:
                u = x["u"]
                if u and units[u - 1]["n"]:
                    split_later_lo(units[u - 1])
                if x["n"] >= 2:
                    eng.wait_ge(sem("sp_made"), u)
                    if x["accs"] > 1:
                        eng.wait_ge(sem("acc_made"), x["accs"] - 1)
                    eng.wait_ge(sem("later_lo_made"), x["laters"] - 1)
                    prev = sp[:, (u - 2) % 4, :] if x["n"] == 2 else acc[:, :]
                    eng.tensor_tensor(acc[:, :], prev, sp[:, (u - 1) % 4, :], ALU.add).then_inc(sem("acc_made"), 1)
                if u and units[u - 1]["kind"] == "page":
                    for b in range(SEQS - 1):
                        load_values(eng, units[u - 1], b)

            split_later_lo(units[-1])
            for b in range(SEQS - 1):
                load_values(eng, units[-1], b)

            with eng.Fori(0, KD // 2) as i:
                for k in range(2):
                    wait_freed(eng, C_GATE_A + 2 * k + 1, 4, i)
                    eng.dma_start(gated_dram[bass.ds(2 * i + k, 1)].rearrange("o p t -> p (o t)"), gated[:, k, :]).then_inc(sem(f"gated_out{k}"), 16)

            eng.wait_ge(sem("gated_out0"), 16 * (KD // 2))
            eng.wait_ge(sem("gated_out1"), 16 * (KD // 2))
            for j in range(2):
                eng.memset(conv_src[:, j, 0:3], 0.0).then_inc(sem("conv_zeros"), 1)
                eng.wait_ge(sem("conv_zeros"), j + 1)

            def conv_io(key):
                n, ct = conv_n[key], src_tile(key)
                seqs = conv_src[:, n % 2, 3 + TP:SRC].rearrange("p (b t) -> p b t", b=NB)
                if n >= 2:
                    eng.wait_ge(sem("conv_made"), n - 1)
                eng.tensor_copy(seqs[:, :, 0:3], conv_in[:, ct, :].rearrange("p (b t) -> p b t", b=NB)).then_inc(sem("conv_heads"), 1)
                eng.wait_ge(sem("conv_heads"), n + 1)
                wait_freed(eng, tile_of[key])
                eng.tensor_copy(conv_out[:, ct, 0:3], conv_src[:, n % 2, TP:TP + 3]).then_inc(sem("conv_tail_made"), 1)
                eng.wait_ge(sem("conv_tail_made"), n + 1)
                eng.tensor_copy(conv_out[:, ct, 3:27].rearrange("p (b t) -> p b t", b=NB), seqs[:, :, TD:TD + 3]).then_inc(sem("conv_tails"), 1)
                eng.wait_ge(sem("conv_tails"), n + 1)

            def old_states_in(g, b):
                n = g * NB + b
                if n >= 2:
                    eng.wait_ge(sem(f"state_stored{b % 2}"), 16 * (n // 2))
                eng.dma_start(old[:, b % 2], state_ssm[0, b, g * HG:(g + 1) * HG].rearrange("(j e) p n -> (e p) j n", e=2)).then_inc(sem(f"state_in{b % 2}"), 16)

            eng.tensor_tensor(a_seq[:, :, :], in_seq[:, :].unsqueeze(1).to_broadcast([TS, NH, NB]),
                              dt_tok[0:TS, NC, NH:2 * NH].unsqueeze(2).to_broadcast([TS, NH, NB]), ALU.mult).then_inc(sem("a_seq_made"), 1)
            eng.wait_ge(sem("a_seq_made"), 1)
            def decay_steps(st):
                g, c = st // 5, st % 5
                m, mask = (P, upto) if c < NC else (TS, upto_b)
                if st:
                    wait_full(eng, ("e" if (st - 1) % 5 else "seg", (st - 1) // 5, (st - 1) % 5, *(() if (st - 1) % 5 else (1,))))
                for part, (src, dst) in enumerate(((a_hi, a_upto_hi), (a_lo, a_upto_lo))):
                    eng.tensor_tensor(dst[0:m, :, 0:m], mask[0:m, 0:m].unsqueeze(1).to_broadcast([m, HG, m]),
                                      f32(src[0:m, c, g * HG:(g + 1) * HG]).unsqueeze(2).to_broadcast([m, HG, m]),
                                      ALU.mult).then_inc(sem("a_upto_made"), 1)
                    eng.wait_ge(sem("a_upto_made"), 2 * st + part + 1)

            eng.wait_ge(sem("a_split"), 2)
            decay_steps(0)
            for key in group_inputs(0):
                conv_io(key)
            for g in range(NG):
                eng.wait_ge(sem("b_tok_made"), g + 1)
                if g:
                    wait_full(eng, ("new_state", g - 1, NB - 1))
                eng.tensor_tensor(b_seq[:, :, :], b_tok[0:TS, NC, :].unsqueeze(1).to_broadcast([TS, NB, P]),
                                  in_seq[:, :].unsqueeze(2).to_broadcast([TS, NB, P]), ALU.mult).then_inc(sem("b_seq_made"), 1)
                eng.wait_ge(sem("b_seq_made"), g + 1)
                plan = ssd_plan(g)
                for c in range(5):
                    before, later = plan[c]
                    if c < NC:
                        for b in (2 * c, 2 * c + 1):
                            old_states_in(g, b)
                    if g * 5 + c + 1 < STEPS:
                        decay_steps(g * 5 + c + 1)
                    for key in before:
                        if key[0] in ("bc", "x"):
                            conv_io(key)
                    if c < NC:
                        for b in (2 * c, 2 * c + 1):
                            wait_full(eng, ("old_t", g, b))
                            eng.tensor_tensor(old[:, b % 2], old[:, b % 2],
                                              seq_decay[:, g * PG:(g + 1) * PG, b:b + 1].to_broadcast([P, PG, P]), ALU.mult)\
                               .then_inc(sem("old_decayed"), 1)
                            eng.wait_ge(sem("old_decayed"), g * NB + b + 1)
                    for key in later:
                        if key[0] in ("bc", "x"):
                            conv_io(key)
                    if c < NC:
                        for b in (2 * c, 2 * c + 1):
                            wait_after_read(eng, ("new_state", g, b))
                            eng.dma_start(ssm_sample[0, b, g * HG:(g + 1) * HG].rearrange("(j e) p n -> (e p) j n", e=2), old[:, b % 2]).then_inc(sem(f"state_stored{b % 2}"), 16)
                wait_after_read(eng, ("state_out", g))
                eng.dma_start(ssm_prompt[0, 0, g * HG:(g + 1) * HG].rearrange("(j e) p n -> (e p) j n", e=2), state_out[:, :, :]).then_inc(sem("stored_prompt_state"), 16)
            for j in range(6):
                wait_after_read(eng, ("conv_out", j))
            rows = xdt[0:27].rearrange("p c h d -> p (c h d)")
            for dst, at in ((conv_prompt[0, 0], slice(0, 3)), (conv_sample[0].rearrange("b t n -> (b t) n"), slice(3, 27))):
                eng.dma_start(dst[:, 0:5 * 512], rows[at, :]).then_inc(sem("stored_conv"), 16)
                eng.dma_start(dst[:, 5 * 512:], conv_rows[5][at, :]).then_inc(sem("stored_conv"), 16)
            for n in range(2):
                eng.wait_ge(sem(f"state_stored{n}"), 16 * NG * NB // 2)
            eng.wait_ge(sem("stored_prompt_state"), 16 * NG)
            eng.wait_ge(sem("stored_conv"), 64)
            eng.wait_ge(sem("y_split"), NG)
            eng.wait_ge(tile_done, T_GATE_B)
            eng.dma_start(x_again[:, 0:NC, :], x_prompt[0].rearrange("(c p) n -> p c n", p=P)).then_inc(sem("x_again_in"), 16)
            eng.dma_start(x_again[0:TS, NC, :], x_sample.rearrange("b t n -> (b t) n")).then_inc(sem("x_again_in"), 16)
            with eng.Fori(0, KD // 2) as i:
                for k in range(2):
                    eng.wait_ge(sem("merged_split"), k + 1 + 2 * i)
                    eng.dma_start(gated_in[:, k, :], gated_dram[bass.ds(2 * i + k, 1)].rearrange("o p t -> p (o t)")).then_inc(sem(f"gated_back{k}"), 16)
            eng.wait_ge(sem("stored_v"), 32)
            with eng.Fori(0, KD) as i:
                eng.wait_ge(sem("y_tok_made"), i + 2)
                eng.dma_start(y_prompt[0].rearrange("(c p) n -> p c n", p=P)[:, :, bass.ds(P * i, P)], y_tok[:, 0:NC, :]).then_inc(sem("y_out"), 16)
                eng.dma_start(y_sample.rearrange("b t n -> (b t) n")[:, bass.ds(P * i, P)], y_tok[0:TS, NC, :]).then_inc(sem("y_out_s"), 16)
            eng.wait_ge(sem("y_out"), 16 * KD)
            eng.wait_ge(sem("y_out_s"), 16 * KD)

        @block.tensor
        def _(pe):
            for k in range(2):
                pe.sem_inc(tile_free[k], 1)
            pe.wait_ge(sem("constants"), sem_const_first[0])
            pe.wait_ge(sem("par_in"), 16 * 9)
            pe.transpose(spare(("par", 0))[:, 0:5 * CT], par_rows[:, :], ident[0:5 * CT, 0:5 * CT]).then_inc(bank_full[use[("par", 0)][0]], 1)
            pe.wait_ge(sem("d_spread"), 1)
            pe.transpose(spare(("par", 1))[:, 0:50], par2_rows[:, :], ident[0:50, 0:50]).then_inc(bank_full[use[("par", 1)][0]], 1)
            pe.wait_ge(sem("conv_state_in"), 16)
            for j in range(2):
                for n in range(12):
                    ct = 12 * j + n
                    mm = pe.transpose(spare(("conv_in", j))[:, 24 * n:24 * n + 24], sc_rows[:, ct * P:(ct + 1) * P], ident[0:24, 0:24])
                mm.then_inc(bank_full[use[("conv_in", j)][0]], 1)

            def first_tile(k):
                for j in range(2):
                    wait_after_read(pe, ("x", k, j))
                pe.wait_ge(split, 1)
                return product(pe, 0, [(w_hi[:, 0, k, :], w_lo[:, 0, k, :])], [(x_hi[:, k, :], x_lo[:, k, :])], start=k == 0, stop=k == KD - 1)

            pe.wait_ge(sem("x_scaled"), 5)
            for k in range(KD):
                for j in range(2):
                    key = ("x", k, j)
                    wait_read(pe, key)
                    for c, t0, m in (token_tiles()[0:NC] if j == 0 else token_tiles()[NC:]):
                        mm = pe.transpose(spare(key)[:, t0 % TP:t0 % TP + m], x_tok[0:m, c, k * P:(k + 1) * P], ident[0:m, 0:m])
                    mm.then_inc(bank_full[use[key][0]], 1)
                if k:
                    first_tile(k - 1)
            first_tile(KD - 1).then_inc(tile_done, 1)

            def norm_sums(n):
                pe.wait_ge(sem("squared"), n + 1)
                for h in range(2):
                    key = ("ss", n, h)
                    wait_read(pe, key)
                    pe.matmul(spare(key)[:, 0:HALF], pair_ones[:, :], sq[:, n % 2, HALVES[h]]).then_inc(bank_full[use[key][0]], 1)

            for c in range(N_FIRST):
                if c:
                    chunk_tile(pe, c, c, x_hi, x_lo, width=P if c < N_FIRST - 1 else NH)
                if 1 <= c <= KD + 2:
                    norm_sums(c - 1)
            for n in range(2):
                wait_freed(pe, KD + 2 + n)
                for c, t0, m in token_tiles():
                    key = ("v", n, c)
                    wait_read(pe, key)
                    pe.transpose(spare(key)[0:m, 0:P], v_t[:, n, t0:t0 + m], ident[:, :]).then_inc(bank_full[use[key][0]], 1)
            pe.wait_ge(sem("qk_made"), 2 * (KD + 2))
            for c, t0, m in token_tiles():
                key = ("k", c)
                wait_read(pe, key)
                for g in range(NKV):
                    mm = pe.transpose(spare(key)[0:m, g * HD:(g + 1) * HD], k_t[0:HD, g, t0:t0 + m], ident[0:HD, 0:HD])
                mm.then_inc(bank_full[use[key][0]], 1)
            key = ("dt", 0)
            wait_read(pe, key)
            pe.wait_ge(sem("dt_made"), 1)
            for c, t0, m in token_tiles():
                mm = pe.transpose(spare(key)[0:m, 2 * NH * c:2 * NH * (c + 1)], dt_t[:, t0:t0 + m], ident[0:2 * NH, 0:2 * NH])
            mm.then_inc(bank_full[use[key][0]], 1)

            pe.wait_ge(sem("constants"), sem_const_all[0])
            for t in (N_FIRST - 1, N_FIRST - 2):
                wait_freed(pe, t)
            for key in keys[FIRST_USES - 4:FIRST_USES]:
                wait_after_read(pe, key)

            def turn_pages(x):
                for half in range(2):
                    if x["page"]:
                        pe.wait_ge(sem(f"kt_made{half}"), x["page"] // SEQS)
                    for b in (2 * half, 2 * half + 1):
                        n = x["page"] + b
                        pe.wait_ge(sem(f"k_page_in{n % K_SLOTS}"), 16 * (n // K_SLOTS + 1))
                        for pair in range(2):
                            at = (b % 2 * 2 + pair) * P
                            mm = pe.transpose(W[2 + half][:, at:at + P], k_page[:, n % K_SLOTS, pair * P:(pair + 1) * P], ident[:, :])
                    mm.then_inc(sem("k_turned"), 1)

            def logits(x):
                u = x["u"]
                if u >= 4:
                    pe.wait_ge(sem("weights_made"), u - 3)
                out = score_bank(u)
                if x["kind"] == "prompt":
                    g, i, j = x["g"], x["i"], x["j"]
                    masked = i == j
                    mm = pe.matmul(out[:, :], k_t[:, g, j * P:(j + 1) * P], q_t[:, g * QG:(g + 1) * QG, i * P:(i + 1) * P],
                                   start=True, stop=not masked, skip_group_check=True)
                    if masked:
                        mm = pe.matmul(out[:, :], big_diag[:, :], bad_prompt[:, :, :], start=False, stop=True, skip_group_check=True)
                elif x["kind"] == "new":
                    for b in range(SEQS):
                        q0 = TP + (x["h"] * SEQS + b) * TD
                        for g in range(NKV):
                            at = (b * NKV + g) * QG * TD
                            pe.matmul(out[0:TS, at:at + QG * TD], k_t[:, g, TP:T], q_t[:, g * QG:(g + 1) * QG, q0:q0 + TD],
                                      start=b == 0 and g == 0, stop=True, skip_group_check=True)
                    mm = pe.matmul(out[0:TS, :], big_diag[0:TS, 0:TS], bad_new[:, x["h"]].rearrange("p b x t -> p (b x t)"),
                                   start=False, stop=True, skip_group_check=True)
                else:
                    if x["page"] == 0:
                        pe.wait_ge(sem("q_paired"), NKV)
                        pe.wait_ge(sem("bias_split"), 2)
                    for part in range(2):
                        bias = bias_cols[HD:HD + 1, part].rearrange("p h t -> p (h t)").unsqueeze(1).to_broadcast([1, SEQS, NQ * TD])
                        pe.matmul(out[:, :], ones_row[HD:HD + 1, :], bias, start=part == 0, stop=True, skip_group_check=True)
                    for b in range(SEQS):
                        if b % 2 == 0:
                            pe.wait_ge(sem(f"kt_made{b // 2}"), x["page"] // SEQS + 1)
                        for pair in range(2):
                            at = (b * 2 + pair) * 2 * QG * TD
                            mm = pe.matmul(out[:, at:at + 2 * QG * TD], kt_page[:, b, pair, :],
                                           q_pair[:, x["h"] * SEQS + b, pair].rearrange("p e c -> p (e c)"),
                                           start=False, stop=True, skip_group_check=True)
                mm.then_inc(sem("logits_done"), 1)

            def subtract_sums(x):
                u = x["u"]
                m = TS if x["kind"] == "new" else P
                pe.wait_ge(sem("sp_made"), u + 1)
                mm = pe.matmul(score_bank(u)[0:m, :], neg_suffix[0:m, 0:m], sp[0:m, u % 4, :], start=False, stop=x["n"] == 0, skip_group_check=True)
                if x["n"]:
                    pe.wait_ge(sem("later_lo_made"), x["laters"])
                    for part in (later_hi[:, u % 2, :], later_lo[:, :]):
                        mm = pe.matmul(score_bank(u)[:, :], neg_ones[:, :], part, start=False, stop=True, skip_group_check=True)
                mm.then_inc(sem("sums_done"), 1)

            def weigh_values(x):
                u, ch = x["u"], x["chain"]
                out = W[ch % 2]
                pe.wait_ge(sem("weights_made"), u + 1)
                if x["n"] == 0 and ch >= 2:
                    pe.wait_ge(sem("out_read"), ch - 1)
                if x["kind"] == "prompt":
                    g = x["g"]
                    mm = pe.matmul(out[0:HD, :], v_tok[:, x["j"], g * HD:(g + 1) * HD], wts[:, u % 2, :], start=x["n"] == 0, stop=x["last"], skip_group_check=True)
                else:
                    for b in range(SEQS):
                        if x["kind"] == "page":
                            n = x["page"] + b
                            pe.wait_ge(sem(f"v_page_in{n % 8}"), 16 * (n // 8 + 1))
                        for pair in range(2):
                            cols = slice(pair * P, (pair + 1) * P)
                            v, m = (v_page[:, n % 8, cols], P) if x["kind"] == "page" else (v_tok[0:TS, NC, cols], TS)
                            at = (b * 2 + pair) * 2 * QG * TD
                            mm = pe.matmul(out[:, at:at + 2 * QG * TD], v, wts[0:m, u % 2, at:at + 2 * QG * TD],
                                           start=x["n"] == 0 and b == 0 and pair == 0, stop=x["last"], skip_group_check=True)
                mm.then_inc(sem("pv_done"), 1)

            for t in range(NU + 3):
                if t < NU:
                    logits(units[t])
                if t + 1 < NU and units[t + 1]["kind"] == "page":
                    turn_pages(units[t + 1])
                if 2 <= t < NU + 2:
                    subtract_sums(units[t - 2])
                if t >= 3:
                    weigh_values(units[t - 3])
                if t == NU:
                    assert C_GATE_A % 2 != (NU - 1) % 4 // 2
                    pe.wait_ge(sem("weights_made"), NU - 2)
                    chunk_tile(pe, C_GATE_A, C_GATE_A, x_hi, x_lo)

            pe.wait_ge(sem("weights_made"), NU)
            pe.wait_ge(sem("out_read"), units[-1]["chain"] + 1)
            chunk_tile(pe, C_GATE_A + 1, C_GATE_A + 1, o_hi, o_lo)
            with pe.Fori(1, KD) as i:
                chunk_tile(pe, C_GATE_A, C_GATE_A, x_hi, x_lo, 2, i)
                chunk_tile(pe, C_GATE_A + 1, C_GATE_A + 1, o_hi, o_lo, 2, i)

            key = ("decays", 0)
            for half in range(2):
                pe.wait_ge(sem(f"kt_made{half}"), NB * PAGES // SEQS)
            pe.wait_ge(sem("out_read"), units[-1]["chain"] + 1)
            out = spare(key)
            for c, t0, m in token_tiles():
                mask = after if c < NC else after_b
                pe.matmul(out[0:m, NH * c:NH * (c + 1)], mask[0:m, 0:m], dt_tok[0:m, c, NH:2 * NH], start=c == 0, stop=True, skip_group_check=True)
            for c in range(NC):
                pe.matmul(out[:, 256 + NH * c:256 + NH * (c + 1)], ones[:, :], dt_tok[:, c, NH:2 * NH], start=False, stop=True, skip_group_check=True)
            pe.wait_ge(sem("a_seq_made"), 1)
            for e in range(2):
                mm = pe.matmul(out[e * HD:(e + 1) * HD, 384:384 + NB * NH // 2], ones[0:TS, 0:HD],
                               a_seq[:, :, :].rearrange("p (j e) b -> p j e b", e=2)[:, :, e, :], start=False, stop=True, skip_group_check=True)
            mm.then_inc(bank_full[use[key][0]], 1)

            def gemm(key):
                c, t = chunk_of[key], tile_of[key]
                if key[0] != "pb":
                    chunk_tile(pe, c, t, x_hi, x_lo)
                    return
                pe.wait_ge(split, c + 1)
                pe.wait_ge(sem("y_split"), key[1] + 1)
                wh = w_hi[:, c % 2].rearrange("p t n -> p (t n)").rearrange("p (t n) -> p t n", t=PG)
                wl = w_lo[:, c % 2].rearrange("p t n -> p (t n)").rearrange("p (t n) -> p t n", t=PG)
                for n in range(2):
                    w = [(wh[:, k, n * P:(n + 1) * P], wl[:, k, n * P:(n + 1) * P]) for k in range(PG)]
                    mm = product(pe, t + n, w, [(y_hi[:, k, :], y_lo[:, k, :]) for k in range(PG)])
                    mm.then_inc(tile_done, 1)

            def by_token(g):
                pe.wait_ge(sem("conv_done"), 6 * (g + 1))
                for c, t0, m in token_tiles():
                    key = ("x_tok", g, c)
                    wait_read(pe, key)
                    for j in range(PG):
                        mm = pe.transpose(spare(key)[0:m, j * P:(j + 1) * P], xs_t[:, j, t0:t0 + m], ident[:, :])
                    mm.then_inc(bank_full[use[key][0]], 1)
                b_t, c_t = bc_t[:, g % 2, 0, :], bc_t[:, g % 2, 1, :]
                key = ("b_tok", g)
                wait_read(pe, key)
                for c in range(NC):
                    mm = pe.transpose(spare(key)[:, c * P:(c + 1) * P], b_t[:, c * P:(c + 1) * P], ident[:, :])
                mm.then_inc(bank_full[use[key][0]], 1)
                key = ("cb", g)
                wait_read(pe, key)
                for c in range(NC):
                    mm = pe.matmul(spare(key)[:, c * P:(c + 1) * P], b_t[:, c * P:(c + 1) * P], c_t[:, c * P:(c + 1) * P],
                                   start=c == 0, stop=True, skip_group_check=True)
                mm.then_inc(bank_full[use[key][0]], 1)
                key = ("sample_bc", g)
                wait_read(pe, key)
                pe.transpose(spare(key)[0:TS, 0:P], b_t[:, TP:T], ident[:, :])
                pe.matmul(spare(key)[0:TS, P:P + TS], b_t[:, TP:T], c_t[:, TP:T], start=True, stop=True,
                          skip_group_check=True).then_inc(bank_full[use[key][0]], 1)

            def segments(g, c):
                m = P if c < NC else TS
                mask = after_r if c < NC else after_b_r
                parts = [a[0:m, :, 0:m] for a in (a_upto_hi, a_upto_lo)]
                pe.wait_ge(sem("a_upto_made"), 2 * (g * 5 + c + 1))
                for q in range(2):
                    key = ("seg", g, c, q)
                    wait_read(pe, key)
                    out = spare(key)[0:m, :].rearrange("p (h l) -> p h l", l=P)[:, :, 0:m]
                    for n, a in enumerate(parts):
                        mm = pe.matmul(out, mask[0:m, 0:m], a[:, 4 * q:4 * q + 4, :], start=n == 0, stop=n == 1, skip_group_check=True)
                    mm.then_inc(bank_full[use[key][0]], 1)
                if c:
                    key = ("e", g, c)
                    wait_read(pe, key)
                    out = spare(key).rearrange("p (j l) -> p j l", l=P)[:, :, 0:m]
                    for e in range(2):
                        for n, a in enumerate(parts):
                            mm = pe.matmul(out, one_half[0:m, e, :], a.rearrange("p (j e) l -> p j e l", e=2)[:, :, e, :],
                                           start=e == 0 and n == 0, stop=e == 1 and n == 1, skip_group_check=True)
                    mm.then_inc(bank_full[use[key][0]], 1)

            def outputs(g, c):
                st = g * 5 + c
                m = P if c < NC else TS
                if 0 < c < NC:
                    key = ("y_chunk_old", g, c)
                    wait_read(pe, key)
                    wait_after_read(pe, ("state", g, c - 1))
                    for j in range(PG):
                        mm = pe.matmul(spare(key)[:, j * P:(j + 1) * P], state[:, (c - 1) % 2, j * P:(j + 1) * P],
                                       bc_t[:, g % 2, 1, c * P:(c + 1) * P], start=j == 0, stop=True, skip_group_check=True)
                    mm.then_inc(bank_full[use[key][0]], 1)
                if c < NC:
                    key = ("state", g, c)
                    wait_read(pe, key)
                    pe.wait_ge(sem("xend_made"), g * NC + c + 1)
                    pe.matmul(spare(key)[:, :], b_tok[:, c, :], xend[:, c % 2].rearrange("p h d -> p (h d)")).then_inc(bank_full[use[key][0]], 1)
                key = ("y_new", g, c)
                wait_read(pe, key)
                pe.wait_ge(sem("decay_made"), st + 1)
                for j in range(PG):
                    for e in range(2):
                        h = 2 * j + e
                        mm = pe.matmul(spare(key)[e * HD:(e + 1) * HD, j * P:j * P + m], xdt[0:m, c, h, :], decay[0:m, h, 0:m],
                                       start=j == 0, stop=True, skip_group_check=True)
                mm.then_inc(bank_full[use[key][0]], 1)

            def turn_old(g, b):
                n = g * NB + b
                key = ("old_t", g, b)
                wait_read(pe, key)
                pe.wait_ge(sem(f"state_in{b % 2}"), 16 * (n // 2 + 1))
                for j in range(PG):
                    mm = pe.transpose(spare(key)[:, j * P:(j + 1) * P], old[:, b % 2, j, :], ident[:, :])
                mm.then_inc(bank_full[use[key][0]], 1)

            def sequence(g, b):
                key = ("y_seq_old", g, b)
                wait_read(pe, key)
                wait_after_read(pe, ("old_t", g, b))
                for j in range(PG):
                    mm = pe.matmul(spare(key)[:, j * TD:(j + 1) * TD], old_t[:, b % 2, j, :],
                                   bc_t[:, g % 2, 1, TP + b * TD:TP + (b + 1) * TD], start=j == 0, stop=True, skip_group_check=True)
                mm.then_inc(bank_full[use[key][0]], 1)
                key = ("new_state", g, b)
                wait_read(pe, key)
                pe.wait_ge(sem("b_seq_made"), g + 1)
                pe.wait_ge(sem("xend_s_made"), g + 1)
                for j in range(PG):
                    mm = pe.matmul(spare(key)[:, j * P:(j + 1) * P], xend_s[:, 2 * j:2 * j + 2, :].rearrange("p h d -> p (h d)"),
                                   b_seq[:, b, :], start=j == 0, stop=True, skip_group_check=True)
                mm.then_inc(bank_full[use[key][0]], 1)

            for key in before_groups:
                gemm(key)
            for g in range(NG):
                by_token(g)
                plan = ssd_plan(g)
                for c in range(5):
                    before, later = plan[c]
                    segments(g, c)
                    for key in before:
                        gemm(key)
                    outputs(g, c)
                    for b in (2 * c, 2 * c + 1) if c < NC else ():
                        turn_old(g, b)
                    for key in later:
                        gemm(key)
                    for b in (2 * c, 2 * c + 1) if c < NC else ():
                        sequence(g, b)
                before, later = plan[5]
                key = ("state_out", g)
                wait_read(pe, key)
                wait_after_read(pe, ("state", g, NC - 1))
                for j in range(PG):
                    mm = pe.transpose(spare(key)[:, j * P:(j + 1) * P], state[:, (NC - 1) % 2, j * P:(j + 1) * P], ident[:, :])
                mm.then_inc(bank_full[use[key][0]], 1)
                for key in before:
                    gemm(key)
                for j in range(PG):
                    pe.wait_ge(sem("y_squared"), PG * g + j + 1)
                    for h in range(2):
                        key = ("y_ss", g, h)
                        if j == 0:
                            wait_read(pe, key)
                        mm = pe.matmul(spare(key)[:, 0:HALF], ones[:, :], conv_acc[:, j % 2, HALVES[h]], start=j == 0, stop=j == PG - 1, skip_group_check=True)
                        if j == PG - 1:
                            mm.then_inc(bank_full[use[key][0]], 1)
                    if j < 2:
                        mm.then_inc(sem("y_summed"), 1)
                for key in later:
                    gemm(key)
            pe.wait_ge(sem("conv_tails"), CT)
            for j in range(6):
                key = ("conv_out", j)
                wait_read(pe, key)
                for n in range(4):
                    mm = pe.transpose(spare(key)[0:27, n * P:(n + 1) * P], conv_out[:, 4 * j + n, :], ident[:, :])
                mm.then_inc(bank_full[use[key][0]], 1)
            for key in last_pb:
                gemm(key)

            with pe.Fori(0, KD // 2) as i:
                for k in range(2):
                    chunk_tile(pe, C_GATE_B + k, T_GATE_B + k, x_hi, x_lo, 2, i)
            for key in keys[N_USES - 4:]:
                wait_after_read(pe, key)
            pe.wait_ge(sem("x_again_in"), 32)

            def res_sums(n):
                pe.wait_ge(sem("res_squared"), n + 1)
                for h in range(2):
                    mm = pe.matmul(W[h][:, 0:HALF], ones[:, :], prod2[:, n % 2, HALVES[h]], start=n == 0, stop=n == KD - 1, skip_group_check=True)
                mm.then_inc(sem("res_summed"), 1)

            for n in range(KD):
                c, t = C_OUT + n, T_OUT + n
                pe.wait_ge(tile_free[t % 2], t // 2 + 1)
                begun = set()
                for cc, t0, m in token_tiles():
                    for h in range(2):
                        a, z = max(t0, HALF * h), min(t0 + m, HALF * (h + 1))
                        if a < z:
                            pe.matmul(G[t % 2][:, h, a - HALF * h:z - HALF * h], x_again[0:m, cc, n * P:(n + 1) * P],
                                      ident[0:m, a - t0:z - t0], start=h not in begun, stop=True, skip_group_check=True)
                            begun.add(h)
                pe.wait_ge(split, c + 1)
                w = [(w_hi[:, c % 2, k, :], w_lo[:, c % 2, k, :]) for k in range(KD)]
                for k in range(KD):
                    if n == 0:
                        pe.wait_ge(sem("merged_split"), k + 3)
                    mm = product(pe, t, w[k:k + 1], [(m_hi[:, k, :], m_lo[:, k, :])], start=False, stop=k == KD - 1, onto=True)
                mm.then_inc(tile_done, 1)
                if n:
                    res_sums(n - 1)
            res_sums(KD - 1)
            pe.wait_ge(split, C_FFN + 1)
            for k in range(KD):
                pe.wait_ge(sem("h2_split"), k + 1)
                mm = product(pe, T_FFN, [(w_hi[:, C_FFN % 2, k, :], w_lo[:, C_FFN % 2, k, :])], [(x_hi[:, k, :], x_lo[:, k, :])],
                             start=k == 0, stop=k == KD - 1)
            mm.then_inc(tile_done, 1)
            chunk_tile(pe, C_FFN + 1, T_FFN + 1, x_hi, x_lo)
            with pe.Fori(1, KF) as i:
                for k in range(2):
                    chunk_tile(pe, C_FFN + k, T_FFN + k, x_hi, x_lo, 2, i)

            def turn_finished(t, step=0, i=0):
                n = (t - T_DOWN) % 2
                wait_freed(pe, t, step, i)
                pe.wait_ge(sem("y_tok_made"), t - T_DOWN + 1 + step * i)
                for cc, t0, m in token_tiles():
                    out = W[2][:, cc * P:(cc + 1) * P] if cc < NC else W[3][0:m, 0:P]
                    mm = pe.transpose(out, prod2[:, n, t0:t0 + m], ident[:, :])
                mm.then_inc(sem("y_turned"), 1)

            def down_tiles(i, first=False):
                for n in range(2):
                    for k, (k0, kn) in enumerate(DOWN_K):
                        c = C_DOWN + 3 * n + k
                        pe.wait_ge(split, c + 1 + 6 * i)
                        if first and n == 0:
                            pe.wait_ge(sem("f_split"), k0 + kn + 2)
                        w = [(w_hi[:, c % 2, q, :], w_lo[:, c % 2, q, :]) for q in range(kn)]
                        x = [(f_hi[:, k0 + q, :], f_lo[:, k0 + q, :]) for q in range(kn)]
                        mm = product(pe, T_DOWN + n, w, x, start=k == 0, stop=k == 2, step=2, i=i)
                        mm.then_inc(tile_done if k == 2 else part_done, 1)
                        if k == 0 and not (first and n == 0):
                            turn_finished(T_DOWN + n - 1, 2, i)

            down_tiles(0, first=True)
            with pe.Fori(1, KD // 2) as i:
                down_tiles(i)
            turn_finished(T_DOWN + KD - 1)

        @block.scalar
        def _(act):
            eng = act
            eng.dma_start(par_rows[0:CW * CT, :], conv_w[0].rearrange("w (t p) -> (w t) p", p=P)).then_inc(sem("par_in"), 16)
            eng.dma_start(par_rows[CW * CT:5 * CT, :], conv_b[0].rearrange("(t p) -> t p", p=P)).then_inc(sem("par_in"), 16)
            for at, w, n in ((PAR_N1, norm1_w, KD), (PAR_N2, norm2_w, KD), (PAR_SSD, ssd_norm_w, DI // P)):
                eng.dma_start(par2_rows[at:at + n, :], w[0].rearrange("(t p) -> t p", p=P)).then_inc(sem("par_in"), 16)
            for at, w in ((PAR_Q, q_norm_w), (PAR_K, k_norm_w)):
                for e in range(2):
                    eng.dma_start(par2_rows[at:at + 1, e * HD:(e + 1) * HD], w).then_inc(sem("par_in"), 16)
            eng.dma_start(d_rows[32:48, :], d_skip[0].rearrange("(j e) -> j e", e=2)).then_inc(sem("d_in"), 16)
            eng.dma_start(dt_par[:, 0:1], dt_bias[0].rearrange("(h o) -> h o", o=1)).then_inc(sem("dt_par_in"), 16)
            eng.dma_start(dt_par[:, 1:2], a_log[0].rearrange("(h o) -> h o", o=1)).then_inc(sem("dt_par_in"), 16)
            eng.dma_start(sc_rows[:, :], state_conv[0].rearrange("b t c -> (b t) c")).then_inc(sem("conv_state_in"), 16)

            eng.wait_ge(sem("constants"), sem_const_first[0])
            for c, t0, m in token_tiles():
                eng.wait_ge(sem(f"x_in{c}"), 16)
                junk = (o_hi if c < NC else o_lo)[0:m, 2 * (c % NC):2 * (c % NC) + 2, 0:512]
                eng.activation(junk, x_tok[0:m, c, :].rearrange("p (a b) -> p a b", a=2), ACT.Square,
                               accum_out=stats[0:m, 0, c:c + 1]).then_inc(sem("x_squared"), 1)
            eng.wait_ge(sem("x_squared"), 5)
            eng.activation(stats[:, 1, :], stats[:, 0, :], ACT.Sqrt, scale=1.0 / D, bias=eps_col[:, 0:1]).then_inc(sem("x_rooted"), 1)
            eng.preload_act_table_set("natural_log_exp_and_others")
            make_hi(0)
            for j, dst in ((0, conv_par), (1, par)):
                key = ("par", j)
                wait_full(eng, key)
                n = 5 * CT if j == 0 else 50
                eng.activation(dst[:, :], spare(key)[:, 0:n], ACT.Copy).then_inc(bank_read[use[key][0]], 1)
            for j in range(2):
                key = ("conv_in", j)
                wait_full(eng, key)
                eng.activation(conv_in[:, 12 * j:12 * j + 12, :].rearrange("p t n -> p (t n)"), spare(key)[:, 0:288], ACT.Copy)\
                   .then_inc(bank_read[use[key][0]], 1)
            wait_after_read(eng, ("par", 1))
            for k in range(KD):
                for j in range(2):
                    wait_full(eng, ("x", k, j))
                    cols = slice(0, TP) if j == 0 else slice(TP, T)
                    n = TP if j == 0 else TS
                    eng.activation(x_hi[:, k, cols], spare(("x", k, j))[:, 0:n], ACT.Copy, scale=par[:, PAR_N1 + k:PAR_N1 + k + 1])\
                       .then_inc(sem("x_hi_made"), 1)

            def root_of_sums(n):
                for h in range(2):
                    key = ("ss", n, h)
                    wait_full(eng, key)
                    eng.activation(root[:, HALVES[h]], spare(key)[:, 0:HALF], ACT.Ln, scale=1.0 / HD, bias=eps_col[:, 0:1])\
                       .then_inc(bank_read[use[key][0]], 1)
                for h in range(2):
                    wait_after_read(eng, ("ss", n, h))
                if n:
                    eng.wait_ge(sem("qk_made"), 2 * n)
                eng.activation(rinv[:, :], root[:, :], ACT.Exp, scale=-0.5).then_inc(sem("rinv_made"), 1)

            for c in range(N_FIRST):
                make_hi(c + 1, width=NH if c + 1 == N_FIRST - 1 else P, after_tiles=c if c else None)
                if 1 <= c <= KD + 2:
                    root_of_sums(c - 1)
                if c < KD + 2:
                    wait_freed(eng, c)
                    if c >= 2:
                        wait_full(eng, ("ss", c - 2, 1))
                    eng.activation(sq[:, c % 2, :], pre[:, c % 2, :], ACT.Square).then_inc(sem("squared"), 1)
            eng.wait_ge(sem("dt_par_in"), 32)
            eng.activation(dt_par[:, 2:3], dt_par[:, 1:2], ACT.Exp).then_inc(sem("a_exp"), 1)
            eng.wait_ge(sem("dt_clamped"), 1)
            eng.activation(dt_w[:, 1, :], dt_w[:, 1, :], ACT.Exp).then_inc(sem("dt_exp"), 1)
            eng.wait_ge(sem("dt_exp"), 1)
            eng.activation(dt_w[:, 1, :], dt_w[:, 1, :], ACT.Ln, bias=1.0).then_inc(sem("dt_ln"), 1)
            for n in range(2):
                for c, t0, m in token_tiles():
                    key = ("v", n, c)
                    wait_full(eng, key)
                    eng.activation(v_tok[0:m, c, n * P:(n + 1) * P], spare(key)[0:m, 0:P], ACT.Copy).then_inc(bank_read[use[key][0]], 1)
            for c, t0, m in token_tiles():
                key = ("k", c)
                wait_full(eng, key)
                eng.activation(k_out[0:m, c, :], spare(key)[0:m, 0:NKV * HD], ACT.Copy).then_inc(bank_read[use[key][0]], 1)
            key = ("dt", 0)
            wait_full(eng, key)
            n = NC * 2 * NH
            eng.activation(dt_tok[:, 0:NC, :].rearrange("p c h -> p (c h)"), spare(key)[:, 0:n], ACT.Copy)
            eng.activation(dt_tok[0:TS, NC, :], spare(key)[0:TS, n:n + 2 * NH], ACT.Copy).then_inc(bank_read[use[key][0]], 1)

            eng.wait_ge(sem("constants"), sem_const_all[0])
            eng.wait_ge(sem("qk_made"), 2 * (KD + 2))
            for g in range(NKV):
                eng.activation(q_pair[g % 2 * HD:(g % 2 + 1) * HD, :, g // 2, g % 2, :].rearrange("p b (x t) -> p b x t", x=QG),
                               q_t[0:HD, g * QG:(g + 1) * QG, TP:T].rearrange("p x (b t) -> p b x t", b=NB), ACT.Copy).then_inc(sem("q_paired"), 1)
            eng.activation(ones_row[HD:HD + 1, :], ones[HD:HD + 1, :], ACT.Copy)
            eng.activation(bias_cols[HD:HD + 1, 0], bias_row[HD:HD + 1, :].unsqueeze(2).to_broadcast([1, NQ, TD]), ACT.Copy).then_inc(sem("bias_split"), 1)
            eng.preload_act_table_set("natural_log_exp_and_others")
            for key in [("k", c) for c in range(5)]:
                wait_after_read(eng, key)
            eng.wait_ge(sem("stored_k"), 32)

            def read_output(x):
                wait_chain(eng, x)
                for src, hi, _ in chain_views(x):
                    eng.activation(hi, src, ACT.Copy).then_inc(sem("o_hi_made"), 1)

            def split_later(x):
                u = x["u"]
                if x["n"] == 1:
                    eng.wait_ge(sem("sp_made"), u)
                else:
                    eng.wait_ge(sem("acc_made"), x["accs"])
                if u >= 2:
                    eng.wait_ge(sem("sums_done"), u - 1)
                eng.activation(later_hi[:, u % 2, :], later_sum(x), ACT.Copy).then_inc(sem("later_hi_made"), 1)

            for t in range(NU + 4):
                if t and t <= NU and units[t - 1]["n"]:
                    split_later(units[t - 1])
                if t < NU:
                    x = units[t]
                    m = TS if x["kind"] == "new" else P
                    z = zs[0:m, t % 2, :]
                    eng.wait_ge(sem("clamped"), t + 1)
                    eng.activation(z, z, ACT.Exp).then_inc(sem("exp_made"), 1)
                    eng.wait_ge(sem("exp_made"), t + 1)
                    eng.activation(z, z, ACT.Ln, bias=1.0).then_inc(sem("ln_made"), 1)
                if t + 1 < NU and units[t + 1]["kind"] == "page":
                    read_turned(eng, nc.scalar.activation, units[t + 1], 0)
                if 2 <= t < NU + 2:
                    u = t - 2
                    m = TS if units[u]["kind"] == "new" else P
                    eng.wait_ge(sem("sums_done"), u + 1)
                    if u >= 2:
                        eng.wait_ge(sem("pv_done"), u - 1)
                    eng.activation(wts[0:m, u % 2, :], score_bank(u)[0:m, :], ACT.Exp).then_inc(sem("weights_made"), 1)
                if t == NU + 2:
                    make_hi(C_GATE_A + 1, after_tiles=C_GATE_A)
                if t >= 4 and units[t - 4]["last"]:
                    read_output(units[t - 4])

            def gates_a(i, first=False):
                eng.preload_act_table_set("sigmoid_and_others")
                for n in range(2):
                    c = C_GATE_A + 2 * n
                    if not (first and n == 0):
                        make_hi(c + 1, 4, i, after_tiles=c + 4 * i)
                    wait_tile(eng, c, 4, i)
                    eng.wait_ge(tile_free[(c + 1) % 2], half(c + 1 - 4, 4, i) + 2)
                    eng.activation(halves(gate[:, n, :]), tile(c), ACT.Sigmoid).then_inc(tile_free[c % 2], 1)
                    make_hi(c + 2, 4, i, after_tiles=c + 1 + 4 * i)

            gates_a(0, first=True)
            with eng.Fori(1, KD // 2) as i:
                gates_a(i)

            for e in range(2):
                eng.wait_ge(sem(f"gated_out{e}"), 16 * (KD // 2))
            eng.activation(after_r[:, :], after[:, :], ACT.Copy)
            eng.activation(after_b_r[:, :], after_b[:, :], ACT.Copy)
            for e in range(2):
                eng.activation(one_half[:, e, e * HD:(e + 1) * HD], ones[:, 0:HD], ACT.Copy)
                eng.activation(one_half[:, e, (1 - e) * HD:(2 - e) * HD], ones[:, 0:HD], ACT.Copy, scale=0.0)
            for rows, cs in ((slice(0, P), slice(0, NC)), (slice(0, TS), slice(NC, NC + 1))):
                eng.activation(a_hi[rows, cs, :], dt_tok[rows, cs, NH:2 * NH], ACT.Copy).then_inc(sem("a_hi_made"), 1)
            key = ("decays", 0)
            wait_full(eng, key)
            for e in range(2):
                eng.wait_ge(sem(f"gated_out{e}"), 16 * (KD // 2))
            src = spare(key)
            eng.activation(end_decay[:, 0:NC, :].rearrange("p c h -> p (c h)"), src[:, 0:NC * NH], ACT.Exp)
            eng.activation(end_decay[0:TS, NC, :], src[0:TS, NC * NH:5 * NH], ACT.Exp)
            eng.activation(chunk_decay[:, :, :].rearrange("p c h -> p (c h)"), src[:, 256:256 + NC * NH], ACT.Exp)
            eng.activation(seq_decay[:, :, :].rearrange("p j b -> p (j b)"), src[:, 384:384 + NB * NH // 2], ACT.Exp)\
               .then_inc(bank_read[use[key][0]], 1)

            def conv_silu(key):
                n = conv_n[key]
                dst = conv_dst(key)
                eng.wait_ge(sem("conv_made"), n + 1)
                src = conv_acc[:, n % 2, :]
                eng.activation(dst[:, 0:TP], src[:, 0:TP], ACT.Silu)
                eng.activation(decode_block(dst, TP), src[:, 3 + TP:SRC].rearrange("p (b t) -> p b t", b=NB)[:, :, 0:TD], ACT.Silu)\
                   .then_inc(sem("conv_done"), 1)

            pending = []

            def flush():
                while pending:
                    conv_silu(pending.pop(0))

            def slot(key):
                c, t = chunk_of[key], tile_of[key]
                if c + 1 < N_CHUNKS:
                    make_hi(c + 1, after_tiles=tiles_after(c - 1))
                if key[0] in ("bc", "x"):
                    n = conv_n[key]
                    wait_tile(eng, t)
                    eng.wait_ge(sem("conv_zeros"), 2)
                    if n >= 2:
                        eng.wait_ge(sem("conv_made"), n - 1)
                        eng.wait_ge(sem("conv_tails"), n - 1)
                    dst = conv_src[:, n % 2, :]
                    eng.activation(dst[:, 3:3 + HALF], G[t % 2][:, 0, 0:HALF], ACT.Copy)
                    eng.activation(dst[:, 3 + HALF:3 + TP], G[t % 2][:, 1, 0:TP - HALF], ACT.Copy)
                    eng.activation(dst[:, 3 + TP:SRC].rearrange("p (b t) -> p b t", b=NB)[:, :, 3:3 + TD],
                                   decode_block(G[t % 2][:, 1, :], TP - HALF), ACT.Copy).then_inc(tile_free[t % 2], 1)
                    flush()
                    pending.append(key)
                elif key[0] == "z":
                    flush()
                    wait_tile(eng, t)
                    if key[1]:
                        eng.wait_ge(sem("y_gated"), PG * key[1])
                    eng.activation(halves(z_s[:, key[2], :]), tile(t), ACT.Silu).then_inc(tile_free[t % 2], 1)

            def by_token(g):
                flush()
                if g:
                    wait_full(eng, ("state", g - 1, NC - 1))
                key = ("b_tok", g)
                wait_full(eng, key)
                eng.activation(b_tok[:, 0:NC, :].rearrange("p c n -> p (c n)"), spare(key)[:, :], ACT.Copy).then_inc(bank_read[use[key][0]], 1)
                key = ("sample_bc", g)
                wait_full(eng, key)
                if g:
                    eng.wait_ge(sem("b_seq_made"), g)
                eng.activation(b_tok[0:TS, NC, :], spare(key)[0:TS, 0:P], ACT.Copy).then_inc(sem("b_tok_made"), 1)

            def segments(g, c):
                st = g * 5 + c
                m = P if c < NC else TS
                for q in range(2):
                    key = ("seg", g, c, q)
                    wait_full(eng, key)
                    if st:
                        wait_full(eng, ("y_new", (st - 1) // 5, (st - 1) % 5))
                    if g and c == 0:
                        eng.wait_ge(sem("y_scaled"), PG * g)
                    eng.activation(decay[0:m, 4 * q:4 * q + 4, 0:m], spare(key).rearrange("p (e l) -> p e l", l=P)[0:m, :, 0:m], ACT.Exp)\
                       .then_inc(bank_read[use[key][0]], 1)
                if c:
                    key = ("e", g, c)
                    wait_full(eng, key)
                    if g * NC + c - 1:
                        eng.wait_ge(sem("y_added"), g * NC + c - 1)
                    if g and c == 1:
                        eng.wait_ge(sem("stored_prompt_state"), 16 * g)
                    eng.activation(e_t[:, :, 0:m], spare(key).rearrange("p (j l) -> p j l", l=P)[:, :, 0:m], ACT.Exp)\
                       .then_inc(bank_read[use[key][0]], 1)

            def sequence(g, b):
                key = ("old_t", g, b)
                wait_full(eng, key)
                n = g * NB + b
                if n >= 2:
                    wait_full(eng, ("y_seq_old", (n - 2) // NB, (n - 2) % NB))
                eng.activation(old_t[:, b % 2].rearrange("p j n -> p (j n)"), spare(key)[:, :], ACT.Copy).then_inc(bank_read[use[key][0]], 1)

            for key in before_groups:
                slot(key)
            for g in range(NG):
                by_token(g)
                plan = ssd_plan(g)
                for c in range(5):
                    before, later = plan[c]
                    segments(g, c)
                    for key in before:
                        slot(key)
                    for b in (2 * c, 2 * c + 1) if c < NC else ():
                        sequence(g, b)
                    for key in later:
                        slot(key)
                before, later = plan[5]
                flush()
                eng.wait_ge(sem("conv_done"), 6 * min(g + 2, NG))
                key = ("state_out", g)
                wait_full(eng, key)
                eng.wait_ge(sem("y_added"), NC * (g + 1))
                eng.activation(state_out[:, :, :].rearrange("p j n -> p (j n)"), spare(key)[:, :], ACT.Copy).then_inc(bank_read[use[key][0]], 1)
                for j in range(PG):
                    eng.wait_ge(sem("y_gated"), PG * g + j + 1)
                    if j >= 2:
                        eng.wait_ge(sem("y_summed"), 2 * g + j - 1)
                    eng.activation(conv_acc[:, j % 2, 0:T], y_t[:, j, :], ACT.Square).then_inc(sem("y_squared"), 1)
                    if j == 1:
                        for key in before:
                            slot(key)
                eng.preload_act_table_set("natural_log_exp_and_others")
                for h in range(2):
                    key = ("y_ss", g, h)
                    wait_full(eng, key)
                    eng.activation(y_root[:, HALVES[h]], spare(key)[:, 0:HALF], ACT.Ln, scale=1.0 / (PG * P), bias=eps_col[:, 0:1])\
                       .then_inc(bank_read[use[key][0]], 1)
                for h in range(2):
                    wait_after_read(eng, ("y_ss", g, h))
                eng.activation(y_rinv, y_root, ACT.Exp, scale=-0.5).then_inc(sem("y_rooted"), 1)
                for j in range(PG):
                    eng.wait_ge(sem("y_scaled"), PG * g + j + 1)
                    if g:
                        wait_tile(eng, tile_of[("pb", g - 1, KD - 2)] + 1)
                    eng.activation(y_hi[:, j, :], y_t[:, j, :], ACT.Copy).then_inc(sem("y_hi_made"), 1)
                for key in later:
                    slot(key)
            for j in range(6):
                key = ("conv_out", j)
                wait_full(eng, key)
                eng.activation(conv_rows[j], spare(key)[0:27, :], ACT.Copy).then_inc(bank_read[use[key][0]], 1)
            for key in last_pb:
                slot(key)

            for n in range(2):
                eng.wait_ge(sem(f"state_stored{n}"), 16 * NG * NB // 2)
            eng.wait_ge(sem("stored_prompt_state"), 16 * NG)
            eng.wait_ge(sem("stored_conv"), 64)
            with eng.Fori(0, KD // 2) as i:
                eng.preload_act_table_set("sigmoid_and_others")
                for n in range(2):
                    c, t = C_GATE_B + n, T_GATE_B + n
                    make_hi(c + 1, 2, i, after_tiles=t + 2 * i)
                    wait_tile(eng, t, 2, i)
                    eng.wait_ge(sem("merged_split"), n + 1 + 2 * i)
                    eng.activation(halves(gate2[:, n, :]), tile(t), ACT.Sigmoid).then_inc(tile_free[t % 2], 1)
                    eng.wait_ge(sem("merged_made"), n + 1 + 2 * i)
                    eng.activation(m_hi[:, bass.ds(2 * i + n, 1), :], prod2[:, n:n + 1, :], ACT.Copy).then_inc(sem("m_hi_made"), 1)
            eng.wait_ge(sem("x_again_in"), 32)
            def res_square(n):
                wait_freed(eng, T_OUT + n)
                if n >= 2:
                    eng.wait_ge(sem("res_summed"), n - 1)
                eng.activation(prod2[:, n % 2, :], x_res[:, n, :], ACT.Square).then_inc(sem("res_squared"), 1)

            for n in range(KD):
                make_hi(C_OUT + n + 1, after_tiles=T_OUT + n)
                res_square(n)
            eng.preload_act_table_set("natural_log_exp_and_others")
            eng.wait_ge(sem("res_summed"), KD)
            for h in range(2):
                eng.activation(root2[:, HALVES[h]], W[h][:, 0:HALF], ACT.Ln, scale=1.0 / D, bias=eps_col[:, 0:1]).then_inc(sem("res_logged"), 1)
            eng.wait_ge(sem("res_logged"), 2)
            eng.activation(rinv2[:, :], root2[:, :], ACT.Exp, scale=-0.5).then_inc(sem("res_rooted"), 1)
            for k in range(KD):
                eng.wait_ge(sem("h2_made"), k + 1)
                eng.activation(x_hi[:, k, :], gate2[:, k % 2, :], ACT.Copy).then_inc(sem("h2_hi_made"), 1)
            with eng.Fori(0, KF // 2) as i:
                eng.preload_act_table_set("silu_and_others")
                for n in range(2):
                    c, t = C_FFN + 2 * n, T_FFN + 2 * n
                    make_hi(c + 1, 4, i, after_tiles=t + 4 * i)
                    wait_tile(eng, t, 4, i)
                    eng.wait_ge(tile_free[(t + 1) % 2], half(t + 1 - 4, 4, i) + 2)
                    eng.activation(halves(gate2[:, n, :]), tile(t), ACT.Silu).then_inc(tile_free[t % 2], 1)
                    make_hi(c + 2, 4, i, after_tiles=t + 1 + 4 * i)
                    wait_freed(eng, t + 1, 4, i)
                    eng.activation(f_hi[:, bass.ds(2 * i + n, 1), :], prod2[:, n:n + 1, :], ACT.Copy).then_inc(sem("f_hi_made"), 1)

            def y_out_of_psum(t, step=0, i=0, drain=True):
                eng.wait_ge(sem("y_turned"), t + 1 + step * i)
                if drain:
                    eng.wait_ge(sem("y_out"), 16 * (t + step * i))
                    eng.wait_ge(sem("y_out_s"), 16 * (t + step * i))
                eng.activation(y_tok[:, 0:NC, :].rearrange("p c n -> p (c n)"), W[2][:, :], ACT.Copy)
                eng.activation(y_tok[0:TS, NC, :], W[3][0:TS, 0:P], ACT.Copy).then_inc(sem("y_tok_made"), 1)

            def down_tile(n, i, first=False, last=False):
                for k in range(3):
                    if last and n == 1 and k == 2:
                        continue
                    after_tiles = T_DOWN + n + 2 * i if k == 0 else None
                    after_part = {0: None, 1: 2 * n + 1 + 4 * i, 2: 2 * n + 2 + 4 * i}[k]
                    make_hi(C_DOWN + 3 * n + k + 1, 6, i, tiles=DOWN_K[(k + 1) % 3][1], after_tiles=after_tiles, after_part=after_part)
                    if k == 0 and not (first and n == 0):
                        y_out_of_psum(n - 1, 2, i, drain=not first)

            eng.sem_inc(sem("y_tok_made"), 1)
            for n in range(2):
                down_tile(n, 0, first=True)
            with eng.Fori(1, KD // 2 - 1) as i:
                for n in range(2):
                    down_tile(n, i)
            for n in range(2):
                down_tile(n, KD // 2 - 1, last=True)
            y_out_of_psum(KD - 1)

        @block.vector
        def _(dve):
            eng = dve
            n_chain = [0]
            chain = sem("dve_chain")

            def link(ins):
                n_chain[0] += 1
                ins.then_inc(chain, 1)
                eng.wait_ge(chain, n_chain[0])

            eng.wait_ge(sem("d_in"), 16)
            eng.tensor_copy(par2_rows[32:48, :].rearrange("j (e p) -> j e p", e=2), d_rows[32:48, :].unsqueeze(2).to_broadcast([16, 2, HD]))\
               .then_inc(sem("d_spread"), 1)
            make_lo(0)
            eng.wait_ge(sem("x_rooted"), 1)
            link(eng.reciprocal(stats[:, 2, :], stats[:, 1, :]))
            for c, t0, m in token_tiles():
                eng.tensor_scalar(x_tok[0:m, c, :], x_tok[0:m, c, :], stats[0:m, 2, c:c + 1], None, ALU.mult).then_inc(sem("x_scaled"), 1)
            for k in range(KD):
                for j in range(2):
                    key = ("x", k, j)
                    eng.wait_ge(sem("x_hi_made"), 2 * k + j + 1)
                    cols = slice(0, TP) if j == 0 else slice(TP, T)
                    n = TP if j == 0 else TS
                    eng.scalar_tensor_tensor(out=x_lo[:, k, cols], in0=spare(key)[:, 0:n], scalar=par[:, PAR_N1 + k:PAR_N1 + k + 1],
                                             in1=f32(x_hi[:, k, cols]), op0=ALU.mult, op1=ALU.subtract).then_inc(bank_read[use[key][0]], 1)
            wait_after_read(eng, ("par", 1))
            link(eng.tensor_scalar(par[:, PAR_Q:PAR_Q + 1], par[:, PAR_Q:PAR_Q + 1], HD ** -0.5, None, ALU.mult))

            def finish_norm(n):
                eng.wait_ge(sem("rinv_made"), n + 1)
                dst, at, col = (q_t, 2 * n, PAR_Q) if n < KD else (k_t, 2 * (n - KD), PAR_K)
                for e in range(2):
                    rows = slice(e * HD, (e + 1) * HD)
                    eng.scalar_tensor_tensor(out=dst[0:HD, at + e, :], in0=pre[rows, n % 2, :], scalar=par[rows, col:col + 1],
                                             in1=rinv[rows, :], op0=ALU.mult, op1=ALU.mult).then_inc(sem("qk_made"), 1)

            for c in range(N_FIRST):
                make_lo(c + 1, width=NH if c + 1 == N_FIRST - 1 else P)
                if c < KD + 2:
                    wait_tile(eng, c)
                    if c >= 2:
                        eng.wait_ge(sem("squared"), c - 1)
                        eng.wait_ge(sem("qk_made"), 2 * (c - 1))
                    eng.tensor_copy(halves(pre[:, c % 2, :]), tile(c)).then_inc(tile_free[c % 2], 1)
                elif c < N_FIRST - 1:
                    wait_tile(eng, c)
                    eng.tensor_copy(halves(v_t[:, c - KD - 2, :]), tile(c)).then_inc(tile_free[c % 2], 1)
                if 1 <= c <= KD + 2:
                    finish_norm(c - 1)
            c = N_FIRST - 1
            wait_tile(eng, c)
            eng.wait_ge(sem("dt_par_in"), 32)
            eng.tensor_scalar(halves(dt_w[:, 0, :]), tile(c, NH), dt_par[:, 0:1], None, ALU.add).then_inc(tile_free[c % 2], 1)
            wait_freed(eng, c)
            eng.tensor_scalar(dt_w[:, 1, :], dt_w[:, 0, :], CLAMP, None, ALU.min).then_inc(sem("dt_clamped"), 1)
            eng.wait_ge(sem("dt_ln"), 1)
            link(eng.tensor_tensor(dt_t[0:NH, :], dt_w[:, 0, :], dt_w[:, 1, :], ALU.max))
            eng.wait_ge(sem("a_exp"), 1)
            link(eng.tensor_scalar(dt_w[:, 0, :], dt_t[0:NH, :], dt_par[:, 2:3], None, ALU.mult))
            eng.tensor_scalar(dt_t[NH:2 * NH, :], dt_w[:, 0, :], -1.0, None, ALU.mult).then_inc(sem("dt_made"), 1)

            eng.wait_ge(sem("bias_split"), 1)
            eng.tensor_tensor(bias_cols[HD:HD + 1, 1], bias_row[HD:HD + 1, :].unsqueeze(2).to_broadcast([1, NQ, TD]),
                              f32(bias_cols[HD:HD + 1, 0]), ALU.subtract).then_inc(sem("bias_split"), 1)
            eng.wait_ge(sem("stored_k"), 32)

            def softplus(u):
                x = units[u]
                m = TS if x["kind"] == "new" else P
                eng.wait_ge(sem("ln_made"), u + 1)
                if u >= 4:
                    eng.wait_ge(sem("sums_done"), u - 2)
                    if units[u - 2]["accs"]:
                        eng.wait_ge(sem("acc_made"), units[u - 2]["accs"])
                if x["kind"] == "new":
                    link(eng.memset(sp[TS:P, u % 4, :], 0.0))
                eng.tensor_tensor(sp[0:m, u % 4, :], score_bank(u)[0:m, :], zs[0:m, u % 2, :], ALU.max).then_inc(sem("sp_made"), 1)

            for t in range(NU + 4):
                if t < NU:
                    m = TS if units[t]["kind"] == "new" else P
                    eng.wait_ge(sem("logits_done"), t + 1)
                    if t >= 2:
                        eng.wait_ge(sem("sp_made"), t - 1)
                    eng.tensor_scalar(zs[0:m, t % 2, :], score_bank(t)[0:m, :], CLAMP, None, ALU.min).then_inc(sem("clamped"), 1)
                if 1 <= t <= NU:
                    softplus(t - 1)
                if t + 1 < NU and units[t + 1]["kind"] == "page":
                    read_turned(eng, lambda o, i, f: nc.vector.tensor_copy(o, i), units[t + 1], 1)
                if t == NU + 2:
                    make_lo(C_GATE_A + 1)
                if t >= 4 and units[t - 4]["last"]:
                    x = units[t - 4]
                    eng.wait_ge(sem("o_hi_made"), views_before(x["chain"], 1))
                    for src, hi, lo in chain_views(x):
                        ins = eng.tensor_tensor(lo, src, f32(hi), ALU.subtract)
                    ins.then_inc(sem("out_read"), 1)

            def gate_a_tiles(i, first=False):
                for n in range(2):
                    c = C_GATE_A + 2 * n
                    if not (first and n == 0):
                        make_lo(c + 1, 4, i)
                    make_lo(c + 2, 4, i)
                    wait_tile(eng, c + 1, 4, i)
                    wait_freed(eng, c, 4, i)
                    if not first:
                        eng.wait_ge(sem(f"gated_out{n}"), 16 * i)
                    eng.tensor_tensor(halves(gated[:, n, :]), tile(c + 1), halves(gate[:, n, :]), ALU.mult).then_inc(tile_free[(c + 1) % 2], 1)

            gate_a_tiles(0, first=True)
            with eng.Fori(1, KD // 2) as i:
                gate_a_tiles(i)

            for e in range(2):
                eng.wait_ge(sem(f"gated_out{e}"), 16 * (KD // 2))

            eng.wait_ge(sem("a_hi_made"), 2)
            for rows, cs in ((slice(0, P), slice(0, NC)), (slice(0, TS), slice(NC, NC + 1))):
                eng.tensor_tensor(a_lo[rows, cs, :], dt_tok[rows, cs, NH:2 * NH], f32(a_hi[rows, cs, :]), ALU.subtract).then_inc(sem("a_split"), 1)

            pending = []

            def convolve(key):
                n, ct = conv_n[key], src_tile(key)
                wait_freed(eng, tile_of[key])
                eng.wait_ge(sem("conv_heads"), n + 1)
                if n >= 2:
                    eng.wait_ge(sem("conv_done"), n - 1)
                src, dst, m = conv_src[:, n % 2, :], conv_acc[:, n % 2, 0:SRC - 3], SRC - 3
                link(eng.tensor_scalar(dst, src[:, 0:m], conv_par[:, ct:ct + 1], conv_par[:, CW * CT + ct:CW * CT + ct + 1], ALU.mult, ALU.add))
                for w in range(1, CW):
                    ins = eng.scalar_tensor_tensor(out=dst, in0=src[:, w:w + m], scalar=conv_par[:, w * CT + ct:w * CT + ct + 1],
                                                   in1=dst, op0=ALU.mult, op1=ALU.add)
                    if w < CW - 1:
                        link(ins)
                ins.then_inc(sem("conv_made"), 1)

            def slot(key, put_off=False):
                c, t = chunk_of[key], tile_of[key]
                make_lo(c + 1)
                if key[0] in ("bc", "x"):
                    if put_off:
                        pending.append(key)
                    else:
                        convolve(key)
                elif key[0] == "pb":
                    _, g, n0 = key
                    for n in range(2):
                        wait_tile(eng, t + n)
                        dst = halves(pb_sum[:, n0 + n, :])
                        if g == 0:
                            ins = eng.tensor_copy(dst, tile(t + n))
                        else:
                            wait_freed(eng, tile_of[("pb", g - 1, n0)] + n)
                            ins = eng.tensor_tensor(dst, dst, tile(t + n), ALU.add)
                        ins.then_inc(tile_free[(t + n) % 2], 1)

            def by_token(g):
                eng.wait_ge(sem("conv_done"), 6 * (g + 1))
                wait_after_read(eng, ("decays", 0))
                if g:
                    eng.wait_ge(sem("y_split"), g)
                    wait_full(eng, ("y_new", g - 1, NC))
                for c, t0, m in token_tiles():
                    key = ("x_tok", g, c)
                    wait_full(eng, key)
                    eng.tensor_tensor(xdt[0:m, c], spare(key)[0:m, :].rearrange("p (h d) -> p h d", h=HG),
                                      dt_tok[0:m, c, g * HG:(g + 1) * HG].unsqueeze(2).to_broadcast([m, HG, HD]), ALU.mult)\
                       .then_inc(bank_read[use[key][0]], 1)
                for j in range(PG):
                    eng.tensor_scalar(y_t[:, j, :], xs_t[:, j, :], par[:, PAR_D + g * PG + j:PAR_D + g * PG + j + 1], None, ALU.mult)\
                       .then_inc(sem("y_begun"), 1)
                key = ("cb", g)
                wait_full(eng, key)
                eng.tensor_tensor(cb_m[:, 0:NC, :], spare(key).rearrange("p (c l) -> p c l", l=P),
                                  upto[:, :].unsqueeze(1).to_broadcast([P, NC, P]), ALU.mult).then_inc(bank_read[use[key][0]], 1)
                key = ("sample_bc", g)
                eng.wait_ge(sem("b_tok_made"), g + 1)
                eng.tensor_tensor(cb_m[0:TS, NC, 0:TS], spare(key)[0:TS, P:P + TS], upto_b[:, :], ALU.mult).then_inc(bank_read[use[key][0]], 1)
                wait_after_read(eng, ("x_tok", g, NC))
                if g:
                    wait_full(eng, ("new_state", g - 1, NB - 1))
                eng.tensor_tensor(xend_s[:, :, :], xdt[0:TS, NC], end_decay[0:TS, NC, g * HG:(g + 1) * HG].unsqueeze(2).to_broadcast([TS, HG, HD]),
                                  ALU.mult).then_inc(sem("xend_s_made"), 1)

            def prepare(g, c):
                m = P if c < NC else TS
                for q in range(2):
                    wait_after_read(eng, ("seg", g, c, q))
                wait_after_read(eng, ("cb", g) if c < NC else ("sample_bc", g))
                eng.tensor_tensor(decay[0:m, :, 0:m], decay[0:m, :, 0:m], cb_m[0:m, c, 0:m].unsqueeze(1).to_broadcast([m, HG, m]), ALU.mult)\
                   .then_inc(sem("decay_made"), 1)
                if c < NC:
                    wait_after_read(eng, ("x_tok", g, c))
                    n = g * NC + c
                    if n >= 2:
                        wait_full(eng, ("state", (n - 2) // NC, (n - 2) % NC))
                    eng.tensor_tensor(xend[:, c % 2], xdt[:, c], end_decay[:, c, g * HG:(g + 1) * HG].unsqueeze(2).to_broadcast([P, HG, HD]), ALU.mult)\
                       .then_inc(sem("xend_made"), 1)

            def outputs(g, c):
                m, t0 = (P, c * P) if c < NC else (TS, TP)
                new = spare(("y_new", g, c)).rearrange("p (j l) -> p j l", l=P)[:, :, 0:m]
                e = e_t[:, :, 0:m]
                y = y_t[:, :, t0:t0 + m]
                eng.wait_ge(sem("y_begun"), PG * (g + 1))
                if c == 0:
                    wait_full(eng, ("y_new", g, c))
                    eng.tensor_tensor(y, y, new, ALU.add).then_inc(bank_read[use[("y_new", g, c)][0]], 1)
                else:
                    wait_after_read(eng, ("e", g, c))
                    if c < NC:
                        key = ("y_chunk_old", g, c)
                        wait_full(eng, key)
                        eng.tensor_tensor(e, e, spare(key).rearrange("p (j l) -> p j l", l=P), ALU.mult).then_inc(bank_read[use[key][0]], 1)
                        wait_after_read(eng, key)
                    else:
                        wait_after_read(eng, ("y_seq_old", g, NB - 1))
                        link(eng.tensor_tensor(e, e, y_old[:, :, :], ALU.mult))
                    wait_full(eng, ("y_new", g, c))
                    eng.tensor_tensor(e, e, new, ALU.add).then_inc(bank_read[use[("y_new", g, c)][0]], 1)
                    wait_after_read(eng, ("y_new", g, c))
                    eng.tensor_tensor(y, y, e, ALU.add).then_inc(sem("y_added"), 1)
                if c < NC:
                    key = ("state", g, c)
                    wait_full(eng, key)
                    if c == 0:
                        if g:
                            wait_full(eng, ("state_out", g - 1))
                        eng.tensor_copy(state[:, 0, :], spare(key)[:, :]).then_inc(bank_read[use[key][0]], 1)
                    else:
                        if c >= 2:
                            wait_full(eng, ("y_chunk_old", g, c - 1))
                        elif g:
                            wait_full(eng, ("state_out", g - 1))
                        wait_after_read(eng, ("state", g, c - 1))
                        s3 = [state[:, k % 2, :].rearrange("p (h d) -> p h d", h=HG) for k in (c - 1, c)]
                        link(eng.tensor_tensor(s3[1], s3[0], chunk_decay[:, c, g * HG:(g + 1) * HG].unsqueeze(2).to_broadcast([P, HG, HD]), ALU.mult))
                        eng.tensor_tensor(state[:, c % 2, :], state[:, c % 2, :], spare(key)[:, :], ALU.add).then_inc(bank_read[use[key][0]], 1)

            def sequence(g, b):
                n = g * NB + b
                key = ("y_seq_old", g, b)
                wait_full(eng, key)
                if g:
                    eng.wait_ge(sem("y_added"), NC * g)
                eng.tensor_copy(y_old[:, :, b * TD:(b + 1) * TD], spare(key)[:, 0:PG * TD].rearrange("p (j t) -> p j t", j=PG))\
                   .then_inc(bank_read[use[key][0]], 1)
                key = ("new_state", g, b)
                wait_full(eng, key)
                eng.wait_ge(sem("old_decayed"), n + 1)
                eng.tensor_tensor(old[:, b % 2], old[:, b % 2], spare(key).rearrange("p (j n) -> p j n", j=PG), ALU.add)\
                   .then_inc(bank_read[use[key][0]], 1)

            for key in before_groups:
                slot(key)
            for g in range(NG):
                by_token(g)
                plan = ssd_plan(g)
                for c in range(5):
                    before, later = plan[c]
                    prepare(g, c)
                    for key in before:
                        slot(key)
                    outputs(g, c)
                    for key in later:
                        slot(key, put_off=True)
                    if c < NC:
                        for b in (2 * c, 2 * c + 1):
                            sequence(g, b)
                    while pending:
                        convolve(pending.pop(0))
                eng.wait_ge(sem("y_added"), NC * (g + 1))
                wait_after_read(eng, ("y_new", g, 0))
                for j in range(PG):
                    wait_freed(eng, tile_of[("z", g, j)])
                    eng.tensor_tensor(y_t[:, j, :], y_t[:, j, :], z_s[:, j, :], ALU.mult).then_inc(sem("y_gated"), 1)
                before, later = plan[5]
                for key in before:
                    slot(key)
                eng.wait_ge(sem("y_rooted"), g + 1)
                for j in range(PG):
                    col = PAR_SSD + g * PG + j
                    eng.wait_ge(sem("y_squared"), PG * g + j + 1)
                    eng.scalar_tensor_tensor(out=y_t[:, j, :], in0=y_t[:, j, :], scalar=par[:, col:col + 1], in1=y_rinv,
                                             op0=ALU.mult, op1=ALU.mult).then_inc(sem("y_scaled"), 1)
                for j in range(PG):
                    eng.wait_ge(sem("y_hi_made"), PG * g + j + 1)
                    ins = eng.tensor_tensor(y_lo[:, j, :], y_t[:, j, :], f32(y_hi[:, j, :]), ALU.subtract)
                ins.then_inc(sem("y_split"), 1)
                for key in later:
                    slot(key)
            for key in last_pb:
                slot(key)

            eng.sem_inc(sem("merged_split"), 2)
            with eng.Fori(0, KD // 2) as i:
                for n in range(2):
                    c, t = C_GATE_B + n, T_GATE_B + n
                    one = bass.ds(2 * i + n, 1)
                    make_lo(c + 1, 2, i)
                    wait_freed(eng, t, 2, i)
                    eng.tensor_tensor(prod2[:, n:n + 1, :], gate2[:, n:n + 1, :], pb_sum[:, one, :], ALU.mult).then_inc(sem("merged_part"), 1)
                    eng.wait_ge(sem("merged_part"), n + 1 + 2 * i)
                    eng.wait_ge(sem(f"gated_back{n}"), 16 + 16 * i)
                    eng.tensor_tensor(prod2[:, n, :], prod2[:, n, :], gated_in[:, n, :], ALU.add).then_inc(sem("merged_made"), 1)
                    eng.wait_ge(sem("m_hi_made"), n + 1 + 2 * i)
                    eng.tensor_tensor(m_lo[:, one, :], prod2[:, n:n + 1, :], f32(m_hi[:, one, :]), ALU.subtract).then_inc(sem("merged_split"), 1)
            for n in range(KD):
                make_lo(C_OUT + n + 1)
                t = T_OUT + n
                wait_tile(eng, t)
                eng.tensor_copy(halves(x_res[:, n, :]), tile(t)).then_inc(tile_free[t % 2], 1)
            eng.wait_ge(sem("res_rooted"), 1)
            for k in range(KD):
                if k >= 2:
                    eng.wait_ge(sem("h2_split"), k - 1)
                eng.scalar_tensor_tensor(out=gate2[:, k % 2, :], in0=x_res[:, k, :], scalar=par[:, PAR_N2 + k:PAR_N2 + k + 1], in1=rinv2[:, :],
                                         op0=ALU.mult, op1=ALU.mult).then_inc(sem("h2_made"), 1)
                eng.wait_ge(sem("h2_hi_made"), k + 1)
                eng.tensor_tensor(x_lo[:, k, :], gate2[:, k % 2, :], f32(x_hi[:, k, :]), ALU.subtract).then_inc(sem("h2_split"), 1)
            eng.sem_inc(sem("f_split"), 2)
            with eng.Fori(0, KF // 2) as i:
                for n in range(2):
                    c, t = C_FFN + 2 * n, T_FFN + 2 * n
                    one = bass.ds(2 * i + n, 1)
                    make_lo(c + 1, 4, i)
                    make_lo(c + 2, 4, i)
                    wait_tile(eng, t + 1, 4, i)
                    wait_freed(eng, t, 4, i)
                    eng.wait_ge(sem("f_split"), n + 1 + 2 * i)
                    eng.tensor_tensor(halves(prod2[:, n, :]), halves(gate2[:, n, :]), tile(t + 1), ALU.mult).then_inc(tile_free[(t + 1) % 2], 1)
                    eng.wait_ge(sem("f_hi_made"), n + 1 + 2 * i)
                    eng.tensor_tensor(f_lo[:, one, :], prod2[:, n:n + 1, :], f32(f_hi[:, one, :]), ALU.subtract).then_inc(sem("f_split"), 1)

            def down_tile(n, i, last):
                for k in range(3):
                    if last and n == 1 and k == 2:
                        continue
                    make_lo(C_DOWN + 3 * n + k + 1, 6, i, tiles=DOWN_K[(k + 1) % 3][1])
                t = T_DOWN + n
                wait_tile(eng, t, 2, i)
                eng.tensor_tensor(prod2[:, n, :].rearrange("p (o h t) -> p o h t", o=1, h=2),
                                  x_res[:, bass.ds(2 * i + n, 1), :].rearrange("p o (h t) -> p o h t", h=2),
                                  tile(t).unsqueeze(1), ALU.add).then_inc(tile_free[t % 2], 1)

            with eng.Fori(0, KD // 2 - 1) as i:
                for n in range(2):
                    down_tile(n, i, False)
            for n in range(2):
                down_tile(n, KD // 2 - 1, True)


_INS = ["x_prompt", "x_sample", "cache_k", "cache_v", "page_table", "state_ssm", "state_conv",
        "norm1_w", "w_in", "q_norm_w", "k_norm_w", "sb_bias", "conv_w", "conv_b", "dt_bias", "a_log",
        "d_skip", "ssd_norm_w", "w_pa", "w_pb", "w_out", "norm2_w", "w_gate", "w_up", "w_down"]
_OUTS = [("y_prompt", (1, TP, D)), ("y_sample", (NB, TD, D)),
         ("k_prompt", (1, 1, TP, NKV, HD)), ("v_prompt", (1, 1, TP, NKV, HD)),
         ("ssm_prompt", (1, 1, NH, HD, P)), ("conv_prompt", (1, 1, CW - 1, CH)),
         ("k_sample", (1, NB, TD, NKV, HD)), ("v_sample", (1, NB, TD, NKV, HD)),
         ("ssm_sample", (1, NB, NH, HD, P)), ("conv_sample", (1, NB, CW - 1, CH))]


def kernel(**inputs):
    import numpy as np
    import concourse.bacc as bacc
    from concourse.bass_utils import run_bass_kernel_spmd

    nc = bacc.Bacc("TRN2", target_bir_lowering=False, num_devices=1)
    arrays, args = {}, []
    for name in _INS:
        a = np.ascontiguousarray(inputs[name])
        arrays[f"in_{name}"] = a
        args.append(nc.dram_tensor(f"in_{name}", a.shape, mybir.dt.from_np(a.dtype), kind="ExternalInput").ap())
    for name, shape in _OUTS:
        args.append(nc.dram_tensor(f"out_{name}", shape, F32, kind="ExternalOutput").ap())
    build(nc, *args)
    r = run_bass_kernel_spmd(nc, [arrays], core_ids=[0])
    return tuple(r.results[0][f"out_{name}"] for name, _ in _OUTS)
```
